# Optimizing a Trainium2 kernel written in Bass

```python
import jax, jax.numpy as jnp
from jax import lax
import numpy as np

D_MODEL = 1024
BATCH = 1
SEQ = 128
DEPTH = 4
DEC_BATCH = 1
DEC_SEQ = 256
PAST_LEN = 128

GRID_W = 64
N_MIXERS = 3
N_HEADS = 16
N_KV_HEADS = 4
HEAD_DIM = 64
Q_PER_KV = N_HEADS // N_KV_HEADS
QKV_DIM = (N_HEADS + 2 * N_KV_HEADS) * HEAD_DIM
WINDOW = 128
BLOCK = 128
ROPE_THETA = 10000.0
MLA_HEADS = 16
MLA_Q_LORA = 384
MLA_KV_LORA = 256
MLA_NOPE = 64
MLA_ROPE = 32
MLA_V = 64
N_EXPERTS = 16
N_GROUPS = 4
EXPERTS_PER_GROUP = N_EXPERTS // N_GROUPS
TOP_K = 2
D_EXPERT = 256
EPS = 1e-6
N_LAYERS_A = (DEPTH + 2) // 3
N_LAYERS_B = (DEPTH + 1) // 3
N_LAYERS_C = DEPTH // 3

kernel_name = 'hybrid_dit_prefix_denoise_step'

def rmsnorm(x, g):
    xf = x.astype(jnp.float32)
    y = xf * lax.rsqrt(jnp.mean(xf * xf, axis=-1, keepdims=True) + EPS)
    return (y * g.astype(jnp.float32)).astype(x.dtype)

def modulate(x, g, shift, scale):
    return rmsnorm(x, g) * (1 + scale) + shift

def adaln(cond, w_mod, b_mod):
    m = jax.nn.silu(cond) @ w_mod + b_mod
    return jnp.split(m, 6, axis=-1)

def grid_positions(n_tokens):
    rows = n_tokens // GRID_W
    r, col = jnp.meshgrid(jnp.arange(rows), jnp.arange(GRID_W), indexing='ij')
    return r.reshape(-1).astype(jnp.float32), col.reshape(-1).astype(jnp.float32)

def rope_2d(x, row, col):
    d = x.shape[-1]
    half, quarter = d // 2, d // 4
    inv = ROPE_THETA ** (-jnp.arange(quarter, dtype=jnp.float32) / quarter)
    ang = jnp.concatenate([row[:, None] * inv, col[:, None] * inv], axis=-1)
    cos = jnp.cos(ang)[:, None, :].astype(x.dtype)
    sin = jnp.sin(ang)[:, None, :].astype(x.dtype)
    x1, x2 = x[..., :half], x[..., half:]
    return jnp.concatenate([x1 * cos - x2 * sin, x2 * cos + x1 * sin], axis=-1)

def attend(qb, k, v, mask=None, sink=None):
    scale = qb.shape[-1] ** -0.5
    s = jnp.einsum('bqkgd,bskd->bkgqs', qb, k).astype(jnp.float32) * scale
    if mask is not None:
        s = jnp.where(mask, s, -jnp.inf)
    m = jnp.max(s, axis=-1, keepdims=True)
    if sink is not None:
        sk = sink.astype(jnp.float32)[None, :, :, None, None]
        m = jnp.maximum(m, sk)
        e = jnp.exp(s - m)
        denom = jnp.sum(e, axis=-1, keepdims=True) + jnp.exp(sk - m)
    else:
        e = jnp.exp(s - m)
        denom = jnp.sum(e, axis=-1, keepdims=True)
    p = (e / denom).astype(v.dtype)
    return jnp.einsum('bkgqs,bskd->bqkgd', p, v)

def sweep_query_blocks(q, fn):
    b, s = q.shape[:2]
    nb = s // BLOCK
    qb = jnp.moveaxis(q.reshape(b, nb, BLOCK, *q.shape[2:]), 1, 0)
    out = lax.map(lambda args: fn(*args), (qb, jnp.arange(nb)))
    return jnp.moveaxis(out, 0, 1).reshape(b, s, *out.shape[3:])

def band_mask(n, s_lat, s_ctx):
    q_pos = n * BLOCK + jnp.arange(BLOCK)
    k_pos = (n - 1) * BLOCK + jnp.arange(3 * BLOCK)
    near = (jnp.abs(k_pos[None, :] - q_pos[:, None]) <= WINDOW) & (k_pos >= 0)[None, :] & (k_pos < s_lat)[None, :]
    return jnp.concatenate([near, jnp.ones((BLOCK, s_ctx), dtype=bool)], axis=1)

def gqa_project(h, wqkv):
    b, s, _ = h.shape
    q, k, v = jnp.split(h @ wqkv, [N_HEADS * HEAD_DIM, (N_HEADS + N_KV_HEADS) * HEAD_DIM], axis=-1)
    return (q.reshape(b, s, N_HEADS, HEAD_DIM), k.reshape(b, s, N_KV_HEADS, HEAD_DIM),
            v.reshape(b, s, N_KV_HEADS, HEAD_DIM))

def group_q(q):
    return q.reshape(q.shape[0], q.shape[1], N_KV_HEADS, Q_PER_KV, q.shape[-1])

def merge_heads(o, wo):
    return o.reshape(o.shape[0], o.shape[1], -1) @ wo

def swa_context(h, wqkv, wo, sink):
    q, k, v = gqa_project(h, wqkv)
    sink_g = sink.reshape(N_KV_HEADS, Q_PER_KV)
    o = sweep_query_blocks(group_q(q), lambda qb, n: attend(qb, k, v, None, sink_g))
    return merge_heads(o, wo), k, v

def swa_latent(h, wqkv, wo, sink, k_ctx, v_ctx, row, col):
    q, k, v = gqa_project(h, wqkv)
    q, k = rope_2d(q, row, col), rope_2d(k, row, col)
    s_lat, s_ctx = h.shape[1], k_ctx.shape[1]
    pad = ((0, 0), (BLOCK, BLOCK), (0, 0), (0, 0))
    k_pad, v_pad = jnp.pad(k, pad), jnp.pad(v, pad)
    sink_g = sink.reshape(N_KV_HEADS, Q_PER_KV)

    def block(qb, n):
        k_loc = lax.dynamic_slice_in_dim(k_pad, n * BLOCK, 3 * BLOCK, axis=1)
        v_loc = lax.dynamic_slice_in_dim(v_pad, n * BLOCK, 3 * BLOCK, axis=1)
        keys = jnp.concatenate([k_loc, k_ctx.astype(k_loc.dtype)], axis=1)
        vals = jnp.concatenate([v_loc, v_ctx.astype(v_loc.dtype)], axis=1)
        return attend(qb, keys, vals, band_mask(n, s_lat, s_ctx), sink_g)

    return merge_heads(sweep_query_blocks(group_q(q), block), wo)

def qkn_context(h, wqkv, wo, qn, kn):
    q, k, v = gqa_project(h, wqkv)
    q, k = rmsnorm(q, qn), rmsnorm(k, kn)
    o = sweep_query_blocks(group_q(q), lambda qb, n: attend(qb, k, v))
    return merge_heads(o, wo), k, v

def qkn_latent(h, wqkv, wo, qn, kn, k_ctx, v_ctx, row, col):
    q, k, v = gqa_project(h, wqkv)
    q = rope_2d(rmsnorm(q, qn), row, col)
    k = rope_2d(rmsnorm(k, kn), row, col)
    keys = jnp.concatenate([k, k_ctx.astype(k.dtype)], axis=1)
    vals = jnp.concatenate([v, v_ctx.astype(v.dtype)], axis=1)
    o = sweep_query_blocks(group_q(q), lambda qb, n: attend(qb, keys, vals))
    return merge_heads(o, wo)

def mla_queries(h, wdq, qnorm, wuq):
    b, s, _ = h.shape
    q = (rmsnorm(h @ wdq, qnorm) @ wuq).reshape(b, s, MLA_HEADS, MLA_NOPE + MLA_ROPE)
    return q[..., :MLA_NOPE], q[..., MLA_NOPE:]

def mla_compress(h, wdkv, kvnorm):
    ckv = h @ wdkv
    return rmsnorm(ckv[..., :MLA_KV_LORA], kvnorm), ckv[..., MLA_KV_LORA:]

def mla_expand(ckv, k_pe, wukv):
    b, s, _ = ckv.shape
    kv = (ckv @ wukv).reshape(b, s, MLA_HEADS, MLA_NOPE + MLA_V)
    k_rot = jnp.broadcast_to(k_pe[:, :, None, :], (b, s, MLA_HEADS, MLA_ROPE))
    return jnp.concatenate([kv[..., :MLA_NOPE], k_rot], axis=-1), kv[..., MLA_NOPE:]

def mla_context(h, wdq, qnorm, wuq, wdkv, kvnorm, wukv, wo):
    q_nope, q_pe = mla_queries(h, wdq, qnorm, wuq)
    ckv, k_pe = mla_compress(h, wdkv, kvnorm)
    k, v = mla_expand(ckv, k_pe, wukv)
    q = jnp.concatenate([q_nope, q_pe], axis=-1)[:, :, :, None, :]
    o = sweep_query_blocks(q, lambda qb, n: attend(qb, k, v))
    return merge_heads(o, wo), ckv, k_pe

def mla_latent(h, wdq, qnorm, wuq, wdkv, kvnorm, wukv, wo, ckv_ctx, kpe_ctx, row, col):
    q_nope, q_pe = mla_queries(h, wdq, qnorm, wuq)
    q_pe = rope_2d(q_pe, row, col)
    ckv, k_pe = mla_compress(h, wdkv, kvnorm)
    k_pe = rope_2d(k_pe[:, :, None, :], row, col)[:, :, 0, :]
    ckv_all = jnp.concatenate([ckv, ckv_ctx.astype(ckv.dtype)], axis=1)
    kpe_all = jnp.concatenate([k_pe, kpe_ctx.astype(k_pe.dtype)], axis=1)
    k, v = mla_expand(ckv_all, kpe_all, wukv)
    q = jnp.concatenate([q_nope, q_pe], axis=-1)[:, :, :, None, :]
    o = sweep_query_blocks(q, lambda qb, n: attend(qb, k, v))
    return merge_heads(o, wo)

def moe(h, w_router, router_bias, w_gate, w_up, w_down):
    s = jax.nn.sigmoid((h @ w_router).astype(jnp.float32))
    sb = s + router_bias.astype(jnp.float32)
    grouped = sb.reshape(*sb.shape[:-1], N_GROUPS, EXPERTS_PER_GROUP)
    group_score = jnp.sum(lax.top_k(grouped, 2)[0], axis=-1)
    gsel = jnp.argmax(group_score, axis=-1)
    gmask = jnp.arange(N_GROUPS) == gsel[..., None]
    emask = jnp.repeat(gmask, EXPERTS_PER_GROUP, axis=-1)
    _, idx = lax.top_k(jnp.where(emask, sb, -jnp.inf), TOP_K)
    w = jnp.take_along_axis(s, idx, axis=-1)
    w = w / jnp.sum(w, axis=-1, keepdims=True)
    gates = jnp.sum(jax.nn.one_hot(idx, N_EXPERTS, dtype=jnp.float32) * w[..., None], axis=-2)
    a = jnp.einsum('bsd,edf->bsef', h, w_gate)
    u = jnp.einsum('bsd,edf->bsef', h, w_up)
    act = jax.nn.silu(a) * u * gates[..., None].astype(h.dtype)
    return jnp.einsum('bsef,efd->bsd', act, w_down)

def setup_inputs(seed: int = 0) -> dict:
    key = jax.random.key(seed)
    ks = iter(jax.random.split(key, 48))

    def nrm(shape, scale):
        return scale * jax.random.normal(next(ks), shape, jnp.float32)

    def gain(shape):
        return 1.0 + 0.05 * jax.random.normal(next(ks), shape, jnp.float32)

    D = D_MODEL
    return {
        'x_prompt': nrm((BATCH, SEQ, D), 1.0),
        'x_sample': nrm((DEC_BATCH, DEC_SEQ, D), 1.0),
        'cache_swa_k': nrm((DEC_BATCH, N_LAYERS_A, PAST_LEN, N_KV_HEADS, HEAD_DIM), 1.0),
        'cache_swa_v': nrm((DEC_BATCH, N_LAYERS_A, PAST_LEN, N_KV_HEADS, HEAD_DIM), 1.0),
        'cache_qkn_k': nrm((DEC_BATCH, N_LAYERS_B, PAST_LEN, N_KV_HEADS, HEAD_DIM), 1.0),
        'cache_qkn_v': nrm((DEC_BATCH, N_LAYERS_B, PAST_LEN, N_KV_HEADS, HEAD_DIM), 1.0),
        'cache_mla_ckv': nrm((DEC_BATCH, N_LAYERS_C, PAST_LEN, MLA_KV_LORA), 1.0),
        'cache_mla_kpe': nrm((DEC_BATCH, N_LAYERS_C, PAST_LEN, MLA_ROPE), 1.0),
        'c': nrm((DEC_BATCH, D), 1.0),
        'c_ctx': nrm((D,), 1.0),
        'w_mod': nrm((DEPTH, D, 6 * D), 0.3 * D ** -0.5),
        'b_mod': nrm((DEPTH, 6 * D), 0.02),
        'norm_mix': gain((DEPTH, D)),
        'norm_ffn': gain((DEPTH, D)),
        'swa_wqkv': nrm((N_LAYERS_A, D, QKV_DIM), D ** -0.5),
        'swa_wo': nrm((N_LAYERS_A, N_HEADS * HEAD_DIM, D), (N_HEADS * HEAD_DIM) ** -0.5),
        'swa_sink': nrm((N_LAYERS_A, N_HEADS), 1.0),
        'qkn_wqkv': nrm((N_LAYERS_B, D, QKV_DIM), D ** -0.5),
        'qkn_wo': nrm((N_LAYERS_B, N_HEADS * HEAD_DIM, D), (N_HEADS * HEAD_DIM) ** -0.5),
        'qkn_qnorm': gain((N_LAYERS_B, HEAD_DIM)),
        'qkn_knorm': gain((N_LAYERS_B, HEAD_DIM)),
        'mla_wdq': nrm((N_LAYERS_C, D, MLA_Q_LORA), D ** -0.5),
        'mla_qnorm': gain((N_LAYERS_C, MLA_Q_LORA)),
        'mla_wuq': nrm((N_LAYERS_C, MLA_Q_LORA, MLA_HEADS * (MLA_NOPE + MLA_ROPE)), MLA_Q_LORA ** -0.5),
        'mla_wdkv': nrm((N_LAYERS_C, D, MLA_KV_LORA + MLA_ROPE), D ** -0.5),
        'mla_kvnorm': gain((N_LAYERS_C, MLA_KV_LORA)),
        'mla_wukv': nrm((N_LAYERS_C, MLA_KV_LORA, MLA_HEADS * (MLA_NOPE + MLA_V)), MLA_KV_LORA ** -0.5),
        'mla_wo': nrm((N_LAYERS_C, MLA_HEADS * MLA_V, D), (MLA_HEADS * MLA_V) ** -0.5),
        'w_router': nrm((D, N_EXPERTS), D ** -0.5),
        'router_bias': nrm((N_EXPERTS,), 0.01),
        'moe_w_gate': nrm((DEPTH, N_EXPERTS, D, D_EXPERT), D ** -0.5),
        'moe_w_up': nrm((DEPTH, N_EXPERTS, D, D_EXPERT), D ** -0.5),
        'moe_w_down': nrm((DEPTH, N_EXPERTS, D_EXPERT, D), D_EXPERT ** -0.5),
        'final_norm': gain((D,)),
    }

def reference(x_prompt, x_sample, cache_swa_k, cache_swa_v, cache_qkn_k, cache_qkn_v, cache_mla_ckv,
              cache_mla_kpe, c, c_ctx, w_mod, b_mod, norm_mix, norm_ffn, swa_wqkv, swa_wo, swa_sink,
              qkn_wqkv, qkn_wo, qkn_qnorm, qkn_knorm, mla_wdq, mla_qnorm, mla_wuq, mla_wdkv, mla_kvnorm,
              mla_wukv, mla_wo, w_router, router_bias, moe_w_gate, moe_w_up, moe_w_down, final_norm):
    xc, xl = x_prompt, x_sample
    row, col = grid_positions(x_sample.shape[1])
    swa_k, swa_v, qkn_k, qkn_v, mla_ckv, mla_kpe = [], [], [], [], [], []
    for i in range(DEPTH):
        kind, j = i % N_MIXERS, i // N_MIXERS
        sh1c, sc1c, g1c, sh2c, sc2c, g2c = adaln(c_ctx, w_mod[i], b_mod[i])
        sh1l, sc1l, g1l, sh2l, sc2l, g2l = [m[:, None, :] for m in adaln(c, w_mod[i], b_mod[i])]
        hc = modulate(xc, norm_mix[i], sh1c, sc1c)
        hl = modulate(xl, norm_mix[i], sh1l, sc1l)
        if kind == 0:
            oc, kc, vc = swa_context(hc, swa_wqkv[j], swa_wo[j], swa_sink[j])
            ol = swa_latent(hl, swa_wqkv[j], swa_wo[j], swa_sink[j], cache_swa_k[:, j], cache_swa_v[:, j], row, col)
            swa_k.append(kc)
            swa_v.append(vc)
        elif kind == 1:
            oc, kc, vc = qkn_context(hc, qkn_wqkv[j], qkn_wo[j], qkn_qnorm[j], qkn_knorm[j])
            ol = qkn_latent(hl, qkn_wqkv[j], qkn_wo[j], qkn_qnorm[j], qkn_knorm[j],
                            cache_qkn_k[:, j], cache_qkn_v[:, j], row, col)
            qkn_k.append(kc)
            qkn_v.append(vc)
        else:
            oc, ckv_c, kpe_c = mla_context(hc, mla_wdq[j], mla_qnorm[j], mla_wuq[j], mla_wdkv[j],
                                           mla_kvnorm[j], mla_wukv[j], mla_wo[j])
            ol = mla_latent(hl, mla_wdq[j], mla_qnorm[j], mla_wuq[j], mla_wdkv[j], mla_kvnorm[j],
                            mla_wukv[j], mla_wo[j], cache_mla_ckv[:, j], cache_mla_kpe[:, j], row, col)
            mla_ckv.append(ckv_c)
            mla_kpe.append(kpe_c)
        xc = xc + g1c * oc
        xl = xl + g1l * ol
        hc = modulate(xc, norm_ffn[i], sh2c, sc2c)
        hl = modulate(xl, norm_ffn[i], sh2l, sc2l)
        xc = xc + g2c * moe(hc, w_router, router_bias, moe_w_gate[i], moe_w_up[i], moe_w_down[i])
        xl = xl + g2l * moe(hl, w_router, router_bias, moe_w_gate[i], moe_w_up[i], moe_w_down[i])
    y_prompt = rmsnorm(xc, final_norm)
    y_sample = rmsnorm(xl, final_norm)
    state_swa_k = jnp.stack(swa_k, axis=1)
    state_swa_v = jnp.stack(swa_v, axis=1)
    state_qkn_k = jnp.stack(qkn_k, axis=1)
    state_qkn_v = jnp.stack(qkn_v, axis=1)
    state_mla_ckv = jnp.stack(mla_ckv, axis=1)
    state_mla_kpe = jnp.stack(mla_kpe, axis=1)
    return (y_prompt, y_sample, state_swa_k, state_swa_v, state_qkn_k, state_qkn_v, state_mla_ckv, state_mla_kpe)


_drawn_inputs = setup_inputs


def setup_inputs(seed=0):
    import zlib

    import numpy as np

    out = dict(_drawn_inputs(seed))
    spreads = {}
    factors = {'cache_qkn_k': 3.88,
     'cache_qkn_v': 3.761,
     'cache_mla_ckv': 5.831,
     'cache_mla_kpe': 7.076,
     'swa_sink': 8.0,
     'qkn_qnorm': 7.349,
     'mla_qnorm': 8.0}
    for name, (base, spread) in spreads.items():
        noise = np.random.default_rng([zlib.crc32(name.encode()), seed]).standard_normal(out[name].shape)
        drawn = base * np.exp(spread * noise) if base else spread * noise
        out[name] = __import__('jax').numpy.asarray(drawn.astype(out[name].dtype))
    for name, factor in factors.items():
        out[name] = (out[name] * factor).astype(out[name].dtype)
    return out
```

```python
from contextlib import ExitStack

import numpy as np

import concourse.bass as bass
from concourse import mybir

F32 = mybir.dt.float32
ALU = mybir.AluOpType
ACT = mybir.ActivationFunctionType
AX = mybir.AxisListType

P = 128
D = 1024
KC = D // P
DEPTH = 4
KINDS = [0, 1, 2, 0]
STACK = [0, 0, 0, 1]
NB = 3
COND = [0, 1, 1]
NT = NB * P
H, G, DH = 16, 4, 64
E, DE = 16, 256
UC = 256
R = 9
PAIRS = E // 2
MLA_Q, MLA_KV, ROPE, DQK = 384, 256, 32, 96
EPS = 1e-6
NEG = -1e30
MODPOS = (3, 4, 8)
GATE_SLOT = ((0, 1, 2), (5, 6, 7))


def host_constants():
    tokens = np.arange(256)
    row, col = (tokens // 64).astype(np.float32), (tokens % 64).astype(np.float32)

    def rope(d):
        quarter = d // 4
        inv = np.float32(10000.0) ** (-np.arange(quarter, dtype=np.float32) / np.float32(quarter))
        ang = np.concatenate([row[:, None] * inv, col[:, None] * inv], axis=-1).astype(np.float32)
        both = np.stack([np.cos(ang), np.sin(ang)], axis=1).astype(np.float32)
        return both.reshape(2, P, d).transpose(1, 0, 2)

    r, c = np.arange(P)[:, None], np.arange(P)[None, :]
    masks = np.stack([np.where(c <= r, 0.0, NEG), np.where(c >= r, 0.0, NEG)], axis=1)
    sel = np.zeros((3, 2 * P + 2), np.float32)
    for s in range(2):
        sel[s, s * P:(s + 1) * P] = 1.0
        sel[s, 2 * P + s] = 1.0
    sel[2, :] = 1.0
    first = np.tile(np.concatenate([np.arange(16, 0, -1), np.arange(4, 0, -1)])[None], (P, 1))
    out = dict(ident=np.eye(P), masks=masks.reshape(P, 2 * P), rope64=rope(64).reshape(P, 128),
               rope32=rope(32).reshape(P, 64), sel=sel, first=first)
    return {k: np.ascontiguousarray(v, dtype=np.float32) for k, v in out.items()}


def mixer_units(L):
    if KINDS[L] < 2:
        return [("qkv", u) for u in range(6)] + [("wo", u) for u in range(4)]
    return ([("dq", 0), ("dq", 1), ("dkv", 0), ("dkv", 1)] + [("uq", u) for u in range(3)]
            + [("ukv", u) for u in range(2)] + [("wo", u) for u in range(4)])


def plan_ring():
    fills, at, place = [0] * R, 0, {}
    for j in MODPOS:
        place[("mod", -1, j)] = (j, fills[j])
        fills[j] += PAIRS
    for L in range(DEPTH):
        for name, u in mixer_units(L):
            place[(name, L, u)] = (at % R, fills[at % R])
            fills[at % R] += 1
            at += 1
        for j in range(R):
            s = (at + j) % R
            kind = "mod" if j in MODPOS else "exp"
            if kind == "mod" and L == DEPTH - 1:
                continue
            place[(kind, L, j)] = (s, fills[s])
            fills[s] += PAIRS
    return place


def plan_jobs():
    order = [("cond", "v"), ("gains", "v")]
    alt = "va"
    for L in range(DEPTH):
        order += [(("modc", L), "v")] + [(("gate", L, j), "a") for j in range(8)]
        order += [(("norm", 2 * L, k), alt[k % 2]) for k in range(KC)]
        if KINDS[L] < 2:
            order += [(("qkv", L, u, b), alt[(3 * u + b) % 2]) for u in range(6) for b in range(NB)]
            order += [(("qT", L, p), alt[p % 2]) for p in range(8)]
            order += [(("kT", L, g), alt[g % 2]) for g in range(G)]
            order += [(("S", L, h, i), "p") for h in range(H) for i in range(2)]
        else:
            order += [(("lat", L, u, b), alt[b % 2]) for u in range(4) for b in range(NB)]
            order += [(("qlT", L, c), "v") for c in range(3)] + [(("ckvT", L, c), "a") for c in range(2)]
            order += [(("kpeT", L), "v")]
            order += [(("uq", L, u, b), alt[b % 2]) for u in range(3) for b in range(NB)]
            order += [(("V", L, u, kb), alt[kb % 2]) for u in range(2) for kb in range(4)]
            for c in range(4):
                order += [(("kT", L, h), alt[h % 2]) for h in range(4 * c, 4 * c + 4)]
                order += [(("qT", L, h), alt[h % 2]) for h in range(4 * c, 4 * c + 4)]
                order += [(("S", L, h, i), "p") for h in range(4 * c, 4 * c + 4) for i in range(2)]
        order += [(("oT", L, k), alt[k % 2]) for k in range(KC)]
        order += [(("wo", L, u, b), "w") for u in range(4) for b in range(NB)]
        order += [(("norm", 2 * L + 1, k), alt[k % 2]) for k in range(KC)]
        order += [(("router", L), "a")]
    jobs, count = {}, {"v": 0, "a": 0, "p": 0, "w": 0}
    for n, (key, eng) in enumerate(order):
        count[eng] += 0 if eng == "p" and key[3] == 1 else 1
        jobs[key] = (n, eng, count[eng])
    by_index = [jobs[key] for key, _ in order]
    return jobs, by_index


def build(nc, A):
    ring_place = plan_ring()
    jobs, job_at = plan_jobs()
    ctx = ExitStack()
    with ctx:
        def sb(name, shape):
            return ctx.enter_context(nc.sbuf_tensor(name, shape, F32))

        def sem(name):
            return ctx.enter_context(nc.semaphore(name))

        ring = sb("ring", [P, R, KC * UC])
        x = sb("x", [P, NB, D])
        xn = sb("xn", [P, NB, D])
        hT = sb("hT", [P, KC, NT])
        work = sb("work", [P, NB * 1536 + 8 * NT])
        V = sb("V", [P, 4, D])
        pp = sb("pp", [P, 2, 2, 896])
        kT = sb("kT", [P, 4, 4 * P])
        gbc = sb("gbc", [P, 2, 2, D])
        kc = sb("kc", [P, 4, 2, DH])
        ident = sb("ident", [P, P])
        masks = sb("masks", [P, 2, P])
        rope64 = sb("rope64", [P, 2, 2, 32])
        rope32 = sb("rope32", [P, 2, 2, 16])
        sel = sb("sel", [3, 2 * P + 2])
        first = sb("first", [P, 20])
        condT = sb("condT", [P, KC, 2])
        gT = sb("gT", [P, 67])
        modc = sb("modc", [P, 4, KC, 2])
        amul = sb("amul", [P, 2, KC, 2])
        wr = sb("wr", [P, KC, E])
        rbias = sb("rbias", [P, E])
        gains = sb("gains", [P, 2, DH])
        kvg = sb("kvg", [P, MLA_KV])
        small = sb("small", [P, 128])
        sink = sb("sink", [P, 2, 2, H])
        neg_max = sb("neg_max", [P, H, NB])
        den = sb("den", [P, H, NB])
        rden = sb("rden", [P, H, NB])
        esink = sb("esink", [P, H, NB])
        gates = sb("gates", [P, NB, E])

        qkv = work[:, 0:NB * 1536].rearrange("p (b n) -> p b n", b=NB)
        qT = work[:, NB * 1536:].rearrange("p (k n) -> p k n", k=8)
        rows = work[0:3, 0:6 * D]
        raw = xn[:, 0, 0:2 * P]
        acc = V[:, 0:NB, :]
        ql = xn[:, 0:2, :].rearrange("p a n -> p (a n)")[:, 0:NB * MLA_Q].rearrange("p (b n) -> p b n", b=NB)
        qlT = hT[:, 0:3, :]
        ckvT = hT[:, 3:6, :].rearrange("p a n -> p (a n)")[:, 0:1024].rearrange("p (c n) -> p c n", c=2)
        wo_tmp = pp[:, 0, :, :].rearrange("p s n -> p (s n)")[:, 0:4 * UC].rearrange("p (s n) -> p s n", s=4)
        squares = pp[:, :, :, :].rearrange("p a s n -> p (a s n)")
        ckv = squares[:, 1408:2560].rearrange("p (b n) -> p b n", b=4)
        kpe = squares[:, 2560:2944].rearrange("p (b n) -> p b n", b=4)
        sil = squares[:, 1024:1536].rearrange("p (s n) -> p s n", s=2)
        act_sb = squares[:, 1536:2048].rearrange("p (s n) -> p s n", s=2)
        actT = squares[:, 2048:2560].rearrange("p (s c n) -> p s c n", s=2, c=2)
        rt = kT[:, :, :].rearrange("p a n -> p (a n)")[:, 0:12 * NB * E].rearrange(
            "p (a b e) -> p a b e", a=12, b=NB)

        bank = [ctx.enter_context(nc.psum_tensor(f"bank{i}", [P, 512], F32)) for i in range(8)]

        slot_full = [sem(f"slot_full{s}") for s in range(R)]
        slot_used = [sem(f"slot_used{s}") for s in range(R)]
        bank_full, freed_v, freed_a = sem("bank_full"), sem("freed_v"), sem("freed_a")
        const_in, x_in, cache_in, bmod_in, out_done = (sem(s) for s in
                                                       ("const_in", "x_in", "cache_in", "bmod_in", "out_done"))
        v_chain, a_chain, p_chain = sem("v_chain"), sem("a_chain"), sem("p_chain")
        raw_silu, raw_ready, mod_ready, mod_full, rows_done = (sem(s) for s in
            ("raw_silu", "raw_ready", "mod_ready", "mod_full", "rows_done"))
        sumsq, rstd_ready, xn_ready, wo_mul, x_mixed, x_moe, moe_mul = (sem(s) for s in
            ("sumsq", "rstd_ready", "xn_ready", "wo_mul", "x_mixed", "x_moe", "moe_mul"))
        head_sq, head_ms, head_rstd, roped_v, roped_p, qk_ready = (sem(s) for s in
            ("head_sq", "head_ms", "head_rstd", "roped_v", "roped_p", "qk_ready"))
        max_ready, probs, pt_full, pt_a, pt_v, o_full, o_ready, esink_in, esink_done = (sem(s) for s in
            ("max_ready", "probs", "pt_full", "pt_a", "pt_v", "o_full", "o_ready", "esink_in", "esink_done"))
        lat_sq, lat_rstd, states = (sem(s) for s in ("lat_sq", "lat_rstd", "states"))
        freed = {"v": freed_v, "a": freed_a, "p": probs, "w": wo_mul}
        gates_ready, acc_zero, au_full, sil_full, act_full, acT_full, acT_ready, y_full, y_used = (sem(s) for s in
            ("gates_ready", "acc_zero", "au_full", "sil_full", "act_full", "acT_full", "acT_ready", "y_full", "y_used"))

        def job_bank(key):
            return bank[jobs[key][0] % 4]

        def wait_bank_free(pe, key):
            n = jobs[key][0]
            if n >= 4:
                _, eng, cnt = job_at[n - 4]
                pe.wait_ge(freed[eng], cnt)

        def wait_bank_full(eng, key):
            eng.wait_ge(bank_full, jobs[key][0] + 1)

        def wait_evacuated(eng, *keys):
            for name in "va":
                cnt = [jobs[k][2] for k in keys if jobs[k][1] == name]
                if cnt:
                    eng.wait_ge(freed[name], max(cnt))

        def unit(key):
            return ring[:, ring_place[key][0], :]

        def pass_on(eng, ukey):
            eng.sem_inc(slot_used[ring_place[ukey][0]], 1)

        LAT = (("dq", 0, 256), ("dq", 1, 128), ("dkv", 0, 256), ("dkv", 1, 32))

        def last_reader_of(key):
            if key[0] in ("qkv", "wo", "uq") and key[3] == 2:
                return key[:3]
            if key[0] == "lat" and key[3] == 2:
                return (LAT[key[2]][0], key[1], LAT[key[2]][1])
            if key[0] == "kT" and KINDS[key[1]] == 2 and key[2] % 8 == 7:
                return ("ukv", key[1], key[2] // 8)
            return None

        def mine(key, name):
            return jobs[key][1] == name

        SW = {0: 0, 3: 1}
        CHUNKS = {L: ([range(H)] if KINDS[L] < 2 else [range(4 * c, 4 * c + 4) for c in range(4)])
                  for L in range(DEPTH)}

        PARTS = [(1, 0, 0, 384), (0, 0, 384, 128), (2, 1, 0, 384)]

        def rope(eng, ops, heads, table, half, scratch, link, done):
            n = heads.shape[1]
            x1, x2 = heads[:, :, 0:half], heads[:, :, half:2 * half]
            cos = table[:, 0, :].unsqueeze(1).to_broadcast([P, n, half])
            sin = table[:, 1, :].unsqueeze(1).to_broadcast([P, n, half])
            t = [scratch[:, j * n * half:(j + 1) * n * half].rearrange("p (h d) -> p h d", d=half) for j in range(4)]
            ops.tensor_tensor(t[0], x1, cos, ALU.mult)
            ops.tensor_tensor(t[1], x2, sin, ALU.mult)
            ops.tensor_tensor(t[2], x2, cos, ALU.mult)
            link(ops.tensor_tensor(t[3], x1, sin, ALU.mult))
            ops.tensor_tensor(x1, t[0], t[1], ALU.subtract)
            ops.tensor_tensor(x2, t[2], t[3], ALU.add).then_inc(done, 1)

        def dest(key):
            ps = job_bank(key)
            if key[0] == "qkv":
                _, L, u, b = key
                if u < 4:
                    return qkv[:, b, u * UC:(u + 1) * UC], ps[:, 0:UC]
                if u == 4:
                    return (qkv[:, b, 1024:1536].rearrange("p (g t d) -> p g t d", g=G, t=2),
                            ps[:, 0:UC].rearrange("p (g d) -> p g d", g=G).unsqueeze(2).to_broadcast([P, G, 2, DH]))
                return V[:, b, 0:UC], ps[:, 0:UC]
            if key[0] == "lat":
                _, L, u, b = key
                if u < 2:
                    n = (256, 128)[u]
                    return ql[:, b, u * 256:u * 256 + n], ps[:, 0:n]
                n = (256, 32)[u - 2]
                return ckv[:, b, (u - 2) * 256:(u - 2) * 256 + n], ps[:, 0:n]
            if key[0] == "uq":
                _, L, u, b = key
                return qkv[:, b, u * 512:(u + 1) * 512], ps[:, :]
            if key[0] == "V":
                _, L, u, kb = key
                return V[:, kb, u * 512:(u + 1) * 512], ps[:, :]
            if key[0] == "ckvT":
                return ckvT[:, key[2], :], ps[:, :]
            if key[0] == "kT":
                if KINDS[key[1]] < 2:
                    return kT[:, key[2], :], ps[:, :]
                return kT[0:64, key[2] % 4, :], ps[0:64, :]
            if key[0] == "oT":
                return hT[:, key[2], :], ps[:, 0:NT]
            raise KeyError(key)

        def turn_act(act, n, slot):
            act.wait_ge(acT_full, n + 1)
            nc.scalar.copy(actT[:, slot], bank[2][:, 0:2 * P].rearrange("p (c n) -> p c n", c=2)).then_inc(acT_ready, 1)

        block = ctx.enter_context(nc.Block())

        @block.sync
        def _(sp):
            def fill(key, src, dst_cols, i=None, shape=None):
                slot, before = ring_place[key]
                n = before if i is None else before + i
                sp.wait_ge(slot_used[slot], n + 1)
                dst = ring[:, slot, 0:dst_cols]
                if shape is not None:
                    dst = dst.rearrange("p (k n) -> p k n", k=shape)
                sp.dma_start(dst, src).then_inc(slot_full[slot], 16)

            def cols(w, n0, n):
                return w[:, n0:n0 + n].rearrange("(k p) n -> p k n", p=P)

            def fill_mod(L, key_layer, i):
                for m, j in enumerate(MODPOS):
                    src = A["w_mod"][L, :, bass.ds(i * (3 * UC) + m * UC, UC)].rearrange("(k p) n -> p k n", p=P)
                    fill(("mod", key_layer, j), src, KC * UC, i, KC)

            for slot in range(R):
                sp.sem_inc(slot_used[slot], 1)
            with sp.Fori(0, PAIRS) as i:
                fill_mod(0, -1, i)
            for L in range(DEPTH):
                s = STACK[L]
                for name, u in mixer_units(L):
                    key = (name, L, u)
                    if name == "qkv":
                        w = A["swa_wqkv" if KINDS[L] == 0 else "qkn_wqkv"][s]
                        fill(key, cols(w, u * UC, UC), KC * UC, None, KC)
                    elif name == "wo":
                        w = A[("swa_wo", "qkn_wo", "mla_wo")[KINDS[L]]][s]
                        fill(key, cols(w, u * UC, UC), KC * UC, None, KC)
                    elif name == "dq":
                        n = (256, 128)[u]
                        fill(key, cols(A["mla_wdq"][s], u * 256, n), KC * n, None, KC)
                    elif name == "dkv":
                        n = (256, 32)[u]
                        fill(key, cols(A["mla_wdkv"][s], u * 256, n), KC * n, None, KC)
                    elif name == "uq":
                        fill(key, cols(A["mla_wuq"][s], u * 512, 512), 3 * 512, None, 3)
                    elif name == "ukv":
                        fill(key, cols(A["mla_wukv"][s], u * 1024, 1024), 2 * 1024, None, 2)
                with sp.Fori(0, PAIRS) as i:
                    for j in range(R):
                        if j in MODPOS:
                            if L < DEPTH - 1:
                                m = MODPOS.index(j)
                                src = A["w_mod"][L + 1, :, bass.ds(i * (3 * UC) + m * UC, UC)].rearrange(
                                    "(k p) n -> p k n", p=P)
                                fill(("mod", L, j), src, KC * UC, i, KC)
                            continue
                        w, e = (j, 0) if j < 3 else (j - 5, 1)
                        if w < 2:
                            src = A[("moe_w_gate", "moe_w_up")[w]][L, bass.ds(i * 2 + e, 1), :, :].rearrange(
                                "e (k p) n -> p (e k) n", p=P)
                            fill(("exp", L, j), src, KC * UC, i, KC)
                        else:
                            src = A["moe_w_down"][L, bass.ds(i * 2 + e, 1), :, :].rearrange(
                                "e (k p) n -> p (e k) n", p=P)
                            fill(("exp", L, j), src, 2 * D, i, 2)

        @block.gpsimd
        def _(pool):
            chain = [0]

            def link(ins):
                chain[0] += 1
                ins.then_inc(p_chain, 1)
                pool.wait_ge(p_chain, chain[0])

            def rms_power(ss, out, n, done):
                link(nc.gpsimd.tensor_scalar(out, ss, 1.0 / n, EPS, ALU.mult, ALU.add))
                nc.gpsimd.tensor_tensor(out, out, exponent(out), ALU.pow).then_inc(done, 1)

            def exponent(like):
                n = 1
                for d in like.shape[1:]:
                    n *= d
                e = minus_half[:, 0:n]
                if len(like.shape) == 3:
                    e = e.rearrange("p (a b) -> p a b", a=like.shape[1])
                return e

            minus_half = small[:, 56:128]
            link(nc.gpsimd.memset(minus_half, -0.5))
            pool.dma_start(x[:, 0, :], A["x_prompt"][0]).then_inc(x_in, 16)
            pool.dma_start(x[:, 1:3, :], A["x_sample"][0].rearrange("(b p) d -> p b d", p=P)).then_inc(x_in, 16)
            pool.dma_start(rows[2:3, :], A["b_mod"][0:1, :]).then_inc(bmod_in, 16)

            def norm_power(n):
                pool.wait_ge(sumsq, 3 * n + 3)
                rms_power(small[:, 0:3], small[:, 4:7], D, rstd_ready)

            nsq = 0
            for L in range(DEPTH):
                s, kind = STACK[L], KINDS[L]
                if L > 0:
                    pool.wait_ge(x_moe, 3 * L)
                if KINDS[L] < 2:
                    ck, cv = (("cache_swa_k", "cache_swa_v"), ("cache_qkn_k", "cache_qkn_v"))[KINDS[L]]
                    for dup in range(2):
                        pool.dma_start(kc[:, :, dup, :], A[ck][0, s]).then_inc(cache_in, 16)
                    pool.dma_start(V[:, 3, 0:256], A[cv][0, s].rearrange("t g d -> t (g d)")).then_inc(cache_in, 16)
                norm_power(2 * L)
                if KINDS[L] == 1:
                    for b in range(NB):
                        pool.wait_ge(head_ms, b + 1)
                        rms_power(small[:, 8:32], small[:, 32:56], DH, head_rstd)
                if KINDS[L] < 2:
                    if KINDS[L] == 0:
                        wait_evacuated(pool, *[("qkv", L, u, 2) for u in range(5)])
                    else:
                        pool.wait_ge(qk_ready, 3)
                    rope(pool, nc.gpsimd, qkv[:, 2, :].rearrange("p (h d) -> p h d", d=DH), rope64[:, 1], 32,
                         squares, link, roped_p)
                else:
                    pool.dma_start(ckv[:, 3, 0:256], A["cache_mla_ckv"][0, s]).then_inc(cache_in, 16)
                    link(nc.gpsimd.memset(kpe[:, :, :], 0.0))
                    pool.dma_start(kpe[:, 3, 64:96], A["cache_mla_kpe"][0, s]).then_inc(cache_in, 16)
                    pool.wait_ge(lat_sq, 1)
                    rms_power(small[:, 8:14], small[:, 14:20], 1, lat_rstd)
                if kind < 2:
                    sk, sv = (("state_swa_k", "state_swa_v"), ("state_qkn_k", "state_qkn_v"))[kind]
                    wait_evacuated(pool, ("qkv", L, 4, 0), ("qkv", L, 5, 0))
                    pool.dma_start(A[sk][0, s], qkv[:, 0, 1024:1536].rearrange("p (g t d) -> p g t d", g=G, t=2)
                                   [:, :, 0, :]).then_inc(states, 16)
                    pool.dma_start(A[sv][0, s].rearrange("t g d -> t (g d)"), V[:, 0, 0:256]).then_inc(states, 16)
                else:
                    pool.wait_ge(roped_v, 4)
                    pool.dma_start(A["state_mla_ckv"][0, s], ckv[:, 0, 0:256]).then_inc(states, 16)
                    pool.dma_start(A["state_mla_kpe"][0, s], kpe[:, 0, 64:96]).then_inc(states, 16)
                for u in range(4):
                    for b in range(NB):
                        g = 12 * L + 3 * u + b
                        pool.wait_ge(wo_mul, g + 1)
                        xs = x[:, b, u * UC:(u + 1) * UC]
                        nc.gpsimd.tensor_tensor(xs, xs, wo_tmp[:, g % 4, :], ALU.add).then_inc(x_mixed, 1)
                pool.wait_ge(x_mixed, 12 * L + 12)
                pool.wait_ge(states, 32 * (L + 1))
                nc.gpsimd.memset(acc, 0.0).then_inc(acc_zero, 1)
                if L < DEPTH - 1:
                    pool.dma_start(rows[2:3, :], A["b_mod"][L + 1:L + 2, :]).then_inc(bmod_in, 16)
                norm_power(2 * L + 1)
                for b in range(NB):
                    pool.wait_ge(moe_mul, 3 * L + b + 1)
                    nc.gpsimd.tensor_tensor(x[:, b, :], x[:, b, :], acc[:, b, :], ALU.add).then_inc(x_moe, 1)
            pool.dma_start(gbc[:, 0, 0, :], A["final_norm"].partition_broadcast(P)).then_inc(x_in, 16)
            norm_power(2 * DEPTH)
            pool.wait_ge(xn_ready, 3 * (2 * DEPTH + 1) + 1)
            pool.dma_start(A["y_prompt"][0], xn[:, 0, :]).then_inc(out_done, 16)
            pool.dma_start(A["y_sample"][0].rearrange("(b p) d -> p b d", p=P), xn[:, 1:3, :]).then_inc(out_done, 16)
            pool.wait_ge(out_done, 32)
            pool.wait_ge(states, 32 * DEPTH)

        @block.scalar
        def _(act):
            chain = [0]

            def link(ins):
                chain[0] += 1
                ins.then_inc(a_chain, 1)
                act.wait_ge(a_chain, chain[0])

            def free(ins):
                ins.then_inc(freed_a, 1)

            def evacuate(*keys):
                for key in keys:
                    if mine(key, "a"):
                        wait_bank_full(act, key)
                        if last_reader_of(key):
                            pass_on(act, last_reader_of(key))
                        free(nc.scalar.copy(*dest(key)))

            def norm_in(n, L, odd):
                for b in range(NB):
                    if n == 0:
                        act.wait_ge(x_in, 32)
                    elif odd:
                        act.wait_ge(x_mixed, 12 * L + 9 + b + 1)
                    else:
                        act.wait_ge(x_moe, 3 * (L - 1) + b + 1)
                    nc.scalar.activation(xn[:, b, :], x[:, b, :], ACT.Square,
                                         accum_out=small[:, b:b + 1]).then_inc(sumsq, 1)

            def norm_out(n, s):
                for k in range(KC):
                    key = ("norm", n, k)
                    if mine(key, "a"):
                        wait_bank_full(act, key)
                        act.wait_ge(mod_ready, n // 2 + 1)
                        ps = job_bank(key)
                        nc.scalar.activation(hT[:, k, 0:P], ps[:, 0:P], ACT.Identity,
                                             bias=modc[:, 2 * s, k, 0:1], scale=amul[:, s, k, 0:1])
                        free(nc.scalar.activation(hT[:, k, P:NT], ps[:, P:NT], ACT.Identity,
                                                  bias=modc[:, 2 * s, k, 1:2], scale=amul[:, s, k, 1:2]))

            def mod_rows(L, base, i, m):
                act.wait_ge(mod_full, base + i * 3 + m + 1)
                pass_on(act, ("mod", L, MODPOS[m]))
                nc.scalar.copy(rows[0:2, bass.ds(i * (3 * UC) + m * UC, UC)], bank[3][0:2, 0:UC]).then_inc(rows_done, 1)

            for dst, src in ((ident[:, :], A["ident"]), (masks[:, :, :], A["masks"].rearrange("p (a n) -> p a n", a=2)),
                             (rope64[:, :, :, :], A["rope64"].rearrange("p (a c n) -> p a c n", a=2, c=2)),
                             (rope32[:, :, :, :], A["rope32"].rearrange("p (a c n) -> p a c n", a=2, c=2)),
                             (sel[:, :], A["sel"]), (first[:, :], A["first"]),
                             (raw[0:8, 0:P], A["c_ctx"].rearrange("(k p) -> k p", p=P)),
                             (raw[8:16, 0:P], A["c"].rearrange("a (k p) -> (a k) p", p=P)),
                             (raw[0:32, P:2 * P], A["norm_mix"].rearrange("l (k p) -> (l k) p", p=P)),
                             (raw[32:64, P:2 * P], A["norm_ffn"].rearrange("l (k p) -> (l k) p", p=P)),
                             (raw[64:67, P:2 * P], A["mla_qnorm"].rearrange("l (k p) -> (l k) p", p=P)),
                             (wr[:, :, :], A["w_router"].rearrange("(k p) e -> p k e", p=P)),
                             (rbias[:, :], A["router_bias"].partition_broadcast(P)),
                             (gains[:, 0, :], A["qkn_qnorm"][0].partition_broadcast(P)),
                             (gains[:, 1, :], A["qkn_knorm"][0].partition_broadcast(P)),
                             (kvg[:, :], A["mla_kvnorm"][0].partition_broadcast(P)),
                             (sink[:, 0, 0, :], A["swa_sink"][0].partition_broadcast(P)),
                             (sink[:, 1, 0, :], A["swa_sink"][1].partition_broadcast(P))):
                act.dma_start(dst, src).then_inc(const_in, 16)
            act.sem_inc(rows_done, 1)
            act.sem_inc(acT_ready, 1)
            act.wait_ge(const_in, 16 * 18)
            nc.scalar.activation(raw[0:16, 0:P], raw[0:16, 0:P], ACT.Silu).then_inc(raw_silu, 1)
            with act.Fori(0, PAIRS) as i:
                for m in range(3):
                    mod_rows(-1, 0, i, m)

            for L in range(DEPTH):
                kind, s = KINDS[L], STACK[L]
                for j in range(8):
                    key = ("gate", L, j)
                    wait_bank_full(act, key)
                    g, c, half = j // 4, j // 2 % 2, j % 2
                    free(nc.scalar.copy(gbc[:, g, c, half * 512:(half + 1) * 512], job_bank(key)[:, :]))
                norm_in(2 * L, L, False)
                norm_out(2 * L, 0)
                if kind < 2:
                    evacuate(*[("qkv", L, u, b) for u in range(6) for b in range(NB)])
                    if kind == 1:
                        for b in range(NB):
                            wait_evacuated(act, *[("qkv", L, u, b) for u in range(5)])
                            if b > 0:
                                act.wait_ge(head_ms, b)
                            nc.scalar.activation(squares[:, 0:1536], qkv[:, b, :], ACT.Square).then_inc(head_sq, 1)
                else:
                    evacuate(*[("lat", L, u, b) for u in range(4) for b in range(NB)])
                    wait_evacuated(act, *[("lat", L, u, b) for u in range(4) for b in range(NB)])
                    for b in range(NB):
                        nc.scalar.activation(squares[:, 448 * b:448 * b + 384], ql[:, b, :], ACT.Square, scale=384 ** -0.5,
                                             accum_out=small[:, 8 + b:9 + b])
                        last = nc.scalar.activation(kT[:, b, 0:256], ckv[:, b, 0:256], ACT.Square,
                                                    scale=256 ** -0.5, accum_out=small[:, 11 + b:12 + b])
                    last.then_inc(lat_sq, 1)
                    evacuate(*[("ckvT", L, c) for c in range(2)])
                    evacuate(*[("uq", L, u, b) for u in range(3) for b in range(NB)])
                    evacuate(*[("V", L, u, kb) for u in range(2) for kb in range(4)])
                if kind == 2:
                    act.wait_ge(states, 32 * (L + 1))
                qscale = (DH if kind < 2 else DQK) ** -0.5
                for heads in CHUNKS[L]:
                    keys = ([("qT", L, p) for p in range(8)] + [("kT", L, g) for g in range(G)] if kind < 2 else
                            [("kT", L, h) for h in heads] + [("qT", L, h) for h in heads])
                    for key in keys:
                        if not mine(key, "a"):
                            continue
                        if key[0] == "kT":
                            evacuate(key)
                            continue
                        wait_bank_full(act, key)
                        rws = P if kind < 2 else DQK
                        free(nc.scalar.mul(qT[0:rws, key[2] % 8, :], job_bank(key)[0:rws, 0:NT], qscale))

                    def turn(h):
                        n = L * H + h
                        act.wait_ge(pt_full, 2 * n + 1)
                        nc.scalar.copy(pp[:, 1, h % 2, 0:512], bank[4][:, :]).then_inc(pt_a, 1)

                    for h in heads:
                        n = L * H + h
                        act.wait_ge(max_ready, n + 1)
                        if h >= 2:
                            act.wait_ge(pt_full, 2 * (n - 2) + 2)
                        if kind == 0:
                            nc.scalar.activation(esink[:, h, :], neg_max[:, h, :], ACT.Exp,
                                                 bias=sink[:, SW[L], 0, h:h + 1])
                        for b, i, c0, w in PARTS:
                            ins = nc.scalar.activation(pp[:, 0, h % 2, 512 * i + c0:512 * i + c0 + w],
                                                       job_bank(("S", L, h, i))[:, c0:c0 + w], ACT.Exp,
                                                       bias=neg_max[:, h, b:b + 1], accum_out=den[:, h, b:b + 1])
                        ins.then_inc(probs, 1)
                        if h > heads[0]:
                            turn(h - 1)
                    turn(heads[-1])
                evacuate(*[("oT", L, k) for k in range(KC)])
                norm_in(2 * L + 1, L, True)
                norm_out(2 * L + 1, 1)
                wait_bank_full(act, ("router", L))
                free(nc.scalar.activation(rt[:, 0], job_bank(("router", L))[:, 0:NB * E].rearrange(
                    "p (b e) -> p b e", b=NB), ACT.Sigmoid))
                with act.Fori(0, PAIRS) as i:
                    for t in range(6):
                        n = 48 * L + i * 6 + t
                        act.wait_ge(au_full, n + 1)
                        if t % 3 == 2:
                            pass_on(act, ("exp", L, GATE_SLOT[t // 3][0]))
                            pass_on(act, ("exp", L, GATE_SLOT[t // 3][1]))
                        act.wait_ge(act_full, n + 1)
                        nc.scalar.activation(sil[:, t % 2, :], bank[t % 2][:, 0:DE], ACT.Silu).then_inc(sil_full, 1)
                        if t > 0:
                            turn_act(act, n - 1, (t - 1) % 2)
                        if L < DEPTH - 1 and t in (2, 3, 5):
                            mod_rows(L, 24 * (L + 1), i, (2, 3, 5).index(t))
                    turn_act(act, 48 * L + i * 6 + 5, 1)
            norm_in(2 * DEPTH, DEPTH, False)

        @block.vector
        def _(dve):
            V_ = nc.vector
            chain = [0]

            def link(ins):
                chain[0] += 1
                ins.then_inc(v_chain, 1)
                dve.wait_ge(v_chain, chain[0])

            def free(ins):
                ins.then_inc(freed_v, 1)

            def evacuate(*keys):
                for key in keys:
                    if mine(key, "v"):
                        wait_bank_full(dve, key)
                        if last_reader_of(key):
                            pass_on(dve, last_reader_of(key))
                        free(V_.tensor_copy(*dest(key)))

            def norm_scale(n):
                dve.wait_ge(rstd_ready, n + 1)
                for b in range(NB):
                    V_.tensor_scalar(xn[:, b, :], x[:, b, :], small[:, 4 + b:5 + b], None,
                                     ALU.mult).then_inc(xn_ready, 1)

            def norm_out(n, s):
                for k in range(KC):
                    key = ("norm", n, k)
                    if mine(key, "v"):
                        wait_bank_full(dve, key)
                        ps = job_bank(key)
                        V_.tensor_scalar(hT[:, k, 0:P], ps[:, 0:P], amul[:, s, k, 0:1], modc[:, 2 * s, k, 0:1],
                                         ALU.mult, ALU.add)
                        free(V_.tensor_scalar(hT[:, k, P:NT], ps[:, P:NT], amul[:, s, k, 1:2],
                                              modc[:, 2 * s, k, 1:2], ALU.mult, ALU.add))

            dve.wait_ge(const_in, 16 * 18)
            for key, dst, n in (("cond", condT[:, :, :].rearrange("p k c -> p c k"), 16), ("gains", gT[:, :], 67)):
                wait_bank_full(dve, key)
                src = job_bank(key)[:, 0:n]
                free(V_.tensor_copy(dst, src.rearrange("p (c k) -> p c k", c=2) if n == 16 else src))
            for w in range(2):
                V_.tensor_scalar(sink[:, w, 1, :], sink[:, w, 0, :], -1.0, None, ALU.mult)
            dve.sem_inc(act_full, 2)
            dve.sem_inc(y_used, 2)

            def route(L):
                s_, sb_, sbm = rt[:, 0], rt[:, 1], rt[:, 2]
                link(V_.tensor_tensor(sb_, s_, rbias[:, :].unsqueeze(1).to_broadcast([P, NB, E]), ALU.add))
                q4 = sb_.rearrange("p b (g j) -> p (b g) j", j=4)
                pair = rt[:, 3:5].rearrange("p a b e -> p (a b e)")[:, 0:72].rearrange("p (q j) -> p q j", j=6)
                V_.tensor_tensor(pair[:, :, 0:3], q4[:, :, 0:3], q4[:, :, 1:4], ALU.add)
                V_.tensor_tensor(pair[:, :, 3:5], q4[:, :, 0:2], q4[:, :, 2:4], ALU.add)
                link(V_.tensor_tensor(pair[:, :, 5:6], q4[:, :, 0:1], q4[:, :, 3:4], ALU.add))
                gs = rt[:, 5, 0, 0:12]
                link(V_.tensor_reduce(gs, pair, AX.X, ALU.max))
                gsb = gs.rearrange("p (b g) -> p b g", b=NB)
                gm = rt[:, 5, 1, 0:3]
                link(V_.tensor_reduce(gm, gsb, AX.X, ALU.max))
                eq = rt[:, 6, 0, 0:12].rearrange("p (b g) -> p b g", b=NB)
                link(V_.tensor_tensor(eq, gsb, gm.unsqueeze(2).to_broadcast([P, NB, 4]), ALU.is_equal))
                link(V_.tensor_tensor(eq, eq, first[:, 16:20].unsqueeze(1).to_broadcast([P, NB, 4]), ALU.mult))
                link(V_.tensor_reduce(gm, eq, AX.X, ALU.max))
                link(V_.tensor_tensor(eq, eq, gm.unsqueeze(2).to_broadcast([P, NB, 4]), ALU.is_equal))
                emask = eq.unsqueeze(3).to_broadcast([P, NB, 4, 4])
                sbm4 = sbm.rearrange("p b (g j) -> p b g j", j=4)
                sb4 = sb_.rearrange("p b (g j) -> p b g j", j=4)
                link(V_.tensor_scalar(rt[:, 7, 0, 0:12], rt[:, 6, 0, 0:12], -NEG, NEG, ALU.mult, ALU.add))
                off = rt[:, 7, 0, 0:12].rearrange("p (b g) -> p b g", b=NB).unsqueeze(3).to_broadcast([P, NB, 4, 4])
                link(V_.tensor_tensor(sbm4, sb4, emask, ALU.mult))
                link(V_.tensor_tensor(sbm4, sbm4, off, ALU.add))
                m = rt[:, 5, 2, 0:3]
                picks = []
                for r in range(2):
                    a = rt[:, 8 + r]
                    link(V_.tensor_reduce(m, sbm, AX.X, ALU.max))
                    link(V_.tensor_tensor(a, sbm, m.unsqueeze(2).to_broadcast([P, NB, E]), ALU.is_equal))
                    link(V_.tensor_tensor(a, a, first[:, 0:16].unsqueeze(1).to_broadcast([P, NB, E]), ALU.mult))
                    link(V_.tensor_reduce(m, a, AX.X, ALU.max))
                    link(V_.tensor_tensor(a, a, m.unsqueeze(2).to_broadcast([P, NB, E]), ALU.is_equal))
                    if r == 0:
                        link(V_.scalar_tensor_tensor(out=sbm, in0=a, scalar=4 * NEG, in1=sbm, op0=ALU.mult,
                                                     op1=ALU.add))
                    picks.append(a)
                link(V_.tensor_tensor(picks[0], picks[0], picks[1], ALU.add))
                link(V_.tensor_tensor(picks[0], picks[0], s_, ALU.mult))
                link(V_.tensor_reduce(m, picks[0], AX.X, ALU.add))
                link(V_.reciprocal(m, m))
                V_.tensor_tensor(gates[:, :, :], picks[0], m.unsqueeze(2).to_broadcast([P, NB, E]),
                                 ALU.mult).then_inc(gates_ready, 1)

            for L in range(DEPTH):
                kind = KINDS[L]
                key = ("modc", L)
                wait_bank_full(dve, key)
                V_.tensor_copy(modc[:, :, :, :], job_bank(key)[:, 0:64].rearrange("p (v k c) -> p v k c", v=4, k=KC))\
                  .then_inc(freed_v, 1)
                dve.wait_ge(freed_v, jobs[key][2])
                for s in range(2):
                    g = gT[:, 32 * s + 8 * L:32 * s + 8 * L + 8].unsqueeze(2).to_broadcast([P, KC, 2])
                    last = V_.scalar_tensor_tensor(out=amul[:, s], in0=modc[:, 2 * s + 1], scalar=1.0, in1=g,
                                                   op0=ALU.add, op1=ALU.mult)
                last.then_inc(mod_ready, 1)
                dve.wait_ge(mod_ready, L + 1)
                norm_scale(2 * L)
                norm_out(2 * L, 0)
                if kind < 2:
                    evacuate(*[("qkv", L, u, b) for u in range(6) for b in range(NB)])
                    qk_heads = [qkv[:, b, :].rearrange("p (h d) -> p h d", d=DH) for b in range(NB)]
                    if kind == 1:
                        for b in range(NB):
                            dve.wait_ge(head_sq, b + 1)
                            V_.tensor_reduce(small[:, 8:32], squares[:, 0:1536].rearrange("p (h d) -> p h d", d=DH),
                                             AX.X, ALU.add).then_inc(head_ms, 1)
                            dve.wait_ge(head_rstd, b + 1)
                            hv = qk_heads[b]
                            link(V_.tensor_tensor(hv, hv, small[:, 32:56].unsqueeze(2).to_broadcast([P, 24, DH]),
                                                  ALU.mult))
                            V_.tensor_tensor(hv[:, 0:H], hv[:, 0:H],
                                             gains[:, 0, :].unsqueeze(1).to_broadcast([P, H, DH]), ALU.mult)
                            V_.tensor_tensor(hv[:, H:24], hv[:, H:24],
                                             gains[:, 1, :].unsqueeze(1).to_broadcast([P, 8, DH]),
                                             ALU.mult).then_inc(qk_ready, 1)
                        dve.wait_ge(qk_ready, 3)
                    else:
                        wait_evacuated(dve, *[("qkv", L, u, 1) for u in range(5)])
                    rope(dve, V_, qk_heads[1], rope64[:, 0], 32, xn[:, :, :].rearrange("p b n -> p (b n)"), link,
                         roped_v)
                else:
                    evacuate(*[("lat", L, u, b) for u in range(4) for b in range(NB)])
                    wait_evacuated(dve, *[("lat", L, u, b) for u in range(4) for b in range(NB)])
                    dve.wait_ge(lat_rstd, 1)
                    dve.wait_ge(cache_in, 16 * (3 * 2 + 2))
                    for b in range(NB):
                        V_.tensor_scalar(ql[:, b, :], ql[:, b, :], small[:, 14 + b:15 + b], None, ALU.mult)
                        V_.scalar_tensor_tensor(out=ckv[:, b, 0:256], in0=ckv[:, b, 0:256],
                                                scalar=small[:, 17 + b:18 + b], in1=kvg[:, :], op0=ALU.mult,
                                                op1=ALU.mult)
                        last = V_.tensor_copy(kpe[:, b, 64:96], ckv[:, b, 256:288])
                    link(last)
                    for b in (1, 2):
                        rope(dve, V_, kpe[:, b:b + 1, 64:96], rope32[:, b - 1], 16, squares[:, 1024 + 64 * b:],
                             link, roped_v)
                    for c in range(3):
                        key = ("qlT", L, c)
                        wait_bank_full(dve, key)
                        free(V_.tensor_scalar(qlT[:, c, :], job_bank(key)[:, 0:NT], gT[:, 64 + c:65 + c], None,
                                              ALU.mult))
                    key = ("kpeT", L)
                    wait_bank_full(dve, key)
                    for j in range(4):
                        last = V_.tensor_copy(kT[64:96, j, :], job_bank(key)[64:96, :])
                    free(last)
                    evacuate(*[("uq", L, u, b) for u in range(3) for b in range(NB)])
                    wait_evacuated(dve, *[("uq", L, u, b) for u in range(3) for b in range(NB)])
                    for b in (1, 2):
                        dve.wait_ge(roped_v, 3 + b)
                        rope(dve, V_, qkv[:, b, :].rearrange("p (h d) -> p h d", d=DQK)[:, :, 64:96],
                             rope32[:, b - 1], 16, squares, link, roped_v)
                    evacuate(*[("V", L, u, kb) for u in range(2) for kb in range(4)])
                qscale = (DH if kind < 2 else DQK) ** -0.5

                def turn(h):
                    n = L * H + h
                    dve.wait_ge(pt_full, 2 * n + 2)
                    V_.tensor_copy(pp[:, 1, h % 2, 512:896], bank[5][:, 0:384]).then_inc(pt_v, 1)

                def finish_pair(j):
                    n = L * 8 + j
                    dve.wait_ge(probs, L * H + 2 * j + 2)
                    d_, r_ = den[:, 2 * j:2 * j + 2, :], rden[:, 2 * j:2 * j + 2, :]
                    if kind == 0:
                        link(V_.tensor_tensor(d_, d_, esink[:, 2 * j:2 * j + 2, :], ALU.add))
                    link(V_.reciprocal(r_, d_))
                    dve.wait_ge(o_full, n + 1)
                    src = bank[6 + j % 2][:, 0:384].rearrange("p (b h d) -> p b h d", b=NB, h=2)
                    for b in range(NB):
                        o = xn[:, b, 2 * j * DH:(2 * j + 2) * DH].rearrange("p (h d) -> p h d", h=2)
                        last = V_.tensor_tensor(o, src[:, b], r_[:, :, b:b + 1].to_broadcast([P, 2, DH]), ALU.mult)
                    last.then_inc(o_ready, 1)

                for heads in CHUNKS[L]:
                    keys = ([("qT", L, p) for p in range(8)] + [("kT", L, g) for g in range(G)] if kind < 2 else
                            [("kT", L, h) for h in heads] + [("qT", L, h) for h in heads])
                    for key in keys:
                        if not mine(key, "v"):
                            continue
                        if key[0] == "kT":
                            evacuate(key)
                            continue
                        wait_bank_full(dve, key)
                        rws = P if kind < 2 else DQK
                        free(V_.tensor_scalar(qT[0:rws, key[2] % 8, :], job_bank(key)[0:rws, 0:NT], qscale, None,
                                              ALU.mult))
                    for h in heads:
                        n = L * H + h
                        for b, i, c0, w in PARTS:
                            if b != 0:
                                wait_bank_full(dve, ("S", L, h, i))
                            last = V_.tensor_reduce(neg_max[:, h, b:b + 1], job_bank(("S", L, h, i))[:, c0:c0 + w],
                                                    AX.X, ALU.max, negate=True)
                        if kind == 0:
                            link(last)
                            last = V_.tensor_scalar(neg_max[:, h, :], neg_max[:, h, :], sink[:, SW[L], 1, h:h + 1],
                                                    None, ALU.min)
                        last.then_inc(max_ready, 1)
                        if h > heads[0]:
                            turn(h - 1)
                        if h >= heads[0] + 3 and h % 2 == 1:
                            finish_pair((h - 3) // 2)
                    turn(heads[-1])
                    finish_pair(heads[-1] // 2)
                evacuate(*[("oT", L, k) for k in range(KC)])
                for u in range(4):
                    for b in range(NB):
                        g = 12 * L + 3 * u + b
                        key = ("wo", L, u, b)
                        wait_bank_full(dve, key)
                        if last_reader_of(key):
                            pass_on(dve, last_reader_of(key))
                        if 3 * u + b >= 4:
                            dve.wait_ge(x_mixed, g - 3)
                        V_.tensor_tensor(wo_tmp[:, g % 4, :], job_bank(key)[:, 0:UC],
                                         gbc[:, 0, COND[b], u * UC:(u + 1) * UC], ALU.mult).then_inc(wo_mul, 1)
                norm_scale(2 * L + 1)
                norm_out(2 * L + 1, 1)
                wait_evacuated(dve, ("router", L))
                route(L)
                dve.wait_ge(gates_ready, L + 1)
                dve.wait_ge(acc_zero, L + 1)
                with dve.Fori(0, PAIRS) as i:
                    def add_block(t):
                        n = 48 * L + i * 6 + t
                        dve.wait_ge(y_full, n + 1)
                        if t % 3 == 2:
                            pass_on(dve, ("exp", L, GATE_SLOT[t // 3][2]))
                        for half in range(2):
                            a = acc[:, t % 3, half * 512:(half + 1) * 512]
                            last = V_.tensor_tensor(a, a, bank[4 + 2 * (t % 2) + half][:, :], ALU.add)
                        last.then_inc(y_used, 1)

                    for t in range(6):
                        n = 48 * L + i * 6 + t
                        dve.wait_ge(sil_full, n + 1)
                        V_.scalar_tensor_tensor(out=act_sb[:, t % 2, :], in0=bank[t % 2][:, DE:2 * DE],
                                                scalar=gates[:, t % 3, bass.ds(i * 2 + t // 3, 1)],
                                                in1=sil[:, t % 2, :], op0=ALU.mult,
                                                op1=ALU.mult).then_inc(act_full, 1)
                        if t > 0:
                            add_block(t - 1)
                    add_block(5)
                for b in range(NB):
                    dve.wait_ge(y_used, 48 * L + 48 + b)
                    V_.tensor_tensor(acc[:, b, :], acc[:, b, :], gbc[:, 1, COND[b], :], ALU.mult).then_inc(moe_mul, 1)
            norm_scale(2 * DEPTH)
            dve.wait_ge(x_in, 48)
            dve.wait_ge(xn_ready, 3 * (2 * DEPTH + 1))
            for b in range(NB):
                last = V_.tensor_tensor(xn[:, b, :], xn[:, b, :], gbc[:, 0, 0, :], ALU.mult)
            last.then_inc(xn_ready, 1)

        @block.tensor
        def _(pe):
            def done(ins):
                ins.then_inc(bank_full, 1)

            def wait_unit(key, i=None):
                slot, before = ring_place[key]
                pe.wait_ge(slot_full[slot], 16 * (before + 1) if i is None else i * 16 + 16 * (before + 1))

            def mm(out, lhsT, rhs, start, stop):
                return pe.matmul(out, lhsT, rhs, start=start, stop=stop)

            def mod_unit(key, base, i, m):
                wait_unit(key, i)
                pe.wait_ge(rows_done, base + i * 3 + m + 1)
                w = unit(key).rearrange("p (k n) -> p k n", k=KC)
                for k in range(KC):
                    ins = mm(bank[3][0:2, 0:UC], condT[:, k, :], w[:, k, :], k == 0, k == KC - 1)
                ins.then_inc(mod_full, 1)

            def project(key, ukey, lhs, kcs, n):
                wait_bank_free(pe, key)
                w = unit(ukey)[:, 0:kcs * n].rearrange("p (k n) -> p k n", k=kcs)
                for k in range(kcs):
                    ins = mm(job_bank(key)[:, 0:n], lhs[:, k, key[3] * P:(key[3] + 1) * P], w[:, k, :],
                             k == 0, k == kcs - 1)
                done(ins)

            pe.wait_ge(const_in, 16 * 18)
            pe.wait_ge(raw_silu, 1)
            done(pe.transpose(job_bank("cond")[:, 0:16], raw[0:16, 0:P], ident[0:16, 0:16]))
            done(pe.transpose(job_bank("gains")[:, 0:67], raw[0:67, P:2 * P], ident[0:67, 0:67]))
            wait_evacuated(pe, "cond", "gains")
            with pe.Fori(0, PAIRS) as i:
                for m, j in enumerate(MODPOS):
                    mod_unit(("mod", -1, j), 0, i, m)

            def norm_turn(n):
                pe.wait_ge(xn_ready, 3 * n + 3)
                for k in range(KC):
                    key = ("norm", n, k)
                    wait_bank_free(pe, key)
                    for b in range(NB):
                        ins = pe.transpose(job_bank(key)[:, b * P:(b + 1) * P], xn[:, b, k * P:(k + 1) * P],
                                           ident[:, :])
                    done(ins)
                wait_evacuated(pe, *[("norm", n, k) for k in range(KC)])

            for L in range(DEPTH):
                kind = KINDS[L]
                pe.wait_ge(rows_done, 24 * (L + 1) + 1)
                pe.wait_ge(bmod_in, 16 * (L + 1))
                key = ("modc", L)
                wait_bank_free(pe, key)
                for v, at in enumerate((0, 1, 3, 4)):
                    for k in range(KC):
                        c = (v * KC + k) * 2
                        ins = mm(job_bank(key)[:, c:c + 2], rows[0:3, at * D + k * P:at * D + (k + 1) * P],
                                 sel[:, 2 * P:2 * P + 2], True, True)
                done(ins)
                for j in range(8):
                    key = ("gate", L, j)
                    wait_bank_free(pe, key)
                    g, c, half = j // 4, j // 2 % 2, j % 2
                    c0 = (2, 5)[g] * D + half * 512
                    done(mm(job_bank(key)[:, :], sel[:, c * P:(c + 1) * P], rows[0:3, c0:c0 + 512], True, True))
                norm_turn(2 * L)
                if kind < 2:
                    for u in range(6):
                        wait_unit(("qkv", L, u))
                        for b in range(NB):
                            project(("qkv", L, u, b), ("qkv", L, u), hT, KC, UC)
                else:
                    for u, (name, w, n) in enumerate(LAT):
                        wait_unit((name, L, w))
                        for b in range(NB):
                            project(("lat", L, u, b), (name, L, w), hT, KC, n)
                    pe.wait_ge(roped_v, 4)
                    pe.wait_ge(cache_in, 16 * 8)
                    for c in range(3):
                        key = ("qlT", L, c)
                        wait_bank_free(pe, key)
                        for b in range(NB):
                            ins = pe.transpose(job_bank(key)[:, b * P:(b + 1) * P], ql[:, b, c * P:(c + 1) * P],
                                               ident[:, :])
                        done(ins)
                    for c in range(2):
                        key = ("ckvT", L, c)
                        wait_bank_free(pe, key)
                        for b in range(4):
                            ins = pe.transpose(job_bank(key)[:, b * P:(b + 1) * P], ckv[:, b, c * P:(c + 1) * P],
                                               ident[:, :])
                        done(ins)
                    key = ("kpeT", L)
                    wait_bank_free(pe, key)
                    for b in range(4):
                        ins = pe.transpose(job_bank(key)[0:DQK, b * P:(b + 1) * P], kpe[:, b, :], ident[:, :])
                    done(ins)
                    wait_evacuated(pe, *[("qlT", L, c) for c in range(3)], *[("ckvT", L, c) for c in range(2)],
                                   ("kpeT", L))
                    for u in range(3):
                        wait_unit(("uq", L, u))
                        for b in range(NB):
                            project(("uq", L, u, b), ("uq", L, u), qlT, 3, 512)
                    for u in range(2):
                        wait_unit(("ukv", L, u))
                        w = unit(("ukv", L, u)).rearrange("p (c h n) -> p c h n", c=2, h=8)
                        for kb in range(4):
                            key = ("V", L, u, kb)
                            wait_bank_free(pe, key)
                            for c in range(2):
                                ins = mm(job_bank(key)[:, :].rearrange("p (h d) -> p h d", h=8),
                                         ckvT[:, c, kb * P:(kb + 1) * P], w[:, c, :, 64:128], c == 0, c == 1)
                            done(ins)

                def scores(h):
                    if kind < 2:
                        r0, r1, q, kk = (h % 2) * 64, (h % 2) * 64 + 64, h // 2, h // 4
                    else:
                        r0, r1, q, kk = 0, DQK, h % 8, h % 4
                    for i in range(2):
                        key = ("S", L, h, i)
                        wait_bank_free(pe, key)
                        b = 1 + i
                        ins = mm(job_bank(key)[:, 0:384], qT[r0:r1, q, b * P:(b + 1) * P], kT[r0:r1, kk, P:4 * P],
                                 True, kind != 0)
                        if kind == 0:
                            ins = mm(job_bank(key)[:, P * (1 - i):P * (2 - i)], ident[:, :], masks[:, i, :],
                                     False, True)
                        if i == 0:
                            ins = mm(job_bank(key)[:, 384:512], qT[r0:r1, q, 0:P], kT[r0:r1, kk, 0:P], True, True)
                        done(ins)

                def turn(h):
                    n = L * H + h
                    pe.wait_ge(probs, n + 1)
                    for i in range(2):
                        if n > 0:
                            pe.wait_ge((pt_a, pt_v)[i], n)
                        for t in range((4, 3)[i]):
                            ins = pe.transpose(bank[4 + i][:, t * P:(t + 1) * P],
                                               pp[:, 0, h % 2, 512 * i + t * P:512 * i + (t + 1) * P], ident[:, :])
                        ins.then_inc(pt_full, 1)

                def weigh(h):
                    n = L * H + h
                    j = L * 8 + h // 2
                    pe.wait_ge(pt_a, n + 1)
                    pe.wait_ge(pt_v, n + 1)
                    if h % 2 == 0 and j >= 2:
                        pe.wait_ge(o_ready, j - 1)
                    vc = (h // 4 if kind < 2 else h) * DH
                    for b, off, kbs in ((0, 384, (0,)), (1, 0, (1, 2, 3)), (2, 512, (1, 2, 3))):
                        out = bank[6 + h // 2 % 2][:, (2 * b + h % 2) * DH:(2 * b + h % 2 + 1) * DH]
                        for t, kb in enumerate(kbs):
                            ins = mm(out, pp[:, 1, h % 2, off + t * P:off + (t + 1) * P], V[:, kb, vc:vc + DH],
                                     t == 0, t == len(kbs) - 1)
                    if h % 2 == 1:
                        ins.then_inc(o_full, 1)

                if kind < 2:
                    if kind == 1:
                        pe.wait_ge(qk_ready, 3)
                    pe.wait_ge(roped_v, (1, 2, 0, 7)[L])
                    pe.wait_ge(roped_p, (1, 2, 0, 3)[L])
                    pe.wait_ge(cache_in, 16 * (3, 6, 0, 11)[L])
                    wait_evacuated(pe, *[("qkv", L, u, b) for u in range(6) for b in range(NB)])
                    for p in range(8):
                        key = ("qT", L, p)
                        wait_bank_free(pe, key)
                        for b in range(NB):
                            ins = pe.transpose(job_bank(key)[:, b * P:(b + 1) * P], qkv[:, b, p * P:(p + 1) * P],
                                               ident[:, :])
                        done(ins)
                    for g in range(G):
                        key = ("kT", L, g)
                        wait_bank_free(pe, key)
                        for b in range(4):
                            src = (qkv[:, b, 1024 + g * P:1024 + (g + 1) * P] if b < 3 else
                                   kc[:, g, :, :].rearrange("p t d -> p (t d)"))
                            ins = pe.transpose(job_bank(key)[:, b * P:(b + 1) * P], src, ident[:, :])
                        done(ins)
                for heads in CHUNKS[L]:
                    if kind == 2:
                        for h in heads:
                            key = ("kT", L, h)
                            wait_bank_free(pe, key)
                            w = unit(("ukv", L, h // 8)).rearrange("p (c h n) -> p c h n", c=2, h=8)
                            for c in range(2):
                                ins = mm(job_bank(key)[0:64, :], w[:, c, h % 8, 0:64], ckvT[:, c, :], c == 0, c == 1)
                            done(ins)
                        if heads[0] == 0:
                            pe.wait_ge(roped_v, 6)
                            wait_evacuated(pe, *[("uq", L, 2, b) for b in range(NB)],
                                           *[("V", L, 1, kb) for kb in range(4)])
                        for h in heads:
                            key = ("qT", L, h)
                            wait_bank_free(pe, key)
                            for b in range(NB):
                                ins = pe.transpose(job_bank(key)[0:DQK, b * P:(b + 1) * P],
                                                   qkv[:, b, h * DQK:(h + 1) * DQK], ident[:, :])
                            done(ins)
                        wait_evacuated(pe, *[(w, L, h) for h in heads for w in ("qT", "kT")])
                    else:
                        wait_evacuated(pe, *[("qT", L, p) for p in range(8)], *[("kT", L, g) for g in range(G)])
                    hs = list(heads)
                    for t in range(len(hs) + 2):
                        if t < len(hs):
                            scores(hs[t])
                        if 1 <= t <= len(hs):
                            turn(hs[t - 1])
                        if t >= 2:
                            weigh(hs[t - 2])
                pe.wait_ge(o_ready, 8 * (L + 1))
                for k in range(KC):
                    key = ("oT", L, k)
                    wait_bank_free(pe, key)
                    for b in range(NB):
                        ins = pe.transpose(job_bank(key)[:, b * P:(b + 1) * P], xn[:, b, k * P:(k + 1) * P],
                                           ident[:, :])
                    done(ins)
                wait_evacuated(pe, *[("oT", L, k) for k in range(KC)])
                for u in range(4):
                    wait_unit(("wo", L, u))
                    for b in range(NB):
                        project(("wo", L, u, b), ("wo", L, u), hT, KC, UC)
                norm_turn(2 * L + 1)
                key = ("router", L)
                wait_bank_free(pe, key)
                for b in range(NB):
                    for k in range(KC):
                        ins = mm(job_bank(key)[:, b * E:(b + 1) * E], hT[:, k, b * P:(b + 1) * P], wr[:, k, :],
                                 k == 0, k == KC - 1)
                done(ins)
                wait_evacuated(pe, key)

                with pe.Fori(0, PAIRS) as i:
                    def gate_up(t):
                        n = 48 * L + i * 6 + t
                        e, b = t // 3, t % 3
                        pe.wait_ge(act_full, n + 1)
                        for w in range(2):
                            key = ("exp", L, GATE_SLOT[e][w])
                            if b == 0:
                                wait_unit(key, i)
                            wv = unit(key).rearrange("p (k n) -> p k n", k=KC)
                            for k in range(KC):
                                ins = mm(bank[t % 2][:, w * DE:(w + 1) * DE], hT[:, k, b * P:(b + 1) * P],
                                         wv[:, k, :], k == 0, k == KC - 1)
                        ins.then_inc(au_full, 1)

                    def down(t):
                        n = 48 * L + i * 6 + t
                        e, b = t // 3, t % 3
                        pe.wait_ge(act_full, n + 3)
                        pe.wait_ge(acT_ready, n + 1)
                        for c in range(2):
                            ins = pe.transpose(bank[2][:, c * P:(c + 1) * P], act_sb[:, t % 2, c * P:(c + 1) * P],
                                               ident[:, :])
                        ins.then_inc(acT_full, 1)
                        key = ("exp", L, GATE_SLOT[e][2])
                        if b == 0:
                            wait_unit(key, i)
                        pe.wait_ge(acT_ready, n + 2)
                        pe.wait_ge(y_used, n + 1)
                        wv = unit(key).rearrange("p (k n) -> p k n", k=2)
                        for half in range(2):
                            for c in range(2):
                                ins = mm(bank[4 + 2 * (t % 2) + half][:, :], actT[:, t % 2, c, :],
                                         wv[:, c, half * 512:(half + 1) * 512], c == 0, c == 1)
                        ins.then_inc(y_full, 1)

                    for t in range(6):
                        gate_up(t)
                        if t > 0:
                            down(t - 1)
                        if L < DEPTH - 1 and t in (2, 3, 5):
                            m = (2, 3, 5).index(t)
                            mod_unit(("mod", L, MODPOS[m]), 24 * (L + 1), i, m)
                    down(5)


def launch_io():
    ins = ["x_prompt", "x_sample", "cache_swa_k", "cache_swa_v", "cache_qkn_k", "cache_qkn_v", "cache_mla_ckv",
           "cache_mla_kpe", "c", "c_ctx", "w_mod", "b_mod", "norm_mix", "norm_ffn", "swa_wqkv", "swa_wo", "swa_sink",
           "qkn_wqkv", "qkn_wo", "qkn_qnorm", "qkn_knorm", "mla_wdq", "mla_qnorm", "mla_wuq", "mla_wdkv",
           "mla_kvnorm", "mla_wukv", "mla_wo", "w_router", "router_bias", "moe_w_gate", "moe_w_up", "moe_w_down",
           "final_norm"]
    outs = {"y_prompt": (1, 128, 1024), "y_sample": (1, 256, 1024), "state_swa_k": (1, 2, 128, 4, 64),
            "state_swa_v": (1, 2, 128, 4, 64), "state_qkn_k": (1, 1, 128, 4, 64), "state_qkn_v": (1, 1, 128, 4, 64),
            "state_mla_ckv": (1, 1, 128, 256), "state_mla_kpe": (1, 1, 128, 32)}
    return ins, outs


def kernel(**inputs):
    import concourse.bacc as bacc
    from concourse.bass_utils import run_bass_kernel_spmd

    nc = bacc.Bacc("TRN2", target_bir_lowering=False, num_devices=1)
    names, outs = launch_io()
    arrays, A = {}, {}
    given = {n: np.ascontiguousarray(inputs[n]) for n in names}
    given.update(host_constants())
    for name, a in given.items():
        arrays[f"in_{name}"] = a
        A[name] = nc.dram_tensor(f"in_{name}", a.shape, mybir.dt.from_np(a.dtype), kind="ExternalInput").ap()
    for name, shape in outs.items():
        A[name] = nc.dram_tensor(f"out_{name}", shape, F32, kind="ExternalOutput").ap()
    build(nc, A)
    r = run_bass_kernel_spmd(nc, [arrays], core_ids=[0])
    return tuple(r.results[0][f"out_{name}"] for name in outs)
```

```python
from contextlib import ExitStack

import numpy as np

import concourse.bass as bass
from concourse import mybir

F32 = mybir.dt.float32
U32 = mybir.dt.uint32
ALU = mybir.AluOpType
ACT = mybir.ActivationFunctionType
AX = mybir.AxisListType

P = 128
D = 1024
KC = D // P
DEPTH = 4
KINDS = [0, 1, 2, 0]
STACK = [0, 0, 0, 1]
NB = 3
COND = [0, 1, 1]
NT = NB * P
H, G, DH = 16, 4, 64
E, DE = 16, 256
UC = 256
R = 8
PAIRS = E // 2
SLOTS = P
STEPS = (NT // SLOTS - 1) * E
MODA, MODB = 4, 4
BIG = 1e6
MLA_Q, MLA_KV, ROPE, DQK = 384, 256, 32, 96
EPS = 1e-6
NEG = -1e30


def host_constants():
    tokens = np.arange(256)
    row, col = (tokens // 64).astype(np.float32), (tokens % 64).astype(np.float32)

    def rope(d):
        quarter = d // 4
        inv = np.float32(10000.0) ** (-np.arange(quarter, dtype=np.float32) / np.float32(quarter))
        ang = np.concatenate([row[:, None] * inv, col[:, None] * inv], axis=-1).astype(np.float32)
        both = np.stack([np.cos(ang), np.sin(ang)], axis=1).astype(np.float32)
        return both.reshape(2, P, d).transpose(1, 0, 2)

    r, c = np.arange(P)[:, None], np.arange(P)[None, :]
    masks = np.stack([np.where(c <= r, 0.0, NEG), np.where(c >= r, 0.0, NEG)], axis=1)
    sel = np.zeros((P, 2 * P + 2), np.float32)
    for s in range(2):
        sel[s::32, s * P:(s + 1) * P] = 1.0
        sel[s::32, 2 * P + s] = 1.0
    first = np.tile(np.concatenate([np.arange(16, 0, -1), np.arange(4, 0, -1)])[None], (P, 1))
    out = dict(ident=np.eye(P), masks=masks.reshape(P, 2 * P), rope64=rope(64).reshape(P, 128),
               rope32=rope(32).reshape(P, 64), sel=sel, first=first,
               before=r < c, iota=np.tile(np.arange(NT)[None], (P, 1)), token=r + P * np.arange(NB)[None])
    return {k: np.ascontiguousarray(v, dtype=np.float32) for k, v in out.items()}


def mixer_units(L):
    if KINDS[L] < 2:
        return [("qkv", u) for u in range(6)] + [("wo", u) for u in range(4)]
    return ([("dq", 0), ("dq", 1), ("dkv", 0), ("dkv", 1)] + [("uq", u) for u in range(3)]
            + [("ukv", u) for u in range(2)] + [("wo", u) for u in range(4)])


def plan_ring():
    fills, at, place = [0] * R, 0, {}
    def once(key):
        nonlocal at
        place[key] = (at % R, fills[at % R])
        fills[at % R] += 1
        at += 1

    for m in range(12):
        once(("mod0", m))
    for L in range(DEPTH):
        for name, u in mixer_units(L):
            once((name, L, u))
        for m in range(12 if L == 0 else 0):
            once(("mod0", 12 + m))
        for m in range(MODA if L < DEPTH - 1 else 0):
            once(("modA", L, m))
        for j in range(R):
            if j % 4 == 3 and L == DEPTH - 1:
                continue
            place[("exp", L, j)] = ((at + j) % R, fills[(at + j) % R])
            fills[(at + j) % R] += PAIRS
        for m in range(MODB if L < DEPTH - 1 else 0):
            once(("modB", L, m))
    return place


def plan_jobs():
    order = [("cond", "v"), ("gains", "v"), (("bias", 0), "v"), (("bias", 1), "v")]
    alt = "va"
    for L in range(DEPTH):
        order += [(("modc", L, s), "v") for s in ((0,) if L == 0 else (0, 1))]
        order += [(("gate", L, j), "v") for j in range(4 if L == 0 else 8)]
        order += [(("norm", 2 * L, k), alt[k % 2]) for k in range(KC)]
        if KINDS[L] < 2:
            order += [(("qkv", L, u, b), alt[(3 * u + b) % 2]) for u in range(6) for b in range(NB)]
            order += [(("qT", L, p), alt[p % 2]) for p in range(8)]
            order += [(("kT", L, g), alt[g % 2]) for g in range(G)]
            order += [(("S", L, h, i), "p") for h in range(H) for i in range(2)]
        else:
            order += [(("lat", L, u, b), alt[b % 2]) for u in range(4) for b in range(NB)]
            order += [(("qlT", L, c), "v") for c in range(3)] + [(("ckvT", L, c), "a") for c in range(2)]
            order += [(("kpeT", L), "v")]
            order += [(("uq", L, u, b), alt[b % 2]) for u in range(3) for b in range(NB)]
            order += [(("V", L, u, kb), alt[kb % 2]) for u in range(2) for kb in range(4)]
            for c in range(4):
                order += [(("kT", L, h), alt[h % 2]) for h in range(4 * c, 4 * c + 4)]
                order += [(("qT", L, h), alt[h % 2]) for h in range(4 * c, 4 * c + 4)]
                order += [(("S", L, h, i), "p") for h in range(4 * c, 4 * c + 4) for i in range(2)]
        order += [(("oT", L, k), alt[k % 2]) for k in range(KC)]
        order += [(("wo", L, u, b), "w") for u in range(4) for b in range(NB)]
        if L == 0:
            order += [(("modc", L, 1), "v")] + [(("gate", L, j), "v") for j in range(4, 8)]
        order += [(("norm", 2 * L + 1, k), alt[k % 2]) for k in range(KC)]
        order += [(("router", L), "a")]
        order += [(("hrow", L, b, half), alt[half]) for b in range(NB) for half in range(2)]
        order += [(("rank", L), "v")] + [(("idx", L, g), "v") for g in range(4)]
    jobs, count = {}, {"v": 0, "a": 0, "p": 0, "w": 0}
    for n, (key, eng) in enumerate(order):
        count[eng] += 0 if eng == "p" and key[3] == 1 else 1
        jobs[key] = (n, eng, count[eng])
    by_index = [jobs[key] for key, _ in order]
    return jobs, by_index


def build(nc, A):
    ring_place = plan_ring()
    jobs, job_at = plan_jobs()
    ctx = ExitStack()
    with ctx:
        def sb(name, shape):
            return ctx.enter_context(nc.sbuf_tensor(name, shape, F32))

        def sem(name):
            return ctx.enter_context(nc.semaphore(name))

        ring = sb("ring", [P, R, KC * UC])
        x = sb("x", [P, NB, D])
        xn = sb("xn", [P, NB, D])
        hT = sb("hT", [P, KC, NT])
        work = sb("work", [P, NB * 1536 + 8 * NT])
        V = sb("V", [P, 4, D])
        pp = sb("pp", [P, 2, 2, 896])
        kT = sb("kT", [P, 4, 4 * P])
        gbc = sb("gbc", [P, 2, 2, D])
        kc = sb("kc", [P, 4, 2, DH])
        ident = sb("ident", [P, P])
        masks = sb("masks", [P, 2, P])
        rope64 = sb("rope64", [P, 2, 2, 32])
        rope32 = sb("rope32", [P, 2, 2, 16])
        sel = sb("sel", [P, 2 * P + 2])
        first = sb("first", [P, 20])
        condT = sb("condT", [P, KC, 32])
        bT = sb("bT", [P, 2, 96])
        gT = sb("gT", [P, 67])
        modc = sb("modc", [P, 4, KC, 2])
        amul = sb("amul", [P, 2, KC, 2])
        wr = sb("wr", [P, KC, E])
        rbias = sb("rbias", [P, E])
        gains = sb("gains", [P, 2, DH])
        kvg = sb("kvg", [P, MLA_KV])
        small = sb("small", [P, 128])
        sink = sb("sink", [P, 2, 2, H])
        neg_max = sb("neg_max", [P, H, NB])
        den = sb("den", [P, H, NB])
        rden = sb("rden", [P, H, NB])
        esink = sb("esink", [P, H, NB])
        gates = sb("gates", [P, NB, E])
        before = sb("before", [P, P])
        ones = sb("ones", [P, P])
        iota = sb("iota", [P, NT])
        token = sb("token", [P, NB])
        slot_of = sb("slot_of", [P, NB, E])
        vals = sb("vals", [P, NB, E, 4])
        slotted = sb("slotted", [P, E, 4])
        idx = ctx.enter_context(nc.sbuf_tensor("idx", [P, 2, E], U32))
        idx_f = sb("idx_f", [P, 2, E])
        load = sb("load", [P, E])
        over_f = sb("over_f", [1, 2 * DEPTH + 2])
        over = ctx.enter_context(nc.sbuf_tensor("over", [1, 2 * DEPTH + 2], U32))
        ov_vals = sb("ov_vals", [P, NB, 4])
        ov_slotted = sb("ov_slotted", [P, 4])
        ov_idx = ctx.enter_context(nc.sbuf_tensor("ov_idx", [P, 2], U32))
        h_rows = nc.dram_tensor("h_rows", [NT, D], F32).ap()
        y_rows = nc.dram_tensor("y_rows", [2 * NT, D], F32).ap()

        qkv = work[:, 0:NB * 1536].rearrange("p (b n) -> p b n", b=NB)
        qT = work[:, NB * 1536:].rearrange("p (k n) -> p k n", k=8)
        rows = work[:, 0:6 * D]
        raw = xn[:, 0, 0:4 * P]
        Vw = V[:, :, :].rearrange("p a n -> p (a n)")
        xw = xn[:, :, :].rearrange("p a n -> p (a n)")
        y_sum, y_second = V[:, 0:NB, :], xn[:, :, :]
        member = Vw[:, 0:3072].rearrange("p (s b e n) -> p s b e n", s=2, b=NB, e=4)
        xg = hT[:, :, :].rearrange("p a n -> p (a n)")[:, 0:2 * D].rearrange("p (s n) -> p s n", s=2)
        ys = kT[:, :, :].rearrange("p a n -> p (a n)").rearrange("p (s n) -> p s n", s=2)
        ql = xn[:, 0:2, :].rearrange("p a n -> p (a n)")[:, 0:NB * MLA_Q].rearrange("p (b n) -> p b n", b=NB)
        qlT = hT[:, 0:3, :]
        ckvT = hT[:, 3:6, :].rearrange("p a n -> p (a n)")[:, 0:1024].rearrange("p (c n) -> p c n", c=2)
        wo_tmp = pp[:, 0, :, :].rearrange("p s n -> p (s n)")[:, 0:4 * UC].rearrange("p (s n) -> p s n", s=4)
        squares = pp[:, :, :, :].rearrange("p a s n -> p (a s n)")
        ckv = squares[:, 1408:2560].rearrange("p (b n) -> p b n", b=4)
        kpe = squares[:, 2560:2944].rearrange("p (b n) -> p b n", b=4)
        sil = squares[:, 0:512].rearrange("p (s n) -> p s n", s=2)
        act_sb = squares[:, 512:1024].rearrange("p (s n) -> p s n", s=2)
        actT = squares[:, 1024:1536].rearrange("p (s c n) -> p s c n", s=2, c=2)
        xT = squares[:, 1536:3584].rearrange("p (s k n) -> p s k n", s=2, k=KC)
        ov_w = [Vw[:, 0:2048].rearrange("p (k n) -> p k n", k=KC), Vw[:, 2048:4096].rearrange("p (k n) -> p k n", k=KC),
                xw[:, 0:2048].rearrange("p (k n) -> p k n", k=2)]
        ov_member = xw[:, 2048:2432].rearrange("p (b n) -> p b n", b=NB)
        rt = kT[:, :, :].rearrange("p a n -> p (a n)")[:, 0:12 * NB * E].rearrange(
            "p (a b e) -> p a b e", a=12, b=NB)

        bank = [ctx.enter_context(nc.psum_tensor(f"bank{i}", [P, 512], F32)) for i in range(8)]

        slot_full = [sem(f"slot_full{s}") for s in range(R)]
        slot_used = [sem(f"slot_used{s}") for s in range(R)]
        bank_full, freed_v, freed_a = sem("bank_full"), sem("freed_v"), sem("freed_a")
        const_in, cond_in, x_in, cache_in, bmod_in, out_done = (sem(s) for s in
            ("const_in", "cond_in", "x_in", "cache_in", "bmod_in", "out_done"))
        v_chain, a_chain, p_chain = sem("v_chain"), sem("a_chain"), sem("p_chain")
        raw_silu, raw_ready, mod_ready, mod_full, rows_done = (sem(s) for s in
            ("raw_silu", "raw_ready", "mod_ready", "mod_full", "rows_done"))
        sumsq, rstd_ready, xn_ready, wo_mul, x_mixed, x_moe, x_moe_v, moe_mul = (sem(s) for s in
            ("sumsq", "rstd_ready", "xn_ready", "wo_mul", "x_mixed", "x_moe", "x_moe_v", "moe_mul"))
        head_sq, head_ms, head_rstd, roped_v, roped_p, qk_ready = (sem(s) for s in
            ("head_sq", "head_ms", "head_rstd", "roped_v", "roped_p", "qk_ready"))
        max_ready, probs, pt_full, pt_a, pt_v, o_full, o_ready, esink_in, esink_done = (sem(s) for s in
            ("max_ready", "probs", "pt_full", "pt_a", "pt_v", "o_full", "o_ready", "esink_in", "esink_done"))
        lat_sq, lat_rstd, states = (sem(s) for s in ("lat_sq", "lat_rstd", "states"))
        freed = {"v": freed_v, "a": freed_a, "p": probs, "w": wo_mul}
        (gates_ready, au_full, sil_full, act_full, acT_full, acT_ready, y_full, y_a, y_v, ys_free) = (sem(s) for s in
            ("gates_ready", "au_full", "sil_full", "act_full", "acT_full", "acT_ready", "y_full", "y_a", "y_v",
             "ys_free"))
        member_ready, idx_ready, over_ready, h_out, xT_full, xT_a, xT_v, y_in, work_free = (sem(s) for s in
            ("member_ready", "idx_ready", "over_ready", "h_out", "xT_full", "xT_a", "xT_v", "y_in", "work_free"))
        g_in, y_out = [sem("g_in0"), sem("g_in1")], [sem("y_out0"), sem("y_out1")]
        (ov_member_ready, ov_idx_full, ov_idx_ready, ov_g_in, ov_xT_full, ov_xT_ready, ov_w_in, ov_au_full, ov_sil,
         ov_act, ov_acT_full, ov_acT_ready, ov_y_full, ov_y, ov_y_out) = (sem(s) for s in
            ("ov_member_ready", "ov_idx_full", "ov_idx_ready", "ov_g_in", "ov_xT_full", "ov_xT_ready", "ov_w_in",
             "ov_au_full", "ov_sil", "ov_act", "ov_acT_full", "ov_acT_ready", "ov_y_full", "ov_y", "ov_y_out"))
        ov_chain, ov_done, ov_issued = sem("ov_chain"), sem("ov_done"), sem("ov_issued")

        def job_bank(key):
            return bank[jobs[key][0] % 4]

        def wait_bank_free(pe, key):
            n = jobs[key][0]
            if n >= 4:
                _, eng, cnt = job_at[n - 4]
                pe.wait_ge(freed[eng], cnt)

        def wait_bank_full(eng, key):
            eng.wait_ge(bank_full, jobs[key][0] + 1)

        def wait_evacuated(eng, *keys):
            for name in "va":
                cnt = [jobs[k][2] for k in keys if jobs[k][1] == name]
                if cnt:
                    eng.wait_ge(freed[name], max(cnt))

        def unit(key):
            return ring[:, ring_place[key][0], :]

        def pass_on(eng, ukey):
            eng.sem_inc(slot_used[ring_place[ukey][0]], 1)

        LAT = (("dq", 0, 256), ("dq", 1, 128), ("dkv", 0, 256), ("dkv", 1, 32))

        def last_reader_of(key):
            if key[0] in ("qkv", "wo", "uq") and key[3] == 2:
                return key[:3]
            if key[0] == "lat" and key[3] == 2:
                return (LAT[key[2]][0], key[1], LAT[key[2]][1])
            if key[0] == "kT" and KINDS[key[1]] == 2 and key[2] % 8 == 7:
                return ("ukv", key[1], key[2] // 8)
            return None

        def mine(key, name):
            return jobs[key][1] == name

        SW = {0: 0, 3: 1}
        CHUNKS = {L: ([range(H)] if KINDS[L] < 2 else [range(4 * c, 4 * c + 4) for c in range(4)])
                  for L in range(DEPTH)}

        PARTS = [(1, 0, 0, 384), (0, 0, 384, 128), (2, 1, 0, 384)]

        def rope(eng, ops, heads, table, half, scratch, link, done):
            n = heads.shape[1]
            x1, x2 = heads[:, :, 0:half], heads[:, :, half:2 * half]
            cos = table[:, 0, :].unsqueeze(1).to_broadcast([P, n, half])
            sin = table[:, 1, :].unsqueeze(1).to_broadcast([P, n, half])
            t = [scratch[:, j * n * half:(j + 1) * n * half].rearrange("p (h d) -> p h d", d=half) for j in range(4)]
            ops.tensor_tensor(t[0], x1, cos, ALU.mult)
            ops.tensor_tensor(t[1], x2, sin, ALU.mult)
            ops.tensor_tensor(t[2], x2, cos, ALU.mult)
            link(ops.tensor_tensor(t[3], x1, sin, ALU.mult))
            ops.tensor_tensor(x1, t[0], t[1], ALU.subtract)
            ops.tensor_tensor(x2, t[2], t[3], ALU.add).then_inc(done, 1)

        def dest(key):
            ps = job_bank(key)
            if key[0] == "qkv":
                _, L, u, b = key
                if u < 4:
                    return qkv[:, b, u * UC:(u + 1) * UC], ps[:, 0:UC]
                if u == 4:
                    return (qkv[:, b, 1024:1536].rearrange("p (g t d) -> p g t d", g=G, t=2),
                            ps[:, 0:UC].rearrange("p (g d) -> p g d", g=G).unsqueeze(2).to_broadcast([P, G, 2, DH]))
                return V[:, b, 0:UC], ps[:, 0:UC]
            if key[0] == "lat":
                _, L, u, b = key
                if u < 2:
                    n = (256, 128)[u]
                    return ql[:, b, u * 256:u * 256 + n], ps[:, 0:n]
                n = (256, 32)[u - 2]
                return ckv[:, b, (u - 2) * 256:(u - 2) * 256 + n], ps[:, 0:n]
            if key[0] == "uq":
                _, L, u, b = key
                return qkv[:, b, u * 512:(u + 1) * 512], ps[:, :]
            if key[0] == "V":
                _, L, u, kb = key
                return V[:, kb, u * 512:(u + 1) * 512], ps[:, :]
            if key[0] == "ckvT":
                return ckvT[:, key[2], :], ps[:, :]
            if key[0] == "kT":
                if KINDS[key[1]] < 2:
                    return kT[:, key[2], :], ps[:, :]
                return kT[0:64, key[2] % 4, :], ps[0:64, :]
            if key[0] == "oT":
                return hT[:, key[2], :], ps[:, 0:NT]
            if key[0] == "hrow":
                return xn[:, key[2], key[3] * 512:(key[3] + 1) * 512], ps[:, :]
            raise KeyError(key)

        def further_passes(eng, L, step):
            eng.wait_ge(over_ready, L + 1)
            flag = eng.value_load(over[0:1, L:L + 1], min_val=0, max_val=1)
            with eng.If(flag > 0):
                gone = eng.value_load(over[0:1, DEPTH + L:DEPTH + L + 1], min_val=0, max_val=STEPS * (DEPTH - 1))
                with eng.Fori(0, NT // SLOTS - 1) as q:
                    with eng.Fori(0, E) as e:
                        step(eng.snap(gone + q * E + e), q, e)

        def each_pair(eng, body):
            with eng.Fori(0, PAIRS - 1) as i:
                body(i, False)
            body(PAIRS - 1, True)

        def turn_act(act, n, slot):
            act.wait_ge(acT_full, n + 1)
            nc.scalar.copy(actT[:, slot], bank[2][:, 0:2 * P].rearrange("p (c n) -> p c n", c=2)).then_inc(acT_ready, 1)

        block = ctx.enter_context(nc.Block())

        @block.sync
        def _(sp):
            def fill(key, src, dst_cols, i=None, shape=None):
                slot, before = ring_place[key]
                n = before if i is None else before + i
                sp.wait_ge(slot_used[slot], n + 1)
                dst = ring[:, slot, 0:dst_cols]
                if shape is not None:
                    dst = dst.rearrange("p (k n) -> p k n", k=shape)
                sp.dma_start(dst, src).then_inc(slot_full[slot], 16)

            def cols(w, n0, n):
                return w[:, n0:n0 + n].rearrange("(k p) n -> p k n", p=P)

            def fill_mod(key, L, m, i=None):
                src = A["w_mod"][L, :, bass.ds(m * UC, UC)] if i is not None else A["w_mod"][L, :, m * UC:(m + 1) * UC]
                fill(key, src.rearrange("(k p) n -> p k n", p=P), KC * UC, i, KC)

            for slot in range(R):
                sp.sem_inc(slot_used[slot], 1)
            for m in range(12):
                fill_mod(("mod0", m), 0, m)
            for L in range(DEPTH):
                s = STACK[L]
                for name, u in mixer_units(L):
                    key = (name, L, u)
                    if name == "qkv":
                        w = A["swa_wqkv" if KINDS[L] == 0 else "qkn_wqkv"][s]
                        fill(key, cols(w, u * UC, UC), KC * UC, None, KC)
                    elif name == "wo":
                        w = A[("swa_wo", "qkn_wo", "mla_wo")[KINDS[L]]][s]
                        fill(key, cols(w, u * UC, UC), KC * UC, None, KC)
                    elif name == "dq":
                        n = (256, 128)[u]
                        fill(key, cols(A["mla_wdq"][s], u * 256, n), KC * n, None, KC)
                    elif name == "dkv":
                        n = (256, 32)[u]
                        fill(key, cols(A["mla_wdkv"][s], u * 256, n), KC * n, None, KC)
                    elif name == "uq":
                        fill(key, cols(A["mla_wuq"][s], u * 512, 512), 3 * 512, None, 3)
                    elif name == "ukv":
                        fill(key, cols(A["mla_wukv"][s], u * 1024, 1024), 2 * 1024, None, 2)
                for m in range(12 if L == 0 else 0):
                    fill_mod(("mod0", 12 + m), 0, 12 + m)
                for m in range(MODA if L < DEPTH - 1 else 0):
                    fill_mod(("modA", L, m), L + 1, m)
                with sp.Fori(0, PAIRS) as i:
                    for j in range(R):
                        e, w = j // 4, j % 4
                        if w == 3:
                            if L < DEPTH - 1:
                                fill_mod(("exp", L, j), L + 1, i * 2 + e + MODA, i)
                            continue
                        src = A[("moe_w_gate", "moe_w_up", "moe_w_down")[w]][L, bass.ds(i * 2 + e, 1), :, :].rearrange(
                            "e (k p) n -> p (e k) n", p=P)
                        fill(("exp", L, j), src, KC * UC, i, (KC, KC, 2)[w])
                for m in range(MODB if L < DEPTH - 1 else 0):
                    fill_mod(("modB", L, m), L + 1, MODA + E + m)

                def step(n, q, e):
                    sp.wait_ge(ov_y_full, n + 1)
                    for w in range(3):
                        src = A[("moe_w_gate", "moe_w_up", "moe_w_down")[w]][L, bass.ds(e, 1), :, :].rearrange(
                            "e (k p) n -> p (e k) n", p=P)
                        sp.dma_start(ov_w[w], src).then_inc(ov_w_in, 16)

                sp.wait_ge(idx_ready, 4 * (L + 1))
                sp.wait_ge(h_out, 16 * (L + 1))
                further_passes(sp, L, step)
                sp.wait_ge(y_in, 32 * (L + 1))

        @block.gpsimd
        def _(pool):
            chain = [0]

            def link(ins):
                chain[0] += 1
                ins.then_inc(p_chain, 1)
                pool.wait_ge(p_chain, chain[0])

            def rms_power(ss, out, n, done):
                link(nc.gpsimd.tensor_scalar(out, ss, 1.0 / n, EPS, ALU.mult, ALU.add))
                nc.gpsimd.tensor_tensor(out, out, exponent(out), ALU.pow).then_inc(done, 1)

            def exponent(like):
                n = 1
                for d in like.shape[1:]:
                    n *= d
                e = minus_half[:, 0:n]
                if len(like.shape) == 3:
                    e = e.rearrange("p (a b) -> p a b", a=like.shape[1])
                return e

            def gate_bias(L):
                for g in range(2):
                    for c in range(2):
                        pool.dma_start(gbc[:, g, c, :], A["b_mod"][L, (2, 5)[g] * D:(3, 6)[g] * D]
                                       .partition_broadcast(P)).then_inc(bmod_in, 16)

            minus_half = small[:, 56:128]
            link(nc.gpsimd.memset(minus_half, -0.5))
            link(nc.gpsimd.memset(ones[:, :], 1.0))
            pool.sem_inc(ys_free, 2)
            pool.sem_inc(ov_done, 1)
            pool.dma_start(x[:, 0, :], A["x_prompt"][0]).then_inc(x_in, 16)
            pool.dma_start(x[:, 1:3, :], A["x_sample"][0].rearrange("(b p) d -> p b d", p=P)).then_inc(x_in, 16)
            gate_bias(0)

            last_token, last_pick = pool.to_reg(NT - 1), pool.to_reg(2 * NT - 1)

            def rows_at(ap):
                return bass.IndirectOffsetOnAxis(ap=ap, axis=0)

            def norm_power(n):
                pool.wait_ge(sumsq, 3 * n + 3)
                rms_power(small[:, 0:3], small[:, 4:7], D, rstd_ready)

            nsq = 0
            for L in range(DEPTH):
                s, kind = STACK[L], KINDS[L]
                if L > 0:
                    pool.wait_ge(x_moe, 3 * L)
                    pool.wait_ge(x_moe_v, 3 * L)
                if KINDS[L] < 2:
                    ck, cv = (("cache_swa_k", "cache_swa_v"), ("cache_qkn_k", "cache_qkn_v"))[KINDS[L]]
                    for dup in range(2):
                        pool.dma_start(kc[:, :, dup, :], A[ck][0, s]).then_inc(cache_in, 16)
                    pool.dma_start(V[:, 3, 0:256], A[cv][0, s].rearrange("t g d -> t (g d)")).then_inc(cache_in, 16)
                norm_power(2 * L)
                if KINDS[L] == 1:
                    for b in range(NB):
                        pool.wait_ge(head_ms, b + 1)
                        rms_power(small[:, 8:32], small[:, 32:56], DH, head_rstd)
                if KINDS[L] < 2:
                    if KINDS[L] == 0:
                        wait_evacuated(pool, *[("qkv", L, u, 2) for u in range(5)])
                    else:
                        pool.wait_ge(qk_ready, 3)
                    rope(pool, nc.gpsimd, qkv[:, 2, :].rearrange("p (h d) -> p h d", d=DH), rope64[:, 1], 32,
                         squares, link, roped_p)
                else:
                    pool.dma_start(ckv[:, 3, 0:256], A["cache_mla_ckv"][0, s]).then_inc(cache_in, 16)
                    link(nc.gpsimd.memset(kpe[:, :, :], 0.0))
                    pool.dma_start(kpe[:, 3, 64:96], A["cache_mla_kpe"][0, s]).then_inc(cache_in, 16)
                    pool.wait_ge(lat_sq, 1)
                    rms_power(small[:, 8:14], small[:, 14:20], 1, lat_rstd)
                if kind < 2:
                    sk, sv = (("state_swa_k", "state_swa_v"), ("state_qkn_k", "state_qkn_v"))[kind]
                    wait_evacuated(pool, ("qkv", L, 4, 0), ("qkv", L, 5, 0))
                    pool.dma_start(A[sk][0, s], qkv[:, 0, 1024:1536].rearrange("p (g t d) -> p g t d", g=G, t=2)
                                   [:, :, 0, :]).then_inc(states, 16)
                    pool.dma_start(A[sv][0, s].rearrange("t g d -> t (g d)"), V[:, 0, 0:256]).then_inc(states, 16)
                else:
                    pool.wait_ge(roped_v, 4)
                    pool.dma_start(A["state_mla_ckv"][0, s], ckv[:, 0, 0:256]).then_inc(states, 16)
                    pool.dma_start(A["state_mla_kpe"][0, s], kpe[:, 0, 64:96]).then_inc(states, 16)
                for u in range(4):
                    for b in range(NB):
                        g = 12 * L + 3 * u + b
                        pool.wait_ge(wo_mul, g + 1)
                        xs = x[:, b, u * UC:(u + 1) * UC]
                        nc.gpsimd.tensor_tensor(xs, xs, wo_tmp[:, g % 4, :], ALU.add).then_inc(x_mixed, 1)
                pool.wait_ge(x_mixed, 12 * L + 12)
                pool.wait_ge(states, 32 * (L + 1))
                pool.sem_inc(work_free, 1)
                norm_power(2 * L + 1)
                wait_evacuated(pool, *[("hrow", L, b, half) for b in range(NB) for half in range(2)])
                pool.dma_start(h_rows.rearrange("(b p) d -> p b d", p=P), xn[:, :, :]).then_inc(h_out, 16)
                pool.wait_ge(h_out, 16 * (L + 1))

                def gather(e):
                    pool.wait_ge(idx_ready, 4 * L + e // 4 + 1)
                    if e >= 2:
                        pool.wait_ge(xT_full, E * L + e - 1)
                    nc.gpsimd.indirect_dma_start(xg[:, e % 2, :], None, h_rows, rows_at(idx[:, 0, e:e + 1]),
                                                 bounds_check=last_token, oob_is_err=False).then_inc(g_in[e % 2], 16)

                def scattered(e):
                    pool.wait_ge(y_out[e % 2], 16 * (E // 2 * L + e // 2 + 1))
                    pool.sem_inc(ys_free, 1)

                gather(0)
                gather(1)
                for e in range(E):
                    if e + 2 < E:
                        gather(e + 2)
                    if e > 0:
                        scattered(e - 1)
                    pool.wait_ge(y_a, E * L + e + 2)
                    pool.wait_ge(y_v, E * L + e + 2)
                    nc.gpsimd.indirect_dma_start(y_rows, rows_at(idx[:, 1, e:e + 1]), ys[:, e % 2, :], None,
                                                 bounds_check=last_pick, oob_is_err=False).then_inc(y_out[e % 2], 16)
                scattered(E - 1)

                def step(n, q, e):
                    pool.wait_ge(ov_idx_ready, n + 1)
                    pool.sem_inc(ov_issued, 1)
                    nc.gpsimd.indirect_dma_start(xg[:, 0, :], None, h_rows, rows_at(ov_idx[:, 0:1]),
                                                 bounds_check=last_token, oob_is_err=False).then_inc(ov_g_in, 16)
                    pool.wait_ge(ov_y, n + 1)
                    pool.sem_inc(ov_issued, 1)
                    nc.gpsimd.indirect_dma_start(y_rows, rows_at(ov_idx[:, 1:2]), ys[:, 0, :], None,
                                                 bounds_check=last_pick, oob_is_err=False).then_inc(ov_y_out, 16)
                    pool.wait_ge(ov_y_out, (n + 1) * 16)
                    pool.sem_inc(ov_done, 1)

                further_passes(pool, L, step)
                for k, dst in enumerate((y_sum, y_second)):
                    pool.dma_start(dst, y_rows[k * NT:(k + 1) * NT, :].rearrange("(b p) d -> p b d", p=P))\
                        .then_inc(y_in, 16)
                for b in range(NB):
                    pool.wait_ge(moe_mul, 3 * L + b + 1)
                    nc.gpsimd.tensor_tensor(x[:, b, 640:], x[:, b, 640:], y_sum[:, b, 640:], ALU.add)\
                        .then_inc(x_moe, 1)
                if L < DEPTH - 1:
                    gate_bias(L + 1)
            pool.dma_start(gbc[:, 0, 0, :], A["final_norm"].partition_broadcast(P)).then_inc(x_in, 16)
            norm_power(2 * DEPTH)
            pool.wait_ge(xn_ready, 3 * (2 * DEPTH + 1) + 1)
            pool.dma_start(A["y_prompt"][0], xn[:, 0, :]).then_inc(out_done, 16)
            pool.dma_start(A["y_sample"][0].rearrange("(b p) d -> p b d", p=P), xn[:, 1:3, :]).then_inc(out_done, 16)
            pool.wait_ge(out_done, 32)
            pool.wait_ge(states, 32 * DEPTH)

        @block.scalar
        def _(act):
            chain = [0]

            def link(ins):
                chain[0] += 1
                ins.then_inc(a_chain, 1)
                act.wait_ge(a_chain, chain[0])

            def free(ins):
                ins.then_inc(freed_a, 1)

            def evacuate(*keys):
                for key in keys:
                    if mine(key, "a"):
                        wait_bank_full(act, key)
                        if last_reader_of(key):
                            pass_on(act, last_reader_of(key))
                        free(nc.scalar.copy(*dest(key)))

            def norm_in(n, L, odd):
                for b in range(NB):
                    if n == 0:
                        act.wait_ge(x_in, 32)
                    elif odd:
                        act.wait_ge(x_mixed, 12 * L + 9 + b + 1)
                    else:
                        act.wait_ge(x_moe, 3 * (L - 1) + b + 1)
                        act.wait_ge(x_moe_v, 3 * (L - 1) + b + 1)
                    nc.scalar.activation(xn[:, b, :], x[:, b, :], ACT.Square,
                                         accum_out=small[:, b:b + 1]).then_inc(sumsq, 1)

            def norm_out(n, s):
                for k in range(KC):
                    key = ("norm", n, k)
                    if mine(key, "a"):
                        wait_bank_full(act, key)
                        act.wait_ge(mod_ready, n + 1)
                        ps = job_bank(key)
                        nc.scalar.activation(hT[:, k, 0:P], ps[:, 0:P], ACT.Identity,
                                             bias=modc[:, 2 * s, k, 0:1], scale=amul[:, s, k, 0:1])
                        free(nc.scalar.activation(hT[:, k, P:NT], ps[:, P:NT], ACT.Identity,
                                                  bias=modc[:, 2 * s, k, 1:2], scale=amul[:, s, k, 1:2]))

            def mod_rows(key, base, m):
                act.wait_ge(mod_full, base + m + 1)
                pass_on(act, key)
                at = slice(m * UC, (m + 1) * UC) if type(m) is int else bass.ds(m * UC, UC)
                nc.scalar.copy(rows[:, at], bank[3][:, 0:UC]).then_inc(rows_done, 1)

            def load(eng, pairs, done):
                for dst, src in pairs:
                    eng.dma_start(dst, src).then_inc(done, 16)

            load(act, ((raw[0:8, 0:P], A["c_ctx"].rearrange("(k p) -> k p", p=P)),
                       (raw[8:16, 0:P], A["c"].rearrange("a (k p) -> (a k) p", p=P)),
                       (ident[:, :], A["ident"]),
                       (raw[0:32, P:2 * P], A["norm_mix"].rearrange("l (k p) -> (l k) p", p=P)),
                       (raw[32:64, P:2 * P], A["norm_ffn"].rearrange("l (k p) -> (l k) p", p=P)),
                       (raw[64:67, P:2 * P], A["mla_qnorm"].rearrange("l (k p) -> (l k) p", p=P)),
                       (raw[0:96, 2 * P:3 * P], A["b_mod"][0:2].rearrange("l (k p) -> (l k) p", p=P)),
                       (raw[0:96, 3 * P:4 * P], A["b_mod"][2:4].rearrange("l (k p) -> (l k) p", p=P))), cond_in)
            load(act, ((masks[:, :, :], A["masks"].rearrange("p (a n) -> p a n", a=2)),
                       (rope64[:, :, :, :], A["rope64"].rearrange("p (a c n) -> p a c n", a=2, c=2)),
                       (rope32[:, :, :, :], A["rope32"].rearrange("p (a c n) -> p a c n", a=2, c=2)),
                       (sel[:, :], A["sel"]), (first[:, :], A["first"]),
                       (before[:, :], A["before"]), (iota[:, :], A["iota"]), (token[:, :], A["token"]),
                       (wr[:, :, :], A["w_router"].rearrange("(k p) e -> p k e", p=P)),
                       (rbias[:, :], A["router_bias"].partition_broadcast(P)),
                       (gains[:, 0, :], A["qkn_qnorm"][0].partition_broadcast(P)),
                       (gains[:, 1, :], A["qkn_knorm"][0].partition_broadcast(P)),
                       (kvg[:, :], A["mla_kvnorm"][0].partition_broadcast(P)),
                       (sink[:, 0, 0, :], A["swa_sink"][0].partition_broadcast(P)),
                       (sink[:, 1, 0, :], A["swa_sink"][1].partition_broadcast(P))), const_in)
            act.sem_inc(rows_done, 1)
            act.sem_inc(acT_ready, 1)
            act.sem_inc(y_a, 1)
            act.sem_inc(xT_a, 1)
            act.sem_inc(ov_y_full, 1)
            act.wait_ge(cond_in, 16 * 8)
            nc.scalar.activation(raw[0:16, 0:P], raw[0:16, 0:P], ACT.Silu).then_inc(raw_silu, 1)
            for m in range(12):
                mod_rows(("mod0", m), 0, m)

            for L in range(DEPTH):
                kind, s = KINDS[L], STACK[L]
                norm_in(2 * L, L, False)
                norm_out(2 * L, 0)
                if kind < 2:
                    evacuate(*[("qkv", L, u, b) for u in range(6) for b in range(NB)])
                    if kind == 1:
                        for b in range(NB):
                            wait_evacuated(act, *[("qkv", L, u, b) for u in range(5)])
                            if b > 0:
                                act.wait_ge(head_ms, b)
                            nc.scalar.activation(squares[:, 0:1536], qkv[:, b, :], ACT.Square).then_inc(head_sq, 1)
                else:
                    evacuate(*[("lat", L, u, b) for u in range(4) for b in range(NB)])
                    wait_evacuated(act, *[("lat", L, u, b) for u in range(4) for b in range(NB)])
                    for b in range(NB):
                        nc.scalar.activation(squares[:, 448 * b:448 * b + 384], ql[:, b, :], ACT.Square, scale=384 ** -0.5,
                                             accum_out=small[:, 8 + b:9 + b])
                        last = nc.scalar.activation(kT[:, b, 0:256], ckv[:, b, 0:256], ACT.Square,
                                                    scale=256 ** -0.5, accum_out=small[:, 11 + b:12 + b])
                    last.then_inc(lat_sq, 1)
                    evacuate(*[("ckvT", L, c) for c in range(2)])
                    evacuate(*[("uq", L, u, b) for u in range(3) for b in range(NB)])
                    evacuate(*[("V", L, u, kb) for u in range(2) for kb in range(4)])
                if kind == 2:
                    act.wait_ge(states, 32 * (L + 1))
                qscale = (DH if kind < 2 else DQK) ** -0.5
                for heads in CHUNKS[L]:
                    keys = ([("qT", L, p) for p in range(8)] + [("kT", L, g) for g in range(G)] if kind < 2 else
                            [("kT", L, h) for h in heads] + [("qT", L, h) for h in heads])
                    for key in keys:
                        if not mine(key, "a"):
                            continue
                        if key[0] == "kT":
                            evacuate(key)
                            continue
                        wait_bank_full(act, key)
                        rws = P if kind < 2 else DQK
                        free(nc.scalar.mul(qT[0:rws, key[2] % 8, :], job_bank(key)[0:rws, 0:NT], qscale))

                    def turn(h):
                        n = L * H + h
                        act.wait_ge(pt_full, 2 * n + 1)
                        nc.scalar.copy(pp[:, 1, h % 2, 0:512], bank[4][:, :]).then_inc(pt_a, 1)

                    for h in heads:
                        n = L * H + h
                        act.wait_ge(max_ready, n + 1)
                        if h >= 2:
                            act.wait_ge(pt_full, 2 * (n - 2) + 2)
                        if kind == 0:
                            nc.scalar.activation(esink[:, h, :], neg_max[:, h, :], ACT.Exp,
                                                 bias=sink[:, SW[L], 0, h:h + 1])
                        for b, i, c0, w in PARTS:
                            ins = nc.scalar.activation(pp[:, 0, h % 2, 512 * i + c0:512 * i + c0 + w],
                                                       job_bank(("S", L, h, i))[:, c0:c0 + w], ACT.Exp,
                                                       bias=neg_max[:, h, b:b + 1], accum_out=den[:, h, b:b + 1])
                        ins.then_inc(probs, 1)
                        if h > heads[0]:
                            turn(h - 1)
                    turn(heads[-1])
                evacuate(*[("oT", L, k) for k in range(KC)])
                for m in range(12 if L == 0 else 0):
                    mod_rows(("mod0", 12 + m), 0, 12 + m)
                norm_in(2 * L + 1, L, True)
                norm_out(2 * L + 1, 1)
                wait_bank_full(act, ("router", L))
                free(nc.scalar.activation(rt[:, 0], job_bank(("router", L))[:, 0:NB * E].rearrange(
                    "p (b e) -> p b e", b=NB), ACT.Sigmoid))
                evacuate(*[("hrow", L, b, half) for b in range(NB) for half in range(2)])
                act.wait_ge(work_free, L + 1)
                for m in range(MODA if L < DEPTH - 1 else 0):
                    mod_rows(("modA", L, m), 24 * (L + 1), m)

                def turned_rows(n, slot):
                    act.wait_ge(xT_full, n + 1)
                    nc.scalar.copy(xT[:, slot, 0:4, :], bank[6][:, :].rearrange("p (k n) -> p k n", k=4))\
                        .then_inc(xT_a, 1)

                def pair(i, last):
                    for e in range(2):
                        n = i * 2 + (E * L + e)
                        act.wait_ge(au_full, n + 1)
                        pass_on(act, ("exp", L, 4 * e))
                        pass_on(act, ("exp", L, 4 * e + 1))
                        act.wait_ge(act_full, n + 1)
                        nc.scalar.activation(sil[:, e, :], bank[e][:, 0:DE], ACT.Silu).then_inc(sil_full, 1)
                        if L < DEPTH - 1:
                            mod_rows(("exp", L, 4 * e + 3), 24 * (L + 1), i * 2 + (MODA + e))
                        turn_act(act, n, e)
                        if not (last and e == 1):
                            turned_rows(n + 1, 1 - e)
                        act.wait_ge(y_full, n + 1)
                        act.wait_ge(ys_free, n + 1)
                        at = slotted[:, bass.ds(i * 2 + e, 1), 3] if type(i) is not int else slotted[:, 2 * i + e, 3:4]
                        nc.scalar.mul(ys[:, e, 0:512], bank[4][:, :], at).then_inc(y_a, 1)

                turned_rows(E * L, 0)
                each_pair(act, pair)
                for m in range(MODB if L < DEPTH - 1 else 0):
                    mod_rows(("modB", L, m), 24 * (L + 1), MODA + E + m)

                def step(n, q, e):
                    act.wait_ge(ov_au_full, n + 1)
                    nc.scalar.activation(sil[:, 0, :], bank[0][:, 0:DE], ACT.Silu).then_inc(ov_sil, 1)
                    act.wait_ge(ov_acT_full, n + 1)
                    nc.scalar.copy(actT[:, 0], bank[2][:, 0:2 * P].rearrange("p (c n) -> p c n", c=2))\
                        .then_inc(ov_acT_ready, 1)

                further_passes(act, L, step)
            norm_in(2 * DEPTH, DEPTH, False)

        @block.vector
        def _(dve):
            V_ = nc.vector
            chain = [0]

            def link(ins):
                chain[0] += 1
                ins.then_inc(v_chain, 1)
                dve.wait_ge(v_chain, chain[0])

            def free(ins):
                ins.then_inc(freed_v, 1)

            def evacuate(*keys):
                for key in keys:
                    if mine(key, "v"):
                        wait_bank_full(dve, key)
                        if last_reader_of(key):
                            pass_on(dve, last_reader_of(key))
                        free(V_.tensor_copy(*dest(key)))

            def norm_scale(n):
                dve.wait_ge(rstd_ready, n + 1)
                for b in range(NB):
                    V_.tensor_scalar(xn[:, b, :], x[:, b, :], small[:, 4 + b:5 + b], None,
                                     ALU.mult).then_inc(xn_ready, 1)

            def norm_out(n, s):
                for k in range(KC):
                    key = ("norm", n, k)
                    if mine(key, "v"):
                        wait_bank_full(dve, key)
                        ps = job_bank(key)
                        V_.tensor_scalar(hT[:, k, 0:P], ps[:, 0:P], amul[:, s, k, 0:1], modc[:, 2 * s, k, 0:1],
                                         ALU.mult, ALU.add)
                        free(V_.tensor_scalar(hT[:, k, P:NT], ps[:, P:NT], amul[:, s, k, 1:2],
                                              modc[:, 2 * s, k, 1:2], ALU.mult, ALU.add))

            link(V_.memset(condT[:, :, :], 0.0))
            for key, dst, n in (("cond", condT[:, :, 0:2].rearrange("p k c -> p c k"), 16), ("gains", gT[:, :], 67),
                                (("bias", 0), bT[:, 0, :], 96), (("bias", 1), bT[:, 1, :], 96)):
                wait_bank_full(dve, key)
                src = job_bank(key)[:, 0:n]
                free(V_.tensor_copy(dst, src.rearrange("p (c k) -> p c k", c=2) if n == 16 else src))
            dve.wait_ge(const_in, 16 * 15)
            for w in range(2):
                V_.tensor_scalar(sink[:, w, 1, :], sink[:, w, 0, :], -1.0, None, ALU.mult)
            dve.sem_inc(act_full, 2)
            dve.sem_inc(y_v, 1)
            dve.sem_inc(xT_v, 1)
            link(V_.memset(over_f[:, :], 0.0))

            def mod_columns(L, s):
                key = ("modc", L, s)
                wait_bank_full(dve, key)
                b = bT[:, L // 2, 48 * (L % 2) + 24 * s:48 * (L % 2) + 24 * s + 16].rearrange("p (v k) -> p v k", v=2)
                free(V_.tensor_tensor(modc[:, 2 * s:2 * s + 2],
                                      job_bank(key)[:, 0:32].rearrange("p (v k c) -> p v k c", v=2, k=KC),
                                      b.unsqueeze(3).to_broadcast([P, 2, KC, 2]), ALU.add))
                dve.wait_ge(freed_v, jobs[key][2])
                g = gT[:, 32 * s + 8 * L:32 * s + 8 * L + 8].unsqueeze(2).to_broadcast([P, KC, 2])
                V_.scalar_tensor_tensor(out=amul[:, s], in0=modc[:, 2 * s + 1], scalar=1.0, in1=g,
                                        op0=ALU.add, op1=ALU.mult).then_inc(mod_ready, 1)
                dve.wait_ge(mod_ready, 2 * L + s + 1)

            def spread_gates(L, g):
                dve.wait_ge(bmod_in, 64 * (L + 1))
                for j in range(4 * g, 4 * g + 4):
                    key = ("gate", L, j)
                    wait_bank_full(dve, key)
                    dst = gbc[:, g, j // 2 % 2, j % 2 * 512:(j % 2 + 1) * 512]
                    free(V_.tensor_tensor(dst, dst, job_bank(key)[:, :], ALU.add))

            def route(L):
                s_, sb_, sbm = rt[:, 0], rt[:, 1], rt[:, 2]
                link(V_.tensor_tensor(sb_, s_, rbias[:, :].unsqueeze(1).to_broadcast([P, NB, E]), ALU.add))
                q4 = sb_.rearrange("p b (g j) -> p (b g) j", j=4)
                pair = rt[:, 3:5].rearrange("p a b e -> p (a b e)")[:, 0:72].rearrange("p (q j) -> p q j", j=6)
                V_.tensor_tensor(pair[:, :, 0:3], q4[:, :, 0:3], q4[:, :, 1:4], ALU.add)
                V_.tensor_tensor(pair[:, :, 3:5], q4[:, :, 0:2], q4[:, :, 2:4], ALU.add)
                link(V_.tensor_tensor(pair[:, :, 5:6], q4[:, :, 0:1], q4[:, :, 3:4], ALU.add))
                gs = rt[:, 5, 0, 0:12]
                link(V_.tensor_reduce(gs, pair, AX.X, ALU.max))
                gsb = gs.rearrange("p (b g) -> p b g", b=NB)
                gm = rt[:, 5, 1, 0:3]
                link(V_.tensor_reduce(gm, gsb, AX.X, ALU.max))
                eq = rt[:, 6, 0, 0:12].rearrange("p (b g) -> p b g", b=NB)
                link(V_.tensor_tensor(eq, gsb, gm.unsqueeze(2).to_broadcast([P, NB, 4]), ALU.is_equal))
                link(V_.tensor_tensor(eq, eq, first[:, 16:20].unsqueeze(1).to_broadcast([P, NB, 4]), ALU.mult))
                link(V_.tensor_reduce(gm, eq, AX.X, ALU.max))
                link(V_.tensor_tensor(eq, eq, gm.unsqueeze(2).to_broadcast([P, NB, 4]), ALU.is_equal))
                emask = eq.unsqueeze(3).to_broadcast([P, NB, 4, 4])
                sbm4 = sbm.rearrange("p b (g j) -> p b g j", j=4)
                sb4 = sb_.rearrange("p b (g j) -> p b g j", j=4)
                link(V_.tensor_scalar(rt[:, 7, 0, 0:12], rt[:, 6, 0, 0:12], -NEG, NEG, ALU.mult, ALU.add))
                off = rt[:, 7, 0, 0:12].rearrange("p (b g) -> p b g", b=NB).unsqueeze(3).to_broadcast([P, NB, 4, 4])
                link(V_.tensor_tensor(sbm4, sb4, emask, ALU.mult))
                link(V_.tensor_tensor(sbm4, sbm4, off, ALU.add))
                m = rt[:, 5, 2, 0:3]
                picks = []
                for r in range(2):
                    a = rt[:, 8 + r]
                    link(V_.tensor_reduce(m, sbm, AX.X, ALU.max))
                    link(V_.tensor_tensor(a, sbm, m.unsqueeze(2).to_broadcast([P, NB, E]), ALU.is_equal))
                    link(V_.tensor_tensor(a, a, first[:, 0:16].unsqueeze(1).to_broadcast([P, NB, E]), ALU.mult))
                    link(V_.tensor_reduce(m, a, AX.X, ALU.max))
                    link(V_.tensor_tensor(a, a, m.unsqueeze(2).to_broadcast([P, NB, E]), ALU.is_equal))
                    if r == 0:
                        link(V_.scalar_tensor_tensor(out=sbm, in0=a, scalar=4 * NEG, in1=sbm, op0=ALU.mult,
                                                     op1=ALU.add))
                    picks.append(a)
                V_.tensor_copy(vals[:, :, :, 2], picks[1])
                V_.tensor_copy(vals[:, :, :, 1], token[:, :].unsqueeze(2).to_broadcast([P, NB, E]))
                link(V_.tensor_tensor(vals[:, :, :, 0], picks[0], picks[1], ALU.add))
                V_.tensor_copy(gates[:, :, :], vals[:, :, :, 0]).then_inc(gates_ready, 1)
                link(V_.tensor_tensor(picks[0], vals[:, :, :, 0], s_, ALU.mult))
                link(V_.tensor_reduce(m, picks[0], AX.X, ALU.add))
                link(V_.reciprocal(m, m))
                link(V_.tensor_tensor(vals[:, :, :, 3], picks[0], m.unsqueeze(2).to_broadcast([P, NB, E]), ALU.mult))

            def numbers(src, dst_f, dst):
                link(V_.tensor_scalar(dst_f[:, 1], src[:, :, 0], -BIG, BIG, ALU.mult, ALU.add))
                link(V_.tensor_tensor(dst_f[:, 0], src[:, :, 1], dst_f[:, 1], ALU.add))
                link(V_.scalar_tensor_tensor(out=dst_f[:, 1], in0=src[:, :, 2], scalar=float(NT), in1=dst_f[:, 0],
                                             op0=ALU.mult, op1=ALU.add))
                return V_.tensor_copy(dst, dst_f)

            def index(L):
                key = ("rank", L)
                wait_bank_full(dve, key)
                V_.tensor_copy(load[:, :], job_bank(key)[:, 48:64])
                free(V_.tensor_copy(rt[:, 10], job_bank(key)[:, 0:48].rearrange("p (b e) -> p b e", b=NB)))
                dve.wait_ge(freed_v, jobs[key][2])
                link(V_.tensor_scalar(rt[:, 11], vals[:, :, :, 0], -BIG, BIG, ALU.mult, ALU.add))
                link(V_.tensor_tensor(slot_of[:, :, :], rt[:, 10], rt[:, 11], ALU.add))

                def members(g):
                    V_.tensor_tensor(member[:, g % 2],
                                     iota[:, 0:SLOTS].unsqueeze(1).unsqueeze(1).to_broadcast([P, NB, 4, SLOTS]),
                                     slot_of[:, :, 4 * g:4 * g + 4].unsqueeze(3).to_broadcast([P, NB, 4, SLOTS]),
                                     ALU.is_equal).then_inc(member_ready, 1)

                def slots(g):
                    key = ("idx", L, g)
                    wait_bank_full(dve, key)
                    e = slice(4 * g, 4 * g + 4)
                    free(V_.tensor_copy(slotted[:, e, :], job_bank(key)[:, 0:16].rearrange("p (e v) -> p e v", e=4)))
                    dve.wait_ge(freed_v, jobs[key][2])
                    numbers(slotted[:, e, :], idx_f[:, :, e], idx[:, :, e]).then_inc(idx_ready, 1)

                dve.wait_ge(work_free, L + 1)
                members(0)
                members(1)
                for g in range(4):
                    slots(g)
                    if g < 2:
                        members(g + 2)
                link(V_.tensor_reduce(load[0:1, 0:1], load[0:1, :], AX.X, ALU.max))
                link(V_.tensor_scalar(over_f[0:1, L:L + 1], load[0:1, 0:1], SLOTS + 0.5, None, ALU.is_gt))
                link(V_.scalar_tensor_tensor(out=over_f[0:1, DEPTH + L + 1:DEPTH + L + 2], in0=over_f[0:1, L:L + 1],
                                             scalar=float(STEPS), in1=over_f[0:1, DEPTH + L:DEPTH + L + 1],
                                             op0=ALU.mult, op1=ALU.add))
                V_.tensor_copy(over[:, :], over_f[:, :]).then_inc(over_ready, 1)

            for L in range(DEPTH):
                kind = KINDS[L]
                norm_scale(2 * L)
                mod_columns(L, 0)
                if L > 0:
                    mod_columns(L, 1)
                spread_gates(L, 0)
                if L > 0:
                    spread_gates(L, 1)
                norm_out(2 * L, 0)
                if kind < 2:
                    evacuate(*[("qkv", L, u, b) for u in range(6) for b in range(NB)])
                    qk_heads = [qkv[:, b, :].rearrange("p (h d) -> p h d", d=DH) for b in range(NB)]
                    if kind == 1:
                        for b in range(NB):
                            dve.wait_ge(head_sq, b + 1)
                            V_.tensor_reduce(small[:, 8:32], squares[:, 0:1536].rearrange("p (h d) -> p h d", d=DH),
                                             AX.X, ALU.add).then_inc(head_ms, 1)
                            dve.wait_ge(head_rstd, b + 1)
                            hv = qk_heads[b]
                            link(V_.tensor_tensor(hv, hv, small[:, 32:56].unsqueeze(2).to_broadcast([P, 24, DH]),
                                                  ALU.mult))
                            V_.tensor_tensor(hv[:, 0:H], hv[:, 0:H],
                                             gains[:, 0, :].unsqueeze(1).to_broadcast([P, H, DH]), ALU.mult)
                            V_.tensor_tensor(hv[:, H:24], hv[:, H:24],
                                             gains[:, 1, :].unsqueeze(1).to_broadcast([P, 8, DH]),
                                             ALU.mult).then_inc(qk_ready, 1)
                        dve.wait_ge(qk_ready, 3)
                    else:
                        wait_evacuated(dve, *[("qkv", L, u, 1) for u in range(5)])
                    rope(dve, V_, qk_heads[1], rope64[:, 0], 32, xn[:, :, :].rearrange("p b n -> p (b n)"), link,
                         roped_v)
                else:
                    evacuate(*[("lat", L, u, b) for u in range(4) for b in range(NB)])
                    wait_evacuated(dve, *[("lat", L, u, b) for u in range(4) for b in range(NB)])
                    dve.wait_ge(lat_rstd, 1)
                    dve.wait_ge(cache_in, 16 * (3 * 2 + 2))
                    for b in range(NB):
                        V_.tensor_scalar(ql[:, b, :], ql[:, b, :], small[:, 14 + b:15 + b], None, ALU.mult)
                        V_.scalar_tensor_tensor(out=ckv[:, b, 0:256], in0=ckv[:, b, 0:256],
                                                scalar=small[:, 17 + b:18 + b], in1=kvg[:, :], op0=ALU.mult,
                                                op1=ALU.mult)
                        last = V_.tensor_copy(kpe[:, b, 64:96], ckv[:, b, 256:288])
                    link(last)
                    for b in (1, 2):
                        rope(dve, V_, kpe[:, b:b + 1, 64:96], rope32[:, b - 1], 16, squares[:, 1024 + 64 * b:],
                             link, roped_v)
                    for c in range(3):
                        key = ("qlT", L, c)
                        wait_bank_full(dve, key)
                        free(V_.tensor_scalar(qlT[:, c, :], job_bank(key)[:, 0:NT], gT[:, 64 + c:65 + c], None,
                                              ALU.mult))
                    key = ("kpeT", L)
                    wait_bank_full(dve, key)
                    for j in range(4):
                        last = V_.tensor_copy(kT[64:96, j, :], job_bank(key)[64:96, :])
                    free(last)
                    evacuate(*[("uq", L, u, b) for u in range(3) for b in range(NB)])
                    wait_evacuated(dve, *[("uq", L, u, b) for u in range(3) for b in range(NB)])
                    for b in (1, 2):
                        dve.wait_ge(roped_v, 3 + b)
                        rope(dve, V_, qkv[:, b, :].rearrange("p (h d) -> p h d", d=DQK)[:, :, 64:96],
                             rope32[:, b - 1], 16, squares, link, roped_v)
                    evacuate(*[("V", L, u, kb) for u in range(2) for kb in range(4)])
                qscale = (DH if kind < 2 else DQK) ** -0.5

                def turn(h):
                    n = L * H + h
                    dve.wait_ge(pt_full, 2 * n + 2)
                    V_.tensor_copy(pp[:, 1, h % 2, 512:896], bank[5][:, 0:384]).then_inc(pt_v, 1)

                def finish_pair(j):
                    n = L * 8 + j
                    dve.wait_ge(probs, L * H + 2 * j + 2)
                    d_, r_ = den[:, 2 * j:2 * j + 2, :], rden[:, 2 * j:2 * j + 2, :]
                    if kind == 0:
                        link(V_.tensor_tensor(d_, d_, esink[:, 2 * j:2 * j + 2, :], ALU.add))
                    link(V_.reciprocal(r_, d_))
                    dve.wait_ge(o_full, n + 1)
                    src = bank[6 + j % 2][:, 0:384].rearrange("p (b h d) -> p b h d", b=NB, h=2)
                    for b in range(NB):
                        o = xn[:, b, 2 * j * DH:(2 * j + 2) * DH].rearrange("p (h d) -> p h d", h=2)
                        last = V_.tensor_tensor(o, src[:, b], r_[:, :, b:b + 1].to_broadcast([P, 2, DH]), ALU.mult)
                    last.then_inc(o_ready, 1)

                for heads in CHUNKS[L]:
                    keys = ([("qT", L, p) for p in range(8)] + [("kT", L, g) for g in range(G)] if kind < 2 else
                            [("kT", L, h) for h in heads] + [("qT", L, h) for h in heads])
                    for key in keys:
                        if not mine(key, "v"):
                            continue
                        if key[0] == "kT":
                            evacuate(key)
                            continue
                        wait_bank_full(dve, key)
                        rws = P if kind < 2 else DQK
                        free(V_.tensor_scalar(qT[0:rws, key[2] % 8, :], job_bank(key)[0:rws, 0:NT], qscale, None,
                                              ALU.mult))
                    for h in heads:
                        n = L * H + h
                        for b, i, c0, w in PARTS:
                            if b != 0:
                                wait_bank_full(dve, ("S", L, h, i))
                            last = V_.tensor_reduce(neg_max[:, h, b:b + 1], job_bank(("S", L, h, i))[:, c0:c0 + w],
                                                    AX.X, ALU.max, negate=True)
                        if kind == 0:
                            link(last)
                            last = V_.tensor_scalar(neg_max[:, h, :], neg_max[:, h, :], sink[:, SW[L], 1, h:h + 1],
                                                    None, ALU.min)
                        last.then_inc(max_ready, 1)
                        if h > heads[0]:
                            turn(h - 1)
                        if h >= heads[0] + 3 and h % 2 == 1:
                            finish_pair((h - 3) // 2)
                    turn(heads[-1])
                    finish_pair(heads[-1] // 2)
                evacuate(*[("oT", L, k) for k in range(KC)])
                for u in range(4):
                    for b in range(NB):
                        g = 12 * L + 3 * u + b
                        key = ("wo", L, u, b)
                        wait_bank_full(dve, key)
                        if last_reader_of(key):
                            pass_on(dve, last_reader_of(key))
                        if 3 * u + b >= 4:
                            dve.wait_ge(x_mixed, g - 3)
                        V_.tensor_tensor(wo_tmp[:, g % 4, :], job_bank(key)[:, 0:UC],
                                         gbc[:, 0, COND[b], u * UC:(u + 1) * UC], ALU.mult).then_inc(wo_mul, 1)
                if L == 0:
                    mod_columns(0, 1)
                    spread_gates(0, 1)
                norm_scale(2 * L + 1)
                norm_out(2 * L + 1, 1)
                wait_evacuated(dve, ("router", L))
                evacuate(*[("hrow", L, b, half) for b in range(NB) for half in range(2)])
                route(L)
                index(L)

                def turned_rows(n, slot):
                    dve.wait_ge(xT_full, n + 1)
                    V_.tensor_copy(xT[:, slot, 4:8, :], bank[7][:, :].rearrange("p (k n) -> p k n", k=4))\
                      .then_inc(xT_v, 1)

                def pair(i, last):
                    for e in range(2):
                        n = i * 2 + (E * L + e)
                        dve.wait_ge(sil_full, n + 1)
                        V_.tensor_tensor(act_sb[:, e, :], bank[e][:, DE:2 * DE], sil[:, e, :],
                                         ALU.mult).then_inc(act_full, 1)
                        if not (last and e == 1):
                            turned_rows(n + 1, 1 - e)
                        dve.wait_ge(y_full, n + 1)
                        pass_on(dve, ("exp", L, 4 * e + 2))
                        dve.wait_ge(ys_free, n + 1)
                        at = slotted[:, bass.ds(i * 2 + e, 1), 3] if type(i) is not int else slotted[:, 2 * i + e, 3:4]
                        V_.tensor_scalar(ys[:, e, 512:1024], bank[5][:, :], at, None, ALU.mult).then_inc(y_v, 1)

                turned_rows(E * L, 0)
                each_pair(dve, pair)

                def step(n, q, e):
                    dve.wait_ge(ov_done, n + 1)
                    for b in range(NB):
                        V_.tensor_scalar(ov_member[:, b, :], iota[:, bass.ds(q * SLOTS + SLOTS, SLOTS)],
                                         slot_of[:, b, bass.ds(e, 1)], None, ALU.is_equal)
                    V_.tensor_copy(ov_vals[:, :, :], vals[:, :, bass.ds(e, 1), :].rearrange("p b e v -> p b (e v)"))\
                      .then_inc(ov_member_ready, 1)
                    dve.wait_ge(ov_idx_full, n + 1)
                    V_.tensor_copy(ov_slotted[:, :], bank[3][:, 0:4]).then_inc(ov_chain, 1)
                    dve.wait_ge(ov_chain, n * 4 + 1)
                    V_.tensor_scalar(idx_f[:, 1, 0:1], ov_slotted[:, 0:1], -BIG, BIG, ALU.mult,
                                     ALU.add).then_inc(ov_chain, 1)
                    dve.wait_ge(ov_chain, n * 4 + 2)
                    V_.tensor_tensor(idx_f[:, 0, 0:1], ov_slotted[:, 1:2], idx_f[:, 1, 0:1], ALU.add)\
                      .then_inc(ov_chain, 1)
                    dve.wait_ge(ov_chain, n * 4 + 3)
                    V_.scalar_tensor_tensor(out=idx_f[:, 1, 0:1], in0=ov_slotted[:, 2:3], scalar=float(NT),
                                            in1=idx_f[:, 0, 0:1], op0=ALU.mult, op1=ALU.add).then_inc(ov_chain, 1)
                    dve.wait_ge(ov_chain, n * 4 + 4)
                    V_.tensor_copy(ov_idx[:, :], idx_f[:, :, 0]).then_inc(ov_idx_ready, 1)
                    dve.wait_ge(ov_xT_full, n + 1)
                    for half in range(2):
                        last = V_.tensor_copy(xT[:, 0, 4 * half:4 * half + 4, :],
                                              bank[6 + half][:, :].rearrange("p (k n) -> p k n", k=4))
                    last.then_inc(ov_xT_ready, 1)
                    dve.wait_ge(ov_sil, n + 1)
                    V_.tensor_tensor(act_sb[:, 0, :], bank[0][:, DE:2 * DE], sil[:, 0, :], ALU.mult)\
                      .then_inc(ov_act, 1)
                    dve.wait_ge(ov_y_full, n + 2)
                    for half in range(2):
                        last = V_.tensor_scalar(ys[:, 0, half * 512:(half + 1) * 512], bank[4 + half][:, :],
                                                ov_slotted[:, 3:4], None, ALU.mult)
                    last.then_inc(ov_y, 1)

                further_passes(dve, L, step)
                dve.wait_ge(y_in, 32 * (L + 1))
                for b in range(NB):
                    link(V_.tensor_tensor(y_sum[:, b, :], y_sum[:, b, :], y_second[:, b, :], ALU.add))
                    V_.tensor_tensor(y_sum[:, b, :], y_sum[:, b, :], gbc[:, 1, COND[b], :],
                                     ALU.mult).then_inc(moe_mul, 1)
                    dve.wait_ge(moe_mul, 3 * L + b + 1)
                    V_.tensor_tensor(x[:, b, 0:640], x[:, b, 0:640], y_sum[:, b, 0:640],
                                     ALU.add).then_inc(x_moe_v, 1)
            norm_scale(2 * DEPTH)
            dve.wait_ge(x_in, 48)
            dve.wait_ge(xn_ready, 3 * (2 * DEPTH + 1))
            for b in range(NB):
                last = V_.tensor_tensor(xn[:, b, :], xn[:, b, :], gbc[:, 0, 0, :], ALU.mult)
            last.then_inc(xn_ready, 1)

        @block.tensor
        def _(pe):
            def done(ins):
                ins.then_inc(bank_full, 1)

            def wait_unit(key, i=None):
                slot, before = ring_place[key]
                pe.wait_ge(slot_full[slot], 16 * (before + 1) if i is None else i * 16 + 16 * (before + 1))

            def mm(out, lhsT, rhs, start, stop):
                return pe.matmul(out, lhsT, rhs, start=start, stop=stop)

            def mod_unit(key, base, m, i=None):
                wait_unit(key, i)
                pe.wait_ge(rows_done, base + m + 1)
                w = unit(key).rearrange("p (k n) -> p k n", k=KC)
                for k in range(KC):
                    g = k % 4 * 32
                    ins = pe.matmul(bank[3][g:g + 32, 0:UC], condT[:, k, :], w[:, k, :], start=k < 4, stop=k >= 4)
                ins.then_inc(mod_full, 1)

            def project(key, ukey, lhs, kcs, n):
                wait_bank_free(pe, key)
                w = unit(ukey)[:, 0:kcs * n].rearrange("p (k n) -> p k n", k=kcs)
                for k in range(kcs):
                    ins = mm(job_bank(key)[:, 0:n], lhs[:, k, key[3] * P:(key[3] + 1) * P], w[:, k, :],
                             k == 0, k == kcs - 1)
                done(ins)

            pe.wait_ge(cond_in, 16 * 8)
            pe.wait_ge(raw_silu, 1)
            done(pe.transpose(job_bank("cond")[:, 0:16], raw[0:16, 0:P], ident[0:16, 0:16]))
            done(pe.transpose(job_bank("gains")[:, 0:67], raw[0:67, P:2 * P], ident[0:67, 0:67]))
            for c in range(2):
                done(pe.transpose(job_bank(("bias", c))[:, 0:96], raw[0:96, (2 + c) * P:(3 + c) * P],
                                  ident[0:96, 0:96]))
            wait_evacuated(pe, "cond", "gains", ("bias", 1))
            for m in range(12):
                mod_unit(("mod0", m), 0, m)
            pe.wait_ge(const_in, 16 * 15)

            def mod_columns(L, s):
                key = ("modc", L, s)
                wait_bank_free(pe, key)
                for v in range(2):
                    for k in range(KC):
                        c = (v * KC + k) * 2
                        at = (3 * s + v) * D + k * P
                        ins = mm(job_bank(key)[:, c:c + 2], rows[:, at:at + P], sel[:, 2 * P:2 * P + 2], True, True)
                done(ins)

            def spread_gates(L, g):
                for j in range(4 * g, 4 * g + 4):
                    key = ("gate", L, j)
                    wait_bank_free(pe, key)
                    c, c0 = j // 2 % 2, (2, 5)[g] * D + j % 2 * 512
                    done(mm(job_bank(key)[:, :], sel[:, c * P:(c + 1) * P], rows[:, c0:c0 + 512], True, True))

            def norm_turn(n):
                pe.wait_ge(xn_ready, 3 * n + 3)
                for k in range(KC):
                    key = ("norm", n, k)
                    wait_bank_free(pe, key)
                    for b in range(NB):
                        ins = pe.transpose(job_bank(key)[:, b * P:(b + 1) * P], xn[:, b, k * P:(k + 1) * P],
                                           ident[:, :])
                    done(ins)
                wait_evacuated(pe, *[("norm", n, k) for k in range(KC)])

            for L in range(DEPTH):
                kind = KINDS[L]
                pe.wait_ge(rows_done, 24 * L + (13 if L == 0 else 25))
                mod_columns(L, 0)
                if L > 0:
                    mod_columns(L, 1)
                spread_gates(L, 0)
                if L > 0:
                    spread_gates(L, 1)
                norm_turn(2 * L)
                if kind < 2:
                    for u in range(6):
                        wait_unit(("qkv", L, u))
                        for b in range(NB):
                            project(("qkv", L, u, b), ("qkv", L, u), hT, KC, UC)
                else:
                    for u, (name, w, n) in enumerate(LAT):
                        wait_unit((name, L, w))
                        for b in range(NB):
                            project(("lat", L, u, b), (name, L, w), hT, KC, n)
                    pe.wait_ge(roped_v, 4)
                    pe.wait_ge(cache_in, 16 * 8)
                    for c in range(3):
                        key = ("qlT", L, c)
                        wait_bank_free(pe, key)
                        for b in range(NB):
                            ins = pe.transpose(job_bank(key)[:, b * P:(b + 1) * P], ql[:, b, c * P:(c + 1) * P],
                                               ident[:, :])
                        done(ins)
                    for c in range(2):
                        key = ("ckvT", L, c)
                        wait_bank_free(pe, key)
                        for b in range(4):
                            ins = pe.transpose(job_bank(key)[:, b * P:(b + 1) * P], ckv[:, b, c * P:(c + 1) * P],
                                               ident[:, :])
                        done(ins)
                    key = ("kpeT", L)
                    wait_bank_free(pe, key)
                    for b in range(4):
                        ins = pe.transpose(job_bank(key)[0:DQK, b * P:(b + 1) * P], kpe[:, b, :], ident[:, :])
                    done(ins)
                    wait_evacuated(pe, *[("qlT", L, c) for c in range(3)], *[("ckvT", L, c) for c in range(2)],
                                   ("kpeT", L))
                    for u in range(3):
                        wait_unit(("uq", L, u))
                        for b in range(NB):
                            project(("uq", L, u, b), ("uq", L, u), qlT, 3, 512)
                    for u in range(2):
                        wait_unit(("ukv", L, u))
                        w = unit(("ukv", L, u)).rearrange("p (c h n) -> p c h n", c=2, h=8)
                        for kb in range(4):
                            key = ("V", L, u, kb)
                            wait_bank_free(pe, key)
                            for c in range(2):
                                ins = mm(job_bank(key)[:, :].rearrange("p (h d) -> p h d", h=8),
                                         ckvT[:, c, kb * P:(kb + 1) * P], w[:, c, :, 64:128], c == 0, c == 1)
                            done(ins)

                def scores(h):
                    if kind < 2:
                        r0, r1, q, kk = (h % 2) * 64, (h % 2) * 64 + 64, h // 2, h // 4
                    else:
                        r0, r1, q, kk = 0, DQK, h % 8, h % 4
                    for i in range(2):
                        key = ("S", L, h, i)
                        wait_bank_free(pe, key)
                        b = 1 + i
                        ins = mm(job_bank(key)[:, 0:384], qT[r0:r1, q, b * P:(b + 1) * P], kT[r0:r1, kk, P:4 * P],
                                 True, kind != 0)
                        if kind == 0:
                            ins = mm(job_bank(key)[:, P * (1 - i):P * (2 - i)], ident[:, :], masks[:, i, :],
                                     False, True)
                        if i == 0:
                            ins = mm(job_bank(key)[:, 384:512], qT[r0:r1, q, 0:P], kT[r0:r1, kk, 0:P], True, True)
                        done(ins)

                def turn(h):
                    n = L * H + h
                    pe.wait_ge(probs, n + 1)
                    for i in range(2):
                        if n > 0:
                            pe.wait_ge((pt_a, pt_v)[i], n)
                        for t in range((4, 3)[i]):
                            ins = pe.transpose(bank[4 + i][:, t * P:(t + 1) * P],
                                               pp[:, 0, h % 2, 512 * i + t * P:512 * i + (t + 1) * P], ident[:, :])
                        ins.then_inc(pt_full, 1)

                def weigh(h):
                    n = L * H + h
                    j = L * 8 + h // 2
                    pe.wait_ge(pt_a, n + 1)
                    pe.wait_ge(pt_v, n + 1)
                    if h % 2 == 0 and j >= 2:
                        pe.wait_ge(o_ready, j - 1)
                    vc = (h // 4 if kind < 2 else h) * DH
                    for b, off, kbs in ((0, 384, (0,)), (1, 0, (1, 2, 3)), (2, 512, (1, 2, 3))):
                        out = bank[6 + h // 2 % 2][:, (2 * b + h % 2) * DH:(2 * b + h % 2 + 1) * DH]
                        for t, kb in enumerate(kbs):
                            ins = mm(out, pp[:, 1, h % 2, off + t * P:off + (t + 1) * P], V[:, kb, vc:vc + DH],
                                     t == 0, t == len(kbs) - 1)
                    if h % 2 == 1:
                        ins.then_inc(o_full, 1)

                if kind < 2:
                    if kind == 1:
                        pe.wait_ge(qk_ready, 3)
                    pe.wait_ge(roped_v, (1, 2, 0, 7)[L])
                    pe.wait_ge(roped_p, (1, 2, 0, 3)[L])
                    pe.wait_ge(cache_in, 16 * (3, 6, 0, 11)[L])
                    wait_evacuated(pe, *[("qkv", L, u, b) for u in range(6) for b in range(NB)])
                    for p in range(8):
                        key = ("qT", L, p)
                        wait_bank_free(pe, key)
                        for b in range(NB):
                            ins = pe.transpose(job_bank(key)[:, b * P:(b + 1) * P], qkv[:, b, p * P:(p + 1) * P],
                                               ident[:, :])
                        done(ins)
                    for g in range(G):
                        key = ("kT", L, g)
                        wait_bank_free(pe, key)
                        for b in range(4):
                            src = (qkv[:, b, 1024 + g * P:1024 + (g + 1) * P] if b < 3 else
                                   kc[:, g, :, :].rearrange("p t d -> p (t d)"))
                            ins = pe.transpose(job_bank(key)[:, b * P:(b + 1) * P], src, ident[:, :])
                        done(ins)
                for heads in CHUNKS[L]:
                    if kind == 2:
                        for h in heads:
                            key = ("kT", L, h)
                            wait_bank_free(pe, key)
                            w = unit(("ukv", L, h // 8)).rearrange("p (c h n) -> p c h n", c=2, h=8)
                            for c in range(2):
                                ins = mm(job_bank(key)[0:64, :], w[:, c, h % 8, 0:64], ckvT[:, c, :], c == 0, c == 1)
                            done(ins)
                        if heads[0] == 0:
                            pe.wait_ge(roped_v, 6)
                            wait_evacuated(pe, *[("uq", L, 2, b) for b in range(NB)],
                                           *[("V", L, 1, kb) for kb in range(4)])
                        for h in heads:
                            key = ("qT", L, h)
                            wait_bank_free(pe, key)
                            for b in range(NB):
                                ins = pe.transpose(job_bank(key)[0:DQK, b * P:(b + 1) * P],
                                                   qkv[:, b, h * DQK:(h + 1) * DQK], ident[:, :])
                            done(ins)
                        wait_evacuated(pe, *[(w, L, h) for h in heads for w in ("qT", "kT")])
                    else:
                        wait_evacuated(pe, *[("qT", L, p) for p in range(8)], *[("kT", L, g) for g in range(G)])
                    hs = list(heads)
                    for t in range(len(hs) + 2):
                        if t < len(hs):
                            scores(hs[t])
                        if 1 <= t <= len(hs):
                            turn(hs[t - 1])
                        if t >= 2:
                            weigh(hs[t - 2])
                pe.wait_ge(o_ready, 8 * (L + 1))
                for k in range(KC):
                    key = ("oT", L, k)
                    wait_bank_free(pe, key)
                    for b in range(NB):
                        ins = pe.transpose(job_bank(key)[:, b * P:(b + 1) * P], xn[:, b, k * P:(k + 1) * P],
                                           ident[:, :])
                    done(ins)
                wait_evacuated(pe, *[("oT", L, k) for k in range(KC)])
                for u in range(4):
                    wait_unit(("wo", L, u))
                    for b in range(NB):
                        project(("wo", L, u, b), ("wo", L, u), hT, KC, UC)
                if L == 0:
                    pe.wait_ge(wo_mul, 12)
                    for m in range(12, 24):
                        mod_unit(("mod0", m), 0, m)
                    pe.wait_ge(rows_done, 25)
                    mod_columns(0, 1)
                    spread_gates(0, 1)
                norm_turn(2 * L + 1)
                key = ("router", L)
                wait_bank_free(pe, key)
                for b in range(NB):
                    for k in range(KC):
                        ins = mm(job_bank(key)[:, b * E:(b + 1) * E], hT[:, k, b * P:(b + 1) * P], wr[:, k, :],
                                 k == 0, k == KC - 1)
                done(ins)
                for b in range(NB):
                    for half in range(2):
                        key = ("hrow", L, b, half)
                        wait_bank_free(pe, key)
                        for k in range(4):
                            ins = pe.transpose(job_bank(key)[:, k * P:(k + 1) * P],
                                               hT[:, 4 * half + k, b * P:(b + 1) * P], ident[:, :])
                        done(ins)
                wait_evacuated(pe, *[("hrow", L, b, half) for b in range(NB) for half in range(2)])
                pe.wait_ge(gates_ready, L + 1)
                key = ("rank", L)
                wait_bank_free(pe, key)
                for b in range(NB):
                    for c in range(b + 1):
                        mm(job_bank(key)[:, b * E:(b + 1) * E], before[:, :] if c == b else ones[:, :],
                           gates[:, c, :], c == 0, c == b)
                for c in range(NB):
                    ins = mm(job_bank(key)[:, 48:64], ones[:, :], gates[:, c, :], c == 0, c == NB - 1)
                done(ins)
                for g in range(4):
                    key = ("idx", L, g)
                    wait_bank_free(pe, key)
                    pe.wait_ge(member_ready, 4 * L + g + 1)
                    for e in range(4):
                        for b in range(NB):
                            ins = mm(job_bank(key)[:, 4 * e:4 * e + 4], member[:, g % 2, b, e, :],
                                     vals[:, b, 4 * g + e, :], b == 0, b == NB - 1)
                    done(ins)
                pe.wait_ge(idx_ready, 4 * (L + 1))
                for m in range(MODA if L < DEPTH - 1 else 0):
                    mod_unit(("modA", L, m), 24 * (L + 1), m)

                def turn_rows(n, slot, gathered):
                    pe.wait_ge(g_in[slot], gathered)
                    pe.wait_ge(xT_a, n + 1)
                    pe.wait_ge(xT_v, n + 1)
                    for k in range(KC):
                        ins = pe.transpose(bank[6 + k // 4][:, k % 4 * P:(k % 4 + 1) * P],
                                           xg[:, slot, k * P:(k + 1) * P], ident[:, :])
                    ins.then_inc(xT_full, 1)

                def gate_up(x_t, out, w):
                    for c in range(2):
                        for k in range(KC):
                            ins = mm(out[:, c * DE:(c + 1) * DE], x_t[:, k, :], w[c][:, k, :], k == 0, k == KC - 1)
                    return ins

                def turn_gated(src):
                    for c in range(2):
                        ins = pe.transpose(bank[2][:, c * P:(c + 1) * P], src[:, c * P:(c + 1) * P], ident[:, :])
                    return ins

                def down(a_t, w):
                    for half in range(2):
                        for c in range(2):
                            ins = mm(bank[4 + half][:, :], a_t[:, c, :], w[:, c, half * 512:(half + 1) * 512],
                                     c == 0, c == 1)
                    return ins

                def pair(i, last):
                    for e in range(2):
                        n = i * 2 + (E * L + e)
                        at = None if i is None else i
                        w = []
                        for c in range(3):
                            key = ("exp", L, 4 * e + c)
                            w.append(unit(key).rearrange("p (k n) -> p k n", k=(KC, KC, 2)[c]))
                            if c < 2:
                                wait_unit(key, at)
                        pe.wait_ge(xT_a, n + 2)
                        pe.wait_ge(xT_v, n + 2)
                        pe.wait_ge(act_full, n + 1)
                        gate_up(xT[:, e], bank[e], w).then_inc(au_full, 1)
                        if L < DEPTH - 1:
                            mod_unit(("exp", L, 4 * e + 3), 24 * (L + 1), i * 2 + (MODA + e), at)
                        pe.wait_ge(act_full, n + 3)
                        pe.wait_ge(acT_ready, n + 1)
                        turn_gated(act_sb[:, e, :]).then_inc(acT_full, 1)
                        if not (last and e == 1):
                            turn_rows(n + 1, 1 - e, (i + e) * 16 + 16 * (E // 2 * L + 1))
                        wait_unit(("exp", L, 4 * e + 2), at)
                        pe.wait_ge(acT_ready, n + 2)
                        pe.wait_ge(y_a, n + 1)
                        pe.wait_ge(y_v, n + 1)
                        down(actT[:, e], w[2]).then_inc(y_full, 1)

                turn_rows(E * L, 0, 16 * (E // 2 * L + 1))
                each_pair(pe, pair)
                for m in range(MODB if L < DEPTH - 1 else 0):
                    mod_unit(("modB", L, m), 24 * (L + 1), MODA + E + m)
                pe.wait_ge(y_a, E * (L + 1) + 1)
                pe.wait_ge(y_v, E * (L + 1) + 1)
                pe.wait_ge(rows_done, 24 * min(L + 2, DEPTH) + 1)

                def step(n, q, e):
                    pe.wait_ge(ov_member_ready, n + 1)
                    for b in range(NB):
                        ins = mm(bank[3][:, 0:4], ov_member[:, b, :], ov_vals[:, b, :], b == 0, b == NB - 1)
                    ins.then_inc(ov_idx_full, 1)
                    pe.wait_ge(ov_g_in, (n + 1) * 16)
                    for k in range(KC):
                        ins = pe.transpose(bank[6 + k // 4][:, k % 4 * P:(k % 4 + 1) * P],
                                           xg[:, 0, k * P:(k + 1) * P], ident[:, :])
                    ins.then_inc(ov_xT_full, 1)
                    pe.wait_ge(ov_xT_ready, n + 1)
                    pe.wait_ge(ov_w_in, (n + 1) * 48)
                    gate_up(xT[:, 0], bank[0], ov_w).then_inc(ov_au_full, 1)
                    pe.wait_ge(ov_act, n + 1)
                    turn_gated(act_sb[:, 0, :]).then_inc(ov_acT_full, 1)
                    pe.wait_ge(ov_acT_ready, n + 1)
                    down(actT[:, 0], ov_w[2]).then_inc(ov_y_full, 1)

                further_passes(pe, L, step)


def launch_io():
    ins = ["x_prompt", "x_sample", "cache_swa_k", "cache_swa_v", "cache_qkn_k", "cache_qkn_v", "cache_mla_ckv",
           "cache_mla_kpe", "c", "c_ctx", "w_mod", "b_mod", "norm_mix", "norm_ffn", "swa_wqkv", "swa_wo", "swa_sink",
           "qkn_wqkv", "qkn_wo", "qkn_qnorm", "qkn_knorm", "mla_wdq", "mla_qnorm", "mla_wuq", "mla_wdkv",
           "mla_kvnorm", "mla_wukv", "mla_wo", "w_router", "router_bias", "moe_w_gate", "moe_w_up", "moe_w_down",
           "final_norm"]
    outs = {"y_prompt": (1, 128, 1024), "y_sample": (1, 256, 1024), "state_swa_k": (1, 2, 128, 4, 64),
            "state_swa_v": (1, 2, 128, 4, 64), "state_qkn_k": (1, 1, 128, 4, 64), "state_qkn_v": (1, 1, 128, 4, 64),
            "state_mla_ckv": (1, 1, 128, 256), "state_mla_kpe": (1, 1, 128, 32)}
    return ins, outs


def kernel(**inputs):
    import concourse.bacc as bacc
    from concourse.bass_utils import run_bass_kernel_spmd

    nc = bacc.Bacc("TRN2", target_bir_lowering=False, num_devices=1)
    names, outs = launch_io()
    arrays, A = {}, {}
    given = {n: np.ascontiguousarray(inputs[n]) for n in names}
    given.update(host_constants())
    for name, a in given.items():
        arrays[f"in_{name}"] = a
        A[name] = nc.dram_tensor(f"in_{name}", a.shape, mybir.dt.from_np(a.dtype), kind="ExternalInput").ap()
    for name, shape in outs.items():
        A[name] = nc.dram_tensor(f"out_{name}", shape, F32, kind="ExternalOutput").ap()
    build(nc, A)
    r = run_bass_kernel_spmd(nc, [arrays], core_ids=[0])
    return tuple(r.results[0][f"out_{name}"] for name in outs)
```

```python
from contextlib import ExitStack

import numpy as np

import concourse.bass as bass
from concourse import mybir

F32 = mybir.dt.float32
U32 = mybir.dt.uint32
ALU = mybir.AluOpType
ACT = mybir.ActivationFunctionType
AX = mybir.AxisListType

P = 128
D = 1024
KC = D // P
DEPTH = 4
KINDS = [0, 1, 2, 0]
STACK = [0, 0, 0, 1]
NB = 3
COND = [0, 1, 1]
NT = NB * P
H, G, DH = 16, 4, 64
E, DE = 16, 256
UC = 256
R = 8
PAIRS = E // 2
SLOTS = P
STEPS = (NT // SLOTS - 1) * E
VC = 704
MODA, MODB = 4, 4
BIG = 1e6
MLA_Q, MLA_KV, ROPE, DQK = 384, 256, 32, 96
EPS = 1e-6
NEG = -1e30


def host_constants():
    tokens = np.arange(256)
    row, col = (tokens // 64).astype(np.float32), (tokens % 64).astype(np.float32)

    def rope(d):
        quarter = d // 4
        inv = np.float32(10000.0) ** (-np.arange(quarter, dtype=np.float32) / np.float32(quarter))
        ang = np.concatenate([row[:, None] * inv, col[:, None] * inv], axis=-1).astype(np.float32)
        both = np.stack([np.cos(ang), np.sin(ang)], axis=1).astype(np.float32)
        return both.reshape(2, P, d).transpose(1, 0, 2)

    r, c = np.arange(P)[:, None], np.arange(P)[None, :]
    masks = np.stack([np.where(c <= r, 0.0, NEG), np.where(c >= r, 0.0, NEG)], axis=1)
    sel = np.zeros((P, 2 * P + 2), np.float32)
    for s in range(2):
        sel[s::32, s * P:(s + 1) * P] = 1.0
        sel[s::32, 2 * P + s] = 1.0
    first = np.tile(np.concatenate([np.arange(16, 0, -1), np.arange(4, 0, -1)])[None], (P, 1))
    out = dict(ident=np.eye(P), masks=masks.reshape(P, 2 * P), rope64=rope(64).reshape(P, 128),
               rope32=rope(32).reshape(P, 64), sel=sel, first=first,
               before=r < c, iota=np.tile(np.arange(NT)[None], (P, 1)), token=r + P * np.arange(NB)[None])
    return {k: np.ascontiguousarray(v, dtype=np.float32) for k, v in out.items()}


def mixer_units(L):
    if KINDS[L] < 2:
        return [("qkv", u) for u in range(6)] + [("wo", u) for u in range(4)]
    return ([("dq", 0), ("dq", 1), ("dkv", 0), ("dkv", 1)] + [("uq", u) for u in range(3)]
            + [("ukv", u) for u in range(2)] + [("wo", u) for u in range(4)])


def layer_units(L):
    units = []
    for name, u in mixer_units(L):
        if L == 0 and name == "wo":
            units += [("mod0", m) for m in range(8, 12)] if u == 0 else []
            units += [(name, L, u)] + [("mod0", m) for m in range(12 + 3 * u, 15 + 3 * u)]
        else:
            units.append((name, L, u))
    return units


def plan_ring():
    fills, at, place = [0] * R, 0, {}
    def once(key):
        nonlocal at
        place[key] = (at % R, fills[at % R])
        fills[at % R] += 1
        at += 1

    for m in range(8):
        once(("mod0", m))
    for L in range(DEPTH):
        for key in layer_units(L):
            once(key)
        for m in range(MODA if L < DEPTH - 1 else 0):
            once(("modA", L, m))
        for j in range(R):
            if j % 4 == 3 and L == DEPTH - 1:
                continue
            place[("exp", L, j)] = ((at + j) % R, fills[(at + j) % R])
            fills[(at + j) % R] += PAIRS
        for m in range(MODB if L < DEPTH - 1 else 0):
            once(("modB", L, m))
    return place


def plan_jobs():
    order = [("cond", "v"), ("gains", "v"), (("bias", 0), "v"), (("bias", 1), "v")]
    alt = "va"
    for L in range(DEPTH):
        order += [(("modc", L, s), "v") for s in ((0,) if L == 0 else (0, 1))]
        order += [(("gate", L, j), "v") for j in range(0 if L == 0 else 8)]
        order += [(("norm", 2 * L, k), alt[k % 2]) for k in range(KC)]
        if KINDS[L] < 2:
            order += [(("qkv", L, u, b), alt[(3 * u + b) % 2]) for u in range(6) for b in range(NB)]
            order += [(("qT", L, p), alt[p % 2]) for p in range(8)]
            order += [(("kT", L, g), alt[g % 2]) for g in range(G)]
            order += [(("S", L, h, i), "p") for h in range(H) for i in range(2)]
        else:
            order += [(("lat", L, u, b), alt[b % 2]) for u in range(4) for b in range(NB)]
            order += [(("qlT", L, c), "v") for c in range(3)] + [(("ckvT", L, c), "a") for c in range(2)]
            order += [(("kpeT", L), "v")]
            order += [(("uq", L, u, b), alt[b % 2]) for u in range(3) for b in range(NB)]
            order += [(("V", L, u, kb), alt[kb % 2]) for u in range(2) for kb in range(4)]
            for c in range(4):
                order += [(("kT", L, h), alt[h % 2]) for h in range(4 * c, 4 * c + 4)]
                order += [(("qT", L, h), alt[h % 2]) for h in range(4 * c, 4 * c + 4)]
                order += [(("S", L, h, i), "p") for h in range(4 * c, 4 * c + 4) for i in range(2)]
        order += [(("oT", L, k), alt[k % 2]) for k in range(KC)]
        order += [(("gate", L, j), "v") for j in range(4 if L == 0 else 0)]
        order += [(("wo", L, u, b), "w") for u in range(4) for b in range(NB)]
        if L == 0:
            order += [(("modc", L, 1), "v")] + [(("gate", L, j), "v") for j in range(4, 8)]
        order += [(("norm", 2 * L + 1, k), alt[k % 2]) for k in range(KC)]
        order += [(("router", L), "a")]
        order += [(("hrow", L, b, half), alt[half]) for b in range(NB) for half in range(2)]
        order += [(("rank", L), "v")] + [(("idx", L, g), "v") for g in range(4)]
    jobs, count = {}, {"v": 0, "a": 0, "p": 0, "w": 0}
    for n, (key, eng) in enumerate(order):
        count[eng] += 0 if eng == "p" and key[3] == 1 else 1
        jobs[key] = (n, eng, count[eng])
    by_index = [jobs[key] for key, _ in order]
    return jobs, by_index


def build(nc, A):
    ring_place = plan_ring()
    jobs, job_at = plan_jobs()
    ctx = ExitStack()
    with ctx:
        def sb(name, shape):
            return ctx.enter_context(nc.sbuf_tensor(name, shape, F32))

        def sem(name):
            return ctx.enter_context(nc.semaphore(name))

        ring = sb("ring", [P, R, KC * UC])
        x = sb("x", [P, NB, D])
        xn = sb("xn", [P, NB, D])
        hT = sb("hT", [P, KC, NT])
        work = sb("work", [P, NB * 1536 + 8 * NT])
        V = sb("V", [P, 4, D])
        pp = sb("pp", [P, 2, 2, 896])
        kT = sb("kT", [P, 4, 4 * P])
        gbc = sb("gbc", [P, 2, 2, D])
        kc = sb("kc", [P, 4, 2, DH])
        ident = sb("ident", [P, P])
        masks = sb("masks", [P, 2, P])
        rope64 = sb("rope64", [P, 2, 2, 32])
        rope32 = sb("rope32", [P, 2, 2, 16])
        sel = sb("sel", [P, 2 * P + 2])
        first = sb("first", [P, 20])
        condT = sb("condT", [P, KC, 32])
        bT = sb("bT", [P, 2, 96])
        gT = sb("gT", [P, 67])
        modc = sb("modc", [P, 4, KC, 2])
        amul = sb("amul", [P, 2, KC, 2])
        wr = sb("wr", [P, KC, E])
        rbias = sb("rbias", [P, E])
        gains = sb("gains", [P, 2, DH])
        kvg = sb("kvg", [P, MLA_KV])
        small = sb("small", [P, 128])
        sink = sb("sink", [P, 2, 2, H])
        neg_max = sb("neg_max", [P, H, NB])
        den = sb("den", [P, H, NB])
        rden = sb("rden", [P, H, NB])
        esink = sb("esink", [P, H, NB])
        gates = sb("gates", [P, NB, E])
        before = sb("before", [P, P])
        ones = sb("ones", [P, P])
        iota = sb("iota", [P, NT])
        token = sb("token", [P, NB])
        slot_of = sb("slot_of", [P, NB, E])
        vals = sb("vals", [P, NB, E, 4])
        slotted = sb("slotted", [P, E, 4])
        idx = ctx.enter_context(nc.sbuf_tensor("idx", [P, 2, E], U32))
        idx_f = sb("idx_f", [P, 2, E])
        load = sb("load", [P, E])
        over_f = sb("over_f", [1, 2 * DEPTH + 2])
        over = ctx.enter_context(nc.sbuf_tensor("over", [1, 2 * DEPTH + 2], U32))
        ov_vals = sb("ov_vals", [P, NB, 4])
        ov_slotted = sb("ov_slotted", [P, 4])
        ov_idx = ctx.enter_context(nc.sbuf_tensor("ov_idx", [P, 2], U32))
        h_rows = nc.dram_tensor("h_rows", [NT, D], F32).ap()
        y_rows = nc.dram_tensor("y_rows", [2 * NT, D], F32).ap()

        qkv = work[:, 0:NB * 1536].rearrange("p (b n) -> p b n", b=NB)
        qT = work[:, NB * 1536:].rearrange("p (k n) -> p k n", k=8)
        rows = work[:, 0:6 * D]
        raw = xn[:, 0, 0:4 * P]
        Vw = V[:, :, :].rearrange("p a n -> p (a n)")
        xw = xn[:, :, :].rearrange("p a n -> p (a n)")
        y_sum, y_second = V[:, 0:NB, :], xn[:, :, :]
        member = Vw[:, 0:3072].rearrange("p (s b e n) -> p s b e n", s=2, b=NB, e=4)
        xg = hT[:, :, :].rearrange("p a n -> p (a n)")[:, 0:2 * D].rearrange("p (s n) -> p s n", s=2)
        ys = kT[:, :, :].rearrange("p a n -> p (a n)").rearrange("p (s n) -> p s n", s=2)
        ql = xn[:, 0:2, :].rearrange("p a n -> p (a n)")[:, 0:NB * MLA_Q].rearrange("p (b n) -> p b n", b=NB)
        qlT = hT[:, 0:3, :]
        ckvT = hT[:, 3:6, :].rearrange("p a n -> p (a n)")[:, 0:1024].rearrange("p (c n) -> p c n", c=2)
        wo_tmp = pp[:, 0, :, :].rearrange("p s n -> p (s n)")[:, 0:4 * UC].rearrange("p (s n) -> p s n", s=4)
        squares = pp[:, :, :, :].rearrange("p a s n -> p (a s n)")
        ckv = squares[:, 1408:2560].rearrange("p (b n) -> p b n", b=4)
        kpe = squares[:, 2560:2944].rearrange("p (b n) -> p b n", b=4)
        sil = squares[:, 0:512].rearrange("p (s n) -> p s n", s=2)
        act_sb = squares[:, 512:1024].rearrange("p (s n) -> p s n", s=2)
        actT = squares[:, 1024:1536].rearrange("p (s c n) -> p s c n", s=2, c=2)
        xT = squares[:, 1536:3584].rearrange("p (s k n) -> p s k n", s=2, k=KC)
        ov_w = [Vw[:, 0:2048].rearrange("p (k n) -> p k n", k=KC), Vw[:, 2048:4096].rearrange("p (k n) -> p k n", k=KC),
                xw[:, 0:2048].rearrange("p (k n) -> p k n", k=2)]
        ov_member = xw[:, 2048:2432].rearrange("p (b n) -> p b n", b=NB)
        rt = kT[:, :, :].rearrange("p a n -> p (a n)")[:, 0:12 * NB * E].rearrange(
            "p (a b e) -> p a b e", a=12, b=NB)

        bank = [ctx.enter_context(nc.psum_tensor(f"bank{i}", [P, 512], F32)) for i in range(8)]

        slot_full = [sem(f"slot_full{s}") for s in range(R)]
        slot_used = [sem(f"slot_used{s}") for s in range(R)]
        bank_full, freed_v, freed_a = sem("bank_full"), sem("freed_v"), sem("freed_a")
        const_in, cond_in, x_in, cache_in, y_stored, out_done = (sem(s) for s in
            ("const_in", "cond_in", "x_in", "cache_in", "y_stored", "out_done"))
        bmod_in, y_in = [sem("bmod_in0"), sem("bmod_in1")], [sem(f"y_in{b}") for b in range(NB)]
        v_chain, a_chain, p_chain = sem("v_chain"), sem("a_chain"), sem("p_chain")
        raw_silu, raw_ready, mod_ready, mod_full, rows_done = (sem(s) for s in
            ("raw_silu", "raw_ready", "mod_ready", "mod_full", "rows_done"))
        sumsq, rstd_ready, xn_ready, wo_mul, x_mixed, x_moe, x_moe_v = (sem(s) for s in
            ("sumsq", "rstd_ready", "xn_ready", "wo_mul", "x_mixed", "x_moe", "x_moe_v"))
        head_sq, head_ms, head_rstd, roped_v, roped_p, qk_ready = (sem(s) for s in
            ("head_sq", "head_ms", "head_rstd", "roped_v", "roped_p", "qk_ready"))
        max_ready, probs, pt_full, pt_a, pt_v, o_full, o_ready, esink_in, esink_done = (sem(s) for s in
            ("max_ready", "probs", "pt_full", "pt_a", "pt_v", "o_full", "o_ready", "esink_in", "esink_done"))
        lat_sq, lat_rstd, states = (sem(s) for s in ("lat_sq", "lat_rstd", "states"))
        freed = {"v": freed_v, "a": freed_a, "p": probs, "w": wo_mul}
        (gates_ready, au_full, sil_full, act_full, acT_full, acT_ready, y_full, y_a, y_v, ys_free) = (sem(s) for s in
            ("gates_ready", "au_full", "sil_full", "act_full", "acT_full", "acT_ready", "y_full", "y_a", "y_v",
             "ys_free"))
        member_ready, idx_ready, over_ready, h_out, xT_full, xT_a, xT_v, work_free = (sem(s) for s in
            ("member_ready", "idx_ready", "over_ready", "h_out", "xT_full", "xT_a", "xT_v", "work_free"))
        g_in, y_out = [sem("g_in0"), sem("g_in1")], [sem("y_out0"), sem("y_out1")]
        (ov_member_ready, ov_idx_full, ov_idx_ready, ov_g_in, ov_xT_full, ov_xT_ready, ov_w_in, ov_au_full, ov_sil,
         ov_act, ov_acT_full, ov_acT_ready, ov_y_full, ov_y, ov_y_out) = (sem(s) for s in
            ("ov_member_ready", "ov_idx_full", "ov_idx_ready", "ov_g_in", "ov_xT_full", "ov_xT_ready", "ov_w_in",
             "ov_au_full", "ov_sil", "ov_act", "ov_acT_full", "ov_acT_ready", "ov_y_full", "ov_y", "ov_y_out"))
        ov_chain, ov_done, ov_issued = sem("ov_chain"), sem("ov_done"), sem("ov_issued")

        def job_bank(key):
            return bank[jobs[key][0] % 4]

        def wait_bank_free(pe, key):
            n = jobs[key][0]
            if n >= 4:
                _, eng, cnt = job_at[n - 4]
                pe.wait_ge(freed[eng], cnt)

        def wait_bank_full(eng, key):
            eng.wait_ge(bank_full, jobs[key][0] + 1)

        def wait_evacuated(eng, *keys):
            for name in "va":
                cnt = [jobs[k][2] for k in keys if jobs[k][1] == name]
                if cnt:
                    eng.wait_ge(freed[name], max(cnt))

        def unit(key):
            return ring[:, ring_place[key][0], :]

        def pass_on(eng, ukey):
            eng.sem_inc(slot_used[ring_place[ukey][0]], 1)

        LAT = (("dq", 0, 256), ("dq", 1, 128), ("dkv", 0, 256), ("dkv", 1, 32))

        def last_reader_of(key):
            if key[0] in ("qkv", "wo", "uq") and key[3] == 2:
                return key[:3]
            if key[0] == "lat" and key[3] == 2:
                return (LAT[key[2]][0], key[1], LAT[key[2]][1])
            if key[0] == "kT" and KINDS[key[1]] == 2 and key[2] % 8 == 7:
                return ("ukv", key[1], key[2] // 8)
            return None

        def mine(key, name):
            return jobs[key][1] == name

        SW = {0: 0, 3: 1}
        CHUNKS = {L: ([range(H)] if KINDS[L] < 2 else [range(4 * c, 4 * c + 4) for c in range(4)])
                  for L in range(DEPTH)}

        PARTS = [(1, 0, 0, 384), (0, 0, 384, 128), (2, 1, 0, 384)]

        def rope(eng, ops, heads, table, half, scratch, link, done):
            n = heads.shape[1]
            x1, x2 = heads[:, :, 0:half], heads[:, :, half:2 * half]
            cos = table[:, 0, :].unsqueeze(1).to_broadcast([P, n, half])
            sin = table[:, 1, :].unsqueeze(1).to_broadcast([P, n, half])
            t = [scratch[:, j * n * half:(j + 1) * n * half].rearrange("p (h d) -> p h d", d=half) for j in range(4)]
            ops.tensor_tensor(t[0], x1, cos, ALU.mult)
            ops.tensor_tensor(t[1], x2, sin, ALU.mult)
            ops.tensor_tensor(t[2], x2, cos, ALU.mult)
            link(ops.tensor_tensor(t[3], x1, sin, ALU.mult))
            ops.tensor_tensor(x1, t[0], t[1], ALU.subtract)
            ops.tensor_tensor(x2, t[2], t[3], ALU.add).then_inc(done, 1)

        def dest(key):
            ps = job_bank(key)
            if key[0] == "qkv":
                _, L, u, b = key
                if u < 4:
                    return qkv[:, b, u * UC:(u + 1) * UC], ps[:, 0:UC]
                if u == 4:
                    return (qkv[:, b, 1024:1536].rearrange("p (g t d) -> p g t d", g=G, t=2),
                            ps[:, 0:UC].rearrange("p (g d) -> p g d", g=G).unsqueeze(2).to_broadcast([P, G, 2, DH]))
                return V[:, b, 0:UC], ps[:, 0:UC]
            if key[0] == "lat":
                _, L, u, b = key
                if u < 2:
                    n = (256, 128)[u]
                    return ql[:, b, u * 256:u * 256 + n], ps[:, 0:n]
                n = (256, 32)[u - 2]
                return ckv[:, b, (u - 2) * 256:(u - 2) * 256 + n], ps[:, 0:n]
            if key[0] == "uq":
                _, L, u, b = key
                return qkv[:, b, u * 512:(u + 1) * 512], ps[:, :]
            if key[0] == "V":
                _, L, u, kb = key
                return V[:, kb, u * 512:(u + 1) * 512], ps[:, :]
            if key[0] == "ckvT":
                return ckvT[:, key[2], :], ps[:, :]
            if key[0] == "kT":
                if KINDS[key[1]] < 2:
                    return kT[:, key[2], :], ps[:, :]
                return kT[0:64, key[2] % 4, :], ps[0:64, :]
            if key[0] == "oT":
                return hT[:, key[2], :], ps[:, 0:NT]
            if key[0] == "hrow":
                return xn[:, key[2], key[3] * 512:(key[3] + 1) * 512], ps[:, :]
            raise KeyError(key)

        def further_passes(eng, L, step):
            eng.wait_ge(over_ready, L + 1)
            flag = eng.value_load(over[0:1, L:L + 1], min_val=0, max_val=1)
            with eng.If(flag > 0):
                gone = eng.value_load(over[0:1, DEPTH + L:DEPTH + L + 1], min_val=0, max_val=STEPS * (DEPTH - 1))
                with eng.Fori(0, NT // SLOTS - 1) as q:
                    with eng.Fori(0, E) as e:
                        step(eng.snap(gone + q * E + e), q, e)

        def each_expert(eng, body):
            body(0, 0)
            with eng.Fori(0, PAIRS - 1) as i:
                body(i, 1)
                body(i + 1, 0)
            body(PAIRS - 1, 1)

        def is_first(t, e):
            return type(t) is int and t == 0 and e == 0

        def is_last(t, e):
            return type(t) is int and t == PAIRS - 1 and e == 1

        def before_one(t, e):
            return (t, 0) if e == 1 else (t - 1, 1)

        def gate_of(t, e):
            return slotted[:, 2 * t + e, 3:4] if type(t) is int else slotted[:, bass.ds(t * 2 + e, 1), 3]

        def turn_act(act, n, slot):
            act.wait_ge(acT_full, n + 1)
            nc.scalar.copy(actT[:, slot], bank[2][:, 0:2 * P].rearrange("p (c n) -> p c n", c=2)).then_inc(acT_ready, 1)

        def unit_heads(u):
            n = UC if u < 4 else 2 * UC
            return qkv[:, :, u * UC:u * UC + n], squares[:, 0:NB * n].rearrange("p (b n) -> p b n", b=NB)

        def load_all(eng, pairs, done):
            for dst, src in pairs:
                eng.dma_start(dst, src).then_inc(done, 16)

        block = ctx.enter_context(nc.Block())

        @block.sync
        def _(sp):
            def fill(key, src, dst_cols, i=None, shape=None):
                slot, before = ring_place[key]
                n = before if i is None else before + i
                sp.wait_ge(slot_used[slot], n + 1)
                dst = ring[:, slot, 0:dst_cols]
                if shape is not None:
                    dst = dst.rearrange("p (k n) -> p k n", k=shape)
                sp.dma_start(dst, src).then_inc(slot_full[slot], 16)

            def cols(w, n0, n):
                return w[:, n0:n0 + n].rearrange("(k p) n -> p k n", p=P)

            def fill_mod(key, L, m, i=None):
                src = A["w_mod"][L, :, bass.ds(m * UC, UC)] if i is not None else A["w_mod"][L, :, m * UC:(m + 1) * UC]
                fill(key, src.rearrange("(k p) n -> p k n", p=P), KC * UC, i, KC)

            for slot in range(R):
                sp.sem_inc(slot_used[slot], 1)
            load_all(sp, ((raw[0:8, 0:P], A["c_ctx"].rearrange("(k p) -> k p", p=P)),
                      (raw[8:16, 0:P], A["c"].rearrange("a (k p) -> (a k) p", p=P)),
                      (ident[:, :], A["ident"]),
                      (raw[0:32, P:2 * P], A["norm_mix"].rearrange("l (k p) -> (l k) p", p=P)),
                      (raw[32:64, P:2 * P], A["norm_ffn"].rearrange("l (k p) -> (l k) p", p=P)),
                      (raw[64:67, P:2 * P], A["mla_qnorm"].rearrange("l (k p) -> (l k) p", p=P)),
                      (raw[0:96, 2 * P:3 * P], A["b_mod"][0:2].rearrange("l (k p) -> (l k) p", p=P)),
                      (raw[0:96, 3 * P:4 * P], A["b_mod"][2:4].rearrange("l (k p) -> (l k) p", p=P))), cond_in)
            for m in range(8):
                fill_mod(("mod0", m), 0, m)
            for L in range(DEPTH):
                s = STACK[L]
                for key in layer_units(L):
                    name, u = key[0], key[-1]
                    if name == "mod0":
                        fill_mod(key, 0, u)
                    elif name == "qkv":
                        w = A["swa_wqkv" if KINDS[L] == 0 else "qkn_wqkv"][s]
                        fill(key, cols(w, u * UC, UC), KC * UC, None, KC)
                    elif name == "wo":
                        w = A[("swa_wo", "qkn_wo", "mla_wo")[KINDS[L]]][s]
                        fill(key, cols(w, u * UC, UC), KC * UC, None, KC)
                    elif name == "dq":
                        n = (256, 128)[u]
                        fill(key, cols(A["mla_wdq"][s], u * 256, n), KC * n, None, KC)
                    elif name == "dkv":
                        n = (256, 32)[u]
                        fill(key, cols(A["mla_wdkv"][s], u * 256, n), KC * n, None, KC)
                    elif name == "uq":
                        fill(key, cols(A["mla_wuq"][s], u * 512, 512), 3 * 512, None, 3)
                    elif name == "ukv":
                        fill(key, cols(A["mla_wukv"][s], u * 1024, 1024), 2 * 1024, None, 2)
                for m in range(MODA if L < DEPTH - 1 else 0):
                    fill_mod(("modA", L, m), L + 1, m)

                def expert_fill(w, t, e):
                    src = A[("moe_w_gate", "moe_w_up", "moe_w_down")[w]][L, bass.ds(t * 2 + e, 1), :, :].rearrange(
                        "e (k p) n -> p (e k) n", p=P)
                    fill(("exp", L, 4 * e + w), src, KC * UC, t, (KC, KC, 2)[w])

                def expert(t, e):
                    expert_fill(0, t, e)
                    expert_fill(1, t, e)
                    if not is_first(t, e):
                        expert_fill(2, *before_one(t, e))
                    if L < DEPTH - 1:
                        fill_mod(("exp", L, 4 * e + 3), L + 1, t * 2 + (e + MODA), t)
                    if is_last(t, e):
                        expert_fill(2, t, e)

                each_expert(sp, expert)
                for m in range(MODB if L < DEPTH - 1 else 0):
                    fill_mod(("modB", L, m), L + 1, MODA + E + m)

                def step(n, q, e):
                    sp.wait_ge(ov_y_full, n + 1)
                    for w in range(3):
                        src = A[("moe_w_gate", "moe_w_up", "moe_w_down")[w]][L, bass.ds(e, 1), :, :].rearrange(
                            "e (k p) n -> p (e k) n", p=P)
                        sp.dma_start(ov_w[w], src).then_inc(ov_w_in, 16)

                sp.wait_ge(idx_ready, 4 * (L + 1))
                sp.wait_ge(h_out, 16 * (L + 1))
                further_passes(sp, L, step)
                for b in range(NB):
                    sp.wait_ge(y_in[b], 32 * (L + 1))

        @block.gpsimd
        def _(pool):
            chain = [0]

            def link(ins):
                chain[0] += 1
                ins.then_inc(p_chain, 1)
                pool.wait_ge(p_chain, chain[0])

            def rms_power(ss, out, n, done):
                link(nc.gpsimd.tensor_scalar(out, ss, 1.0 / n, EPS, ALU.mult, ALU.add))
                nc.gpsimd.tensor_tensor(out, out, exponent(out), ALU.pow).then_inc(done, 1)

            def exponent(like):
                n = 1
                for d in like.shape[1:]:
                    n *= d
                e = minus_half[:, 0:n]
                if len(like.shape) == 3:
                    e = e.rearrange("p (a b) -> p a b", a=like.shape[1])
                return e

            def gate_bias(L, g, dst):
                for c in range(2):
                    pool.dma_start(dst[:, c, :], A["b_mod"][L, (2, 5)[g] * D:(3, 6)[g] * D]
                                   .partition_broadcast(P)).then_inc(bmod_in[g], 16)

            minus_half = small[:, 56:128]
            link(nc.gpsimd.memset(minus_half, -0.5))
            link(nc.gpsimd.memset(ones[:, :], 1.0))
            pool.sem_inc(ys_free, 2)
            pool.sem_inc(ov_done, 1)
            pool.wait_ge(cond_in, 16 * 8)
            pool.dma_start(x[:, 0, :], A["x_prompt"][0]).then_inc(x_in, 16)
            pool.dma_start(x[:, 1:3, :], A["x_sample"][0].rearrange("(b p) d -> p b d", p=P)).then_inc(x_in, 16)
            gate_bias(0, 0, gbc[:, 0])
            gate_bias(0, 1, gbc[:, 1])

            last_token, last_pick = pool.to_reg(NT - 1), pool.to_reg(2 * NT - 1)

            def rows_at(ap):
                return bass.IndirectOffsetOnAxis(ap=ap, axis=0)

            def norm_power(n):
                pool.wait_ge(sumsq, 3 * n + 3)
                rms_power(small[:, 0:3], small[:, 4:7], D, rstd_ready)

            nsq = 0
            for L in range(DEPTH):
                s, kind = STACK[L], KINDS[L]
                norm_power(2 * L)
                if L > 0:
                    pool.wait_ge(x_moe, 3 * L)
                    pool.wait_ge(x_moe_v, 3 * L)
                if KINDS[L] < 2:
                    ck, cv = (("cache_swa_k", "cache_swa_v"), ("cache_qkn_k", "cache_qkn_v"))[KINDS[L]]
                    for dup in range(2):
                        pool.dma_start(kc[:, :, dup, :], A[ck][0, s]).then_inc(cache_in, 16)
                    pool.dma_start(V[:, 3, 0:256], A[cv][0, s].rearrange("t g d -> t (g d)")).then_inc(cache_in, 16)
                if KINDS[L] == 1:
                    for u in range(5):
                        n = NB * (4 if u < 4 else 8)
                        pool.wait_ge(head_ms, u + 1)
                        rms_power(small[:, 8:8 + n], small[:, 32:32 + n], DH, head_rstd)
                if KINDS[L] < 2:
                    if KINDS[L] == 0:
                        wait_evacuated(pool, *[("qkv", L, u, 2) for u in range(5)])
                    else:
                        pool.wait_ge(qk_ready, 5)
                    rope(pool, nc.gpsimd, qkv[:, 2, :].rearrange("p (h d) -> p h d", d=DH), rope64[:, 1], 32,
                         squares, link, roped_p)
                else:
                    pool.dma_start(ckv[:, 3, 0:256], A["cache_mla_ckv"][0, s]).then_inc(cache_in, 16)
                    link(nc.gpsimd.memset(kpe[:, :, :], 0.0))
                    pool.dma_start(kpe[:, 3, 64:96], A["cache_mla_kpe"][0, s]).then_inc(cache_in, 16)
                    pool.wait_ge(lat_sq, 1)
                    rms_power(small[:, 8:14], small[:, 14:20], 1, lat_rstd)
                if kind < 2:
                    sk, sv = (("state_swa_k", "state_swa_v"), ("state_qkn_k", "state_qkn_v"))[kind]
                    wait_evacuated(pool, ("qkv", L, 4, 0), ("qkv", L, 5, 0))
                    pool.dma_start(A[sk][0, s], qkv[:, 0, 1024:1536].rearrange("p (g t d) -> p g t d", g=G, t=2)
                                   [:, :, 0, :]).then_inc(states, 16)
                    pool.dma_start(A[sv][0, s].rearrange("t g d -> t (g d)"), V[:, 0, 0:256]).then_inc(states, 16)
                else:
                    pool.wait_ge(roped_v, 4)
                    pool.dma_start(A["state_mla_ckv"][0, s], ckv[:, 0, 0:256]).then_inc(states, 16)
                    pool.dma_start(A["state_mla_kpe"][0, s], kpe[:, 0, 64:96]).then_inc(states, 16)
                for u in range(4):
                    for b in range(NB):
                        g = 12 * L + 3 * u + b
                        pool.wait_ge(wo_mul, g + 1)
                        xs = x[:, b, u * UC:(u + 1) * UC]
                        nc.gpsimd.tensor_tensor(xs, xs, wo_tmp[:, g % 4, :], ALU.add).then_inc(x_mixed, 1)
                pool.wait_ge(x_mixed, 12 * L + 12)
                pool.wait_ge(states, 32 * (L + 1))
                pool.sem_inc(work_free, 1)
                norm_power(2 * L + 1)
                wait_evacuated(pool, *[("hrow", L, b, half) for b in range(NB) for half in range(2)])
                pool.dma_start(h_rows.rearrange("(b p) d -> p b d", p=P), xn[:, :, :]).then_inc(h_out, 16)
                pool.wait_ge(h_out, 16 * (L + 1))

                def gather(e):
                    pool.wait_ge(idx_ready, 4 * L + e // 4 + 1)
                    if e >= 2:
                        pool.wait_ge(xT_full, E * L + e - 1)
                    nc.gpsimd.indirect_dma_start(xg[:, e % 2, :], None, h_rows, rows_at(idx[:, 0, e:e + 1]),
                                                 bounds_check=last_token, oob_is_err=False).then_inc(g_in[e % 2], 16)

                def scattered(e):
                    pool.wait_ge(y_out[e % 2], 16 * (E // 2 * L + e // 2 + 1))
                    pool.sem_inc(ys_free, 1)

                gather(0)
                gather(1)
                if L < DEPTH - 1:
                    gate_bias(L + 1, 0, gbc[:, 0])
                else:
                    pool.dma_start(gbc[:, 0, 0, :], A["final_norm"].partition_broadcast(P)).then_inc(x_in, 16)
                gather(2)
                for e in range(E):
                    if e + 3 < E:
                        gather(e + 3)
                    if e > 0:
                        scattered(e - 1)
                    pool.wait_ge(y_a, E * L + e + 2)
                    pool.wait_ge(y_v, E * L + e + 2)
                    nc.gpsimd.indirect_dma_start(y_rows, rows_at(idx[:, 1, e:e + 1]), ys[:, e % 2, :], None,
                                                 bounds_check=last_pick, oob_is_err=False).then_inc(y_out[e % 2], 16)
                scattered(E - 1)

                def step(n, q, e):
                    pool.wait_ge(ov_idx_ready, n + 1)
                    pool.sem_inc(ov_issued, 1)
                    nc.gpsimd.indirect_dma_start(xg[:, 0, :], None, h_rows, rows_at(ov_idx[:, 0:1]),
                                                 bounds_check=last_token, oob_is_err=False).then_inc(ov_g_in, 16)
                    pool.wait_ge(ov_y, n + 1)
                    pool.sem_inc(ov_issued, 1)
                    nc.gpsimd.indirect_dma_start(y_rows, rows_at(ov_idx[:, 1:2]), ys[:, 0, :], None,
                                                 bounds_check=last_pick, oob_is_err=False).then_inc(ov_y_out, 16)
                    pool.wait_ge(ov_y_out, (n + 1) * 16)
                    pool.sem_inc(ov_done, 1)

                further_passes(pool, L, step)
                pool.sem_inc(y_stored, 1)
                if L < DEPTH - 1:
                    gate_bias(L + 1, 1, ys)
                for b in range(NB):
                    pool.wait_ge(y_in[b], 32 * (L + 1))
                    c = slice(VC, D)
                    link(nc.gpsimd.tensor_tensor(y_sum[:, b, c], y_sum[:, b, c], y_second[:, b, c], ALU.add))
                    link(nc.gpsimd.tensor_tensor(y_sum[:, b, c], y_sum[:, b, c], gbc[:, 1, COND[b], c], ALU.mult))
                    nc.gpsimd.tensor_tensor(x[:, b, c], x[:, b, c], y_sum[:, b, c], ALU.add).then_inc(x_moe, 1)
            norm_power(2 * DEPTH)
            pool.wait_ge(xn_ready, 3 * (2 * DEPTH + 1) + 1)
            pool.dma_start(A["y_prompt"][0], xn[:, 0, :]).then_inc(out_done, 16)
            pool.dma_start(A["y_sample"][0].rearrange("(b p) d -> p b d", p=P), xn[:, 1:3, :]).then_inc(out_done, 16)
            pool.wait_ge(out_done, 32)
            pool.wait_ge(states, 32 * DEPTH)

        @block.scalar
        def _(act):
            chain = [0]

            def link(ins):
                chain[0] += 1
                ins.then_inc(a_chain, 1)
                act.wait_ge(a_chain, chain[0])

            def free(ins):
                ins.then_inc(freed_a, 1)

            def evacuate(*keys):
                for key in keys:
                    if mine(key, "a"):
                        wait_bank_full(act, key)
                        if last_reader_of(key):
                            pass_on(act, last_reader_of(key))
                        free(nc.scalar.copy(*dest(key)))

            def norm_in(n, L, odd):
                for b in range(NB):
                    if n == 0:
                        act.wait_ge(x_in, 32)
                    elif odd:
                        act.wait_ge(x_mixed, 12 * L + 9 + b + 1)
                    else:
                        act.wait_ge(x_moe, 3 * (L - 1) + b + 1)
                        act.wait_ge(x_moe_v, 3 * (L - 1) + b + 1)
                    nc.scalar.activation(xn[:, b, :], x[:, b, :], ACT.Square,
                                         accum_out=small[:, b:b + 1]).then_inc(sumsq, 1)

            def norm_out(n, s):
                for k in range(KC):
                    key = ("norm", n, k)
                    if mine(key, "a"):
                        wait_bank_full(act, key)
                        act.wait_ge(mod_ready, n + 1)
                        ps = job_bank(key)
                        nc.scalar.activation(hT[:, k, 0:P], ps[:, 0:P], ACT.Identity,
                                             bias=modc[:, 2 * s, k, 0:1], scale=amul[:, s, k, 0:1])
                        free(nc.scalar.activation(hT[:, k, P:NT], ps[:, P:NT], ACT.Identity,
                                                  bias=modc[:, 2 * s, k, 1:2], scale=amul[:, s, k, 1:2]))

            def mod_rows(key, base, m, bk):
                act.wait_ge(mod_full, base + m + 1)
                pass_on(act, key)
                at = slice(m * UC, (m + 1) * UC) if type(m) is int else bass.ds(m * UC, UC)
                nc.scalar.copy(rows[:, at], bank[bk][:, 0:UC]).then_inc(rows_done, 1)

            load_all(act, ((masks[:, :, :], A["masks"].rearrange("p (a n) -> p a n", a=2)),
                       (rope64[:, :, :, :], A["rope64"].rearrange("p (a c n) -> p a c n", a=2, c=2)),
                       (rope32[:, :, :, :], A["rope32"].rearrange("p (a c n) -> p a c n", a=2, c=2)),
                       (sel[:, :], A["sel"]), (first[:, :], A["first"]),
                       (before[:, :], A["before"]), (iota[:, :], A["iota"]), (token[:, :], A["token"]),
                       (wr[:, :, :], A["w_router"].rearrange("(k p) e -> p k e", p=P)),
                       (rbias[:, :], A["router_bias"].partition_broadcast(P)),
                       (gains[:, 0, :], A["qkn_qnorm"][0].partition_broadcast(P)),
                       (gains[:, 1, :], A["qkn_knorm"][0].partition_broadcast(P)),
                       (kvg[:, :], A["mla_kvnorm"][0].partition_broadcast(P)),
                       (sink[:, 0, 0, :], A["swa_sink"][0].partition_broadcast(P)),
                       (sink[:, 1, 0, :], A["swa_sink"][1].partition_broadcast(P))), const_in)
            act.sem_inc(rows_done, 1)
            act.sem_inc(acT_ready, 1)
            act.sem_inc(y_a, 1)
            act.sem_inc(xT_a, 1)
            act.sem_inc(ov_y_full, 1)
            act.wait_ge(cond_in, 16 * 8)
            nc.scalar.activation(raw[0:16, 0:P], raw[0:16, 0:P], ACT.Silu).then_inc(raw_silu, 1)
            for m in range(8):
                mod_rows(("mod0", m), 0, m, 7)

            for L in range(DEPTH):
                kind, s = KINDS[L], STACK[L]
                norm_in(2 * L, L, False)
                norm_out(2 * L, 0)
                if kind < 2:
                    for u in range(6):
                        evacuate(*[("qkv", L, u, b) for b in range(NB)])
                        if kind == 1 and u < 5:
                            wait_evacuated(act, *[("qkv", L, u, b) for b in range(NB)])
                            if u > 0:
                                act.wait_ge(head_ms, u)
                            src, sq = unit_heads(u)
                            nc.scalar.activation(sq, src, ACT.Square).then_inc(head_sq, 1)
                else:
                    evacuate(*[("lat", L, u, b) for u in range(4) for b in range(NB)])
                    wait_evacuated(act, *[("lat", L, u, b) for u in range(4) for b in range(NB)])
                    for b in range(NB):
                        nc.scalar.activation(squares[:, 448 * b:448 * b + 384], ql[:, b, :], ACT.Square, scale=384 ** -0.5,
                                             accum_out=small[:, 8 + b:9 + b])
                        last = nc.scalar.activation(kT[:, b, 0:256], ckv[:, b, 0:256], ACT.Square,
                                                    scale=256 ** -0.5, accum_out=small[:, 11 + b:12 + b])
                    last.then_inc(lat_sq, 1)
                    evacuate(*[("ckvT", L, c) for c in range(2)])
                    evacuate(*[("uq", L, u, b) for u in range(3) for b in range(NB)])
                    evacuate(*[("V", L, u, kb) for u in range(2) for kb in range(4)])
                if kind == 2:
                    act.wait_ge(states, 32 * (L + 1))
                qscale = (DH if kind < 2 else DQK) ** -0.5
                for heads in CHUNKS[L]:
                    keys = ([("qT", L, p) for p in range(8)] + [("kT", L, g) for g in range(G)] if kind < 2 else
                            [("kT", L, h) for h in heads] + [("qT", L, h) for h in heads])
                    for key in keys:
                        if not mine(key, "a"):
                            continue
                        if key[0] == "kT":
                            evacuate(key)
                            continue
                        wait_bank_full(act, key)
                        rws = P if kind < 2 else DQK
                        free(nc.scalar.mul(qT[0:rws, key[2] % 8, :], job_bank(key)[0:rws, 0:NT], qscale))

                    def turn(h):
                        n = L * H + h
                        act.wait_ge(pt_full, 2 * n + 1)
                        nc.scalar.copy(pp[:, 1, h % 2, 0:512], bank[4][:, :]).then_inc(pt_a, 1)

                    for h in heads:
                        n = L * H + h
                        act.wait_ge(max_ready, n + 1)
                        if h >= 2:
                            act.wait_ge(pt_full, 2 * (n - 2) + 2)
                        if kind == 0:
                            nc.scalar.activation(esink[:, h, :], neg_max[:, h, :], ACT.Exp,
                                                 bias=sink[:, SW[L], 0, h:h + 1])
                        for b, i, c0, w in PARTS:
                            ins = nc.scalar.activation(pp[:, 0, h % 2, 512 * i + c0:512 * i + c0 + w],
                                                       job_bank(("S", L, h, i))[:, c0:c0 + w], ACT.Exp,
                                                       bias=neg_max[:, h, b:b + 1], accum_out=den[:, h, b:b + 1])
                        ins.then_inc(probs, 1)
                        if h > heads[0]:
                            turn(h - 1)
                    turn(heads[-1])
                evacuate(*[("oT", L, k) for k in range(KC)])
                for m in range(8, 24 if L == 0 else 8):
                    mod_rows(("mod0", m), 0, m, 7)
                norm_in(2 * L + 1, L, True)
                norm_out(2 * L + 1, 1)
                wait_bank_full(act, ("router", L))
                free(nc.scalar.activation(rt[:, 0], job_bank(("router", L))[:, 0:NB * E].rearrange(
                    "p (b e) -> p b e", b=NB), ACT.Sigmoid))
                evacuate(*[("hrow", L, b, half) for b in range(NB) for half in range(2)])
                act.wait_ge(work_free, L + 1)
                for m in range(MODA if L < DEPTH - 1 else 0):
                    mod_rows(("modA", L, m), 24 * (L + 1), m, 7)

                def turned_rows(n, slot):
                    act.wait_ge(xT_full, n + 1)
                    nc.scalar.copy(xT[:, slot, 0:4, :], bank[6][:, :].rearrange("p (k n) -> p k n", k=4))\
                        .then_inc(xT_a, 1)

                def first_half(t, e):
                    n = t * 2 + (E * L + e)
                    act.wait_ge(y_full, n + 1)
                    act.wait_ge(ys_free, n + 1)
                    nc.scalar.mul(ys[:, e, 0:512], bank[4][:, :], gate_of(t, e)).then_inc(y_a, 1)

                def expert(t, e):
                    n = t * 2 + (E * L + e)
                    act.wait_ge(au_full, n + 1)
                    pass_on(act, ("exp", L, 4 * e))
                    pass_on(act, ("exp", L, 4 * e + 1))
                    act.wait_ge(act_full, n + 1)
                    nc.scalar.activation(sil[:, e, :], bank[e][:, 0:DE], ACT.Silu).then_inc(sil_full, 1)
                    if not is_first(t, e):
                        first_half(*before_one(t, e))
                    if not is_last(t, e):
                        turned_rows(n + 1, 1 - e)
                    if L < DEPTH - 1:
                        mod_rows(("exp", L, 4 * e + 3), 24 * (L + 1), t * 2 + (MODA + e), 3)
                    turn_act(act, n, e)
                    if is_last(t, e):
                        first_half(t, e)

                turned_rows(E * L, 0)
                each_expert(act, expert)
                for m in range(MODB if L < DEPTH - 1 else 0):
                    mod_rows(("modB", L, m), 24 * (L + 1), MODA + E + m, 3)

                def step(n, q, e):
                    act.wait_ge(ov_au_full, n + 1)
                    nc.scalar.activation(sil[:, 0, :], bank[0][:, 0:DE], ACT.Silu).then_inc(ov_sil, 1)
                    act.wait_ge(ov_acT_full, n + 1)
                    nc.scalar.copy(actT[:, 0], bank[2][:, 0:2 * P].rearrange("p (c n) -> p c n", c=2))\
                        .then_inc(ov_acT_ready, 1)

                further_passes(act, L, step)
                act.wait_ge(y_stored, L + 1)
                for b in range(NB):
                    for k, dst in enumerate((y_sum, y_second)):
                        act.dma_start(dst[:, b, :], y_rows[k * NT + b * P:k * NT + (b + 1) * P, :]).then_inc(y_in[b], 16)
            norm_in(2 * DEPTH, DEPTH, False)

        @block.vector
        def _(dve):
            V_ = nc.vector
            chain = [0]

            def link(ins):
                chain[0] += 1
                ins.then_inc(v_chain, 1)
                dve.wait_ge(v_chain, chain[0])

            def free(ins):
                ins.then_inc(freed_v, 1)

            def evacuate(*keys):
                for key in keys:
                    if mine(key, "v"):
                        wait_bank_full(dve, key)
                        if last_reader_of(key):
                            pass_on(dve, last_reader_of(key))
                        free(V_.tensor_copy(*dest(key)))

            def norm_scale(n):
                dve.wait_ge(rstd_ready, n + 1)
                for b in range(NB):
                    V_.tensor_scalar(xn[:, b, :], x[:, b, :], small[:, 4 + b:5 + b], None,
                                     ALU.mult).then_inc(xn_ready, 1)

            def norm_out(n, s):
                for k in range(KC):
                    key = ("norm", n, k)
                    if mine(key, "v"):
                        wait_bank_full(dve, key)
                        ps = job_bank(key)
                        V_.tensor_scalar(hT[:, k, 0:P], ps[:, 0:P], amul[:, s, k, 0:1], modc[:, 2 * s, k, 0:1],
                                         ALU.mult, ALU.add)
                        free(V_.tensor_scalar(hT[:, k, P:NT], ps[:, P:NT], amul[:, s, k, 1:2],
                                              modc[:, 2 * s, k, 1:2], ALU.mult, ALU.add))

            link(V_.memset(condT[:, :, :], 0.0))
            for key, dst, n in (("cond", condT[:, :, 0:2].rearrange("p k c -> p c k"), 16), ("gains", gT[:, :], 67),
                                (("bias", 0), bT[:, 0, :], 96), (("bias", 1), bT[:, 1, :], 96)):
                wait_bank_full(dve, key)
                src = job_bank(key)[:, 0:n]
                free(V_.tensor_copy(dst, src.rearrange("p (c k) -> p c k", c=2) if n == 16 else src))
            dve.wait_ge(const_in, 16 * 15)
            for w in range(2):
                V_.tensor_scalar(sink[:, w, 1, :], sink[:, w, 0, :], -1.0, None, ALU.mult)
            dve.sem_inc(act_full, 2)
            dve.sem_inc(y_v, 1)
            dve.sem_inc(xT_v, 1)
            link(V_.memset(over_f[:, :], 0.0))

            def mod_columns(L, s):
                key = ("modc", L, s)
                wait_bank_full(dve, key)
                b = bT[:, L // 2, 48 * (L % 2) + 24 * s:48 * (L % 2) + 24 * s + 16].rearrange("p (v k) -> p v k", v=2)
                free(V_.tensor_tensor(modc[:, 2 * s:2 * s + 2],
                                      job_bank(key)[:, 0:32].rearrange("p (v k c) -> p v k c", v=2, k=KC),
                                      b.unsqueeze(3).to_broadcast([P, 2, KC, 2]), ALU.add))
                dve.wait_ge(freed_v, jobs[key][2])
                g = gT[:, 32 * s + 8 * L:32 * s + 8 * L + 8].unsqueeze(2).to_broadcast([P, KC, 2])
                V_.scalar_tensor_tensor(out=amul[:, s], in0=modc[:, 2 * s + 1], scalar=1.0, in1=g,
                                        op0=ALU.add, op1=ALU.mult).then_inc(mod_ready, 1)
                dve.wait_ge(mod_ready, 2 * L + s + 1)

            def spread_gates(L, g):
                dve.wait_ge(bmod_in[g], 32 * (L + 1))
                for j in range(4 * g, 4 * g + 4):
                    key = ("gate", L, j)
                    wait_bank_full(dve, key)
                    bias = ys if g == 1 and L > 0 else gbc[:, g]
                    c = slice(j % 2 * 512, (j % 2 + 1) * 512)
                    free(V_.tensor_tensor(gbc[:, g, j // 2 % 2, c], bias[:, j // 2 % 2, c], job_bank(key)[:, :],
                                          ALU.add))
                dve.wait_ge(freed_v, jobs[("gate", L, 4 * g + 3)][2])

            def route(L):
                s_, sb_, sbm = rt[:, 0], rt[:, 1], rt[:, 2]
                link(V_.tensor_tensor(sb_, s_, rbias[:, :].unsqueeze(1).to_broadcast([P, NB, E]), ALU.add))
                q4 = sb_.rearrange("p b (g j) -> p (b g) j", j=4)
                pair = rt[:, 3:5].rearrange("p a b e -> p (a b e)")[:, 0:72].rearrange("p (q j) -> p q j", j=6)
                V_.tensor_tensor(pair[:, :, 0:3], q4[:, :, 0:3], q4[:, :, 1:4], ALU.add)
                V_.tensor_tensor(pair[:, :, 3:5], q4[:, :, 0:2], q4[:, :, 2:4], ALU.add)
                link(V_.tensor_tensor(pair[:, :, 5:6], q4[:, :, 0:1], q4[:, :, 3:4], ALU.add))
                gs = rt[:, 5, 0, 0:12]
                link(V_.tensor_reduce(gs, pair, AX.X, ALU.max))
                gsb = gs.rearrange("p (b g) -> p b g", b=NB)
                gm = rt[:, 5, 1, 0:3]
                link(V_.tensor_reduce(gm, gsb, AX.X, ALU.max))
                eq = rt[:, 6, 0, 0:12].rearrange("p (b g) -> p b g", b=NB)
                link(V_.tensor_tensor(eq, gsb, gm.unsqueeze(2).to_broadcast([P, NB, 4]), ALU.is_equal))
                link(V_.tensor_tensor(eq, eq, first[:, 16:20].unsqueeze(1).to_broadcast([P, NB, 4]), ALU.mult))
                link(V_.tensor_reduce(gm, eq, AX.X, ALU.max))
                link(V_.tensor_tensor(eq, eq, gm.unsqueeze(2).to_broadcast([P, NB, 4]), ALU.is_equal))
                emask = eq.unsqueeze(3).to_broadcast([P, NB, 4, 4])
                sbm4 = sbm.rearrange("p b (g j) -> p b g j", j=4)
                sb4 = sb_.rearrange("p b (g j) -> p b g j", j=4)
                link(V_.tensor_scalar(rt[:, 7, 0, 0:12], rt[:, 6, 0, 0:12], -NEG, NEG, ALU.mult, ALU.add))
                off = rt[:, 7, 0, 0:12].rearrange("p (b g) -> p b g", b=NB).unsqueeze(3).to_broadcast([P, NB, 4, 4])
                link(V_.tensor_tensor(sbm4, sb4, emask, ALU.mult))
                link(V_.tensor_tensor(sbm4, sbm4, off, ALU.add))
                m = rt[:, 5, 2, 0:3]
                picks = []
                for r in range(2):
                    a = rt[:, 8 + r]
                    link(V_.tensor_reduce(m, sbm, AX.X, ALU.max))
                    link(V_.tensor_tensor(a, sbm, m.unsqueeze(2).to_broadcast([P, NB, E]), ALU.is_equal))
                    link(V_.tensor_tensor(a, a, first[:, 0:16].unsqueeze(1).to_broadcast([P, NB, E]), ALU.mult))
                    link(V_.tensor_reduce(m, a, AX.X, ALU.max))
                    link(V_.tensor_tensor(a, a, m.unsqueeze(2).to_broadcast([P, NB, E]), ALU.is_equal))
                    if r == 0:
                        link(V_.scalar_tensor_tensor(out=sbm, in0=a, scalar=4 * NEG, in1=sbm, op0=ALU.mult,
                                                     op1=ALU.add))
                    picks.append(a)
                V_.tensor_copy(vals[:, :, :, 2], picks[1])
                V_.tensor_copy(vals[:, :, :, 1], token[:, :].unsqueeze(2).to_broadcast([P, NB, E]))
                link(V_.tensor_tensor(vals[:, :, :, 0], picks[0], picks[1], ALU.add))
                V_.tensor_copy(gates[:, :, :], vals[:, :, :, 0]).then_inc(gates_ready, 1)
                link(V_.tensor_tensor(picks[0], vals[:, :, :, 0], s_, ALU.mult))
                link(V_.tensor_reduce(m, picks[0], AX.X, ALU.add))
                link(V_.reciprocal(m, m))
                link(V_.tensor_tensor(vals[:, :, :, 3], picks[0], m.unsqueeze(2).to_broadcast([P, NB, E]), ALU.mult))

            def numbers(src, dst_f, dst):
                link(V_.tensor_scalar(dst_f[:, 1], src[:, :, 0], -BIG, BIG, ALU.mult, ALU.add))
                link(V_.tensor_tensor(dst_f[:, 0], src[:, :, 1], dst_f[:, 1], ALU.add))
                link(V_.scalar_tensor_tensor(out=dst_f[:, 1], in0=src[:, :, 2], scalar=float(NT), in1=dst_f[:, 0],
                                             op0=ALU.mult, op1=ALU.add))
                return V_.tensor_copy(dst, dst_f)

            def index(L):
                key = ("rank", L)
                wait_bank_full(dve, key)
                V_.tensor_copy(load[:, :], job_bank(key)[:, 48:64])
                free(V_.tensor_copy(rt[:, 10], job_bank(key)[:, 0:48].rearrange("p (b e) -> p b e", b=NB)))
                dve.wait_ge(freed_v, jobs[key][2])
                link(V_.tensor_scalar(rt[:, 11], vals[:, :, :, 0], -BIG, BIG, ALU.mult, ALU.add))
                link(V_.tensor_tensor(slot_of[:, :, :], rt[:, 10], rt[:, 11], ALU.add))

                def members(g):
                    V_.tensor_tensor(member[:, g % 2],
                                     iota[:, 0:SLOTS].unsqueeze(1).unsqueeze(1).to_broadcast([P, NB, 4, SLOTS]),
                                     slot_of[:, :, 4 * g:4 * g + 4].unsqueeze(3).to_broadcast([P, NB, 4, SLOTS]),
                                     ALU.is_equal).then_inc(member_ready, 1)

                def slots(g):
                    key = ("idx", L, g)
                    wait_bank_full(dve, key)
                    e = slice(4 * g, 4 * g + 4)
                    free(V_.tensor_copy(slotted[:, e, :], job_bank(key)[:, 0:16].rearrange("p (e v) -> p e v", e=4)))
                    dve.wait_ge(freed_v, jobs[key][2])
                    numbers(slotted[:, e, :], idx_f[:, :, e], idx[:, :, e]).then_inc(idx_ready, 1)

                dve.wait_ge(work_free, L + 1)
                members(0)
                members(1)
                for g in range(4):
                    slots(g)
                    if g < 2:
                        members(g + 2)
                link(V_.tensor_reduce(load[0:1, 0:1], load[0:1, :], AX.X, ALU.max))
                link(V_.tensor_scalar(over_f[0:1, L:L + 1], load[0:1, 0:1], SLOTS + 0.5, None, ALU.is_gt))
                link(V_.scalar_tensor_tensor(out=over_f[0:1, DEPTH + L + 1:DEPTH + L + 2], in0=over_f[0:1, L:L + 1],
                                             scalar=float(STEPS), in1=over_f[0:1, DEPTH + L:DEPTH + L + 1],
                                             op0=ALU.mult, op1=ALU.add))
                V_.tensor_copy(over[:, :], over_f[:, :]).then_inc(over_ready, 1)

            for L in range(DEPTH):
                kind = KINDS[L]
                norm_scale(2 * L)
                if L == 0:
                    mod_columns(0, 0)
                norm_out(2 * L, 0)
                if kind < 2:

                    def normalise(u):
                        hv, sq = unit_heads(u)
                        heads = 4 if u < 4 else 8
                        dve.wait_ge(head_sq, u + 1)
                        V_.tensor_reduce(small[:, 8:8 + NB * heads], sq.rearrange("p b (h d) -> p (b h) d", d=DH),
                                         AX.X, ALU.add).then_inc(head_ms, 1)
                        dve.wait_ge(head_rstd, u + 1)
                        hv = hv.rearrange("p b (h d) -> p b h d", d=DH)
                        rstd = small[:, 32:32 + NB * heads].rearrange("p (b h) -> p b h", b=NB)
                        link(V_.tensor_tensor(hv, hv, rstd.unsqueeze(3).to_broadcast([P, NB, heads, DH]), ALU.mult))
                        gain = gains[:, 0 if u < 4 else 1, :].unsqueeze(1).unsqueeze(1)
                        V_.tensor_tensor(hv, hv, gain.to_broadcast([P, NB, heads, DH]), ALU.mult).then_inc(qk_ready, 1)

                    for u in range(6):
                        evacuate(*[("qkv", L, u, b) for b in range(NB)])
                        if kind == 1 and 1 <= u <= 4:
                            normalise(u - 1)
                        if kind == 1 and u == 4:
                            normalise(4)
                    qk_heads = [qkv[:, b, :].rearrange("p (h d) -> p h d", d=DH) for b in range(NB)]
                    if kind == 1:
                        dve.wait_ge(qk_ready, 5)
                    else:
                        wait_evacuated(dve, *[("qkv", L, u, 1) for u in range(5)])
                    rope(dve, V_, qk_heads[1], rope64[:, 0], 32, xn[:, :, :].rearrange("p b n -> p (b n)"), link,
                         roped_v)
                else:
                    evacuate(*[("lat", L, u, b) for u in range(4) for b in range(NB)])
                    wait_evacuated(dve, *[("lat", L, u, b) for u in range(4) for b in range(NB)])
                    dve.wait_ge(lat_rstd, 1)
                    dve.wait_ge(cache_in, 16 * (3 * 2 + 2))
                    for b in range(NB):
                        V_.tensor_scalar(ql[:, b, :], ql[:, b, :], small[:, 14 + b:15 + b], None, ALU.mult)
                        V_.scalar_tensor_tensor(out=ckv[:, b, 0:256], in0=ckv[:, b, 0:256],
                                                scalar=small[:, 17 + b:18 + b], in1=kvg[:, :], op0=ALU.mult,
                                                op1=ALU.mult)
                        last = V_.tensor_copy(kpe[:, b, 64:96], ckv[:, b, 256:288])
                    link(last)
                    for b in (1, 2):
                        rope(dve, V_, kpe[:, b:b + 1, 64:96], rope32[:, b - 1], 16, squares[:, 1024 + 64 * b:],
                             link, roped_v)
                    for c in range(3):
                        key = ("qlT", L, c)
                        wait_bank_full(dve, key)
                        free(V_.tensor_scalar(qlT[:, c, :], job_bank(key)[:, 0:NT], gT[:, 64 + c:65 + c], None,
                                              ALU.mult))
                    key = ("kpeT", L)
                    wait_bank_full(dve, key)
                    for j in range(4):
                        last = V_.tensor_copy(kT[64:96, j, :], job_bank(key)[64:96, :])
                    free(last)
                    evacuate(*[("uq", L, u, b) for u in range(3) for b in range(NB)])
                    wait_evacuated(dve, *[("uq", L, u, b) for u in range(3) for b in range(NB)])
                    for b in (1, 2):
                        dve.wait_ge(roped_v, 3 + b)
                        rope(dve, V_, qkv[:, b, :].rearrange("p (h d) -> p h d", d=DQK)[:, :, 64:96],
                             rope32[:, b - 1], 16, squares, link, roped_v)
                    evacuate(*[("V", L, u, kb) for u in range(2) for kb in range(4)])
                qscale = (DH if kind < 2 else DQK) ** -0.5

                def turn(h):
                    n = L * H + h
                    dve.wait_ge(pt_full, 2 * n + 2)
                    V_.tensor_copy(pp[:, 1, h % 2, 512:896], bank[5][:, 0:384]).then_inc(pt_v, 1)

                def finish_pair(j):
                    n = L * 8 + j
                    dve.wait_ge(probs, L * H + 2 * j + 2)
                    d_, r_ = den[:, 2 * j:2 * j + 2, :], rden[:, 2 * j:2 * j + 2, :]
                    if kind == 0:
                        link(V_.tensor_tensor(d_, d_, esink[:, 2 * j:2 * j + 2, :], ALU.add))
                    link(V_.reciprocal(r_, d_))
                    dve.wait_ge(o_full, n + 1)
                    src = bank[6 + j % 2][:, 0:384].rearrange("p (b h d) -> p b h d", b=NB, h=2)
                    for b in range(NB):
                        o = xn[:, b, 2 * j * DH:(2 * j + 2) * DH].rearrange("p (h d) -> p h d", h=2)
                        last = V_.tensor_tensor(o, src[:, b], r_[:, :, b:b + 1].to_broadcast([P, 2, DH]), ALU.mult)
                    last.then_inc(o_ready, 1)

                for heads in CHUNKS[L]:
                    keys = ([("qT", L, p) for p in range(8)] + [("kT", L, g) for g in range(G)] if kind < 2 else
                            [("kT", L, h) for h in heads] + [("qT", L, h) for h in heads])
                    for key in keys:
                        if not mine(key, "v"):
                            continue
                        if key[0] == "kT":
                            evacuate(key)
                            continue
                        wait_bank_full(dve, key)
                        rws = P if kind < 2 else DQK
                        free(V_.tensor_scalar(qT[0:rws, key[2] % 8, :], job_bank(key)[0:rws, 0:NT], qscale, None,
                                              ALU.mult))
                    for h in heads:
                        n = L * H + h
                        for b, i, c0, w in PARTS:
                            if b != 0:
                                wait_bank_full(dve, ("S", L, h, i))
                            last = V_.tensor_reduce(neg_max[:, h, b:b + 1], job_bank(("S", L, h, i))[:, c0:c0 + w],
                                                    AX.X, ALU.max, negate=True)
                        if kind == 0:
                            link(last)
                            last = V_.tensor_scalar(neg_max[:, h, :], neg_max[:, h, :], sink[:, SW[L], 1, h:h + 1],
                                                    None, ALU.min)
                        last.then_inc(max_ready, 1)
                        if h > heads[0]:
                            turn(h - 1)
                        if h >= heads[0] + 3 and h % 2 == 1:
                            finish_pair((h - 3) // 2)
                    turn(heads[-1])
                    finish_pair(heads[-1] // 2)
                evacuate(*[("oT", L, k) for k in range(KC)])
                if L == 0:
                    spread_gates(0, 0)
                for u in range(4):
                    for b in range(NB):
                        g = 12 * L + 3 * u + b
                        key = ("wo", L, u, b)
                        wait_bank_full(dve, key)
                        if last_reader_of(key):
                            pass_on(dve, last_reader_of(key))
                        if 3 * u + b >= 4:
                            dve.wait_ge(x_mixed, g - 3)
                        V_.tensor_tensor(wo_tmp[:, g % 4, :], job_bank(key)[:, 0:UC],
                                         gbc[:, 0, COND[b], u * UC:(u + 1) * UC], ALU.mult).then_inc(wo_mul, 1)
                if L == 0:
                    mod_columns(0, 1)
                    spread_gates(0, 1)
                norm_scale(2 * L + 1)
                norm_out(2 * L + 1, 1)
                wait_evacuated(dve, ("router", L))
                evacuate(*[("hrow", L, b, half) for b in range(NB) for half in range(2)])
                route(L)
                index(L)

                def turned_rows(n, slot):
                    dve.wait_ge(xT_full, n + 1)
                    V_.tensor_copy(xT[:, slot, 4:8, :], bank[7][:, :].rearrange("p (k n) -> p k n", k=4))\
                      .then_inc(xT_v, 1)

                def second_half(t, e):
                    n = t * 2 + (E * L + e)
                    dve.wait_ge(y_full, n + 1)
                    pass_on(dve, ("exp", L, 4 * e + 2))
                    dve.wait_ge(ys_free, n + 1)
                    V_.tensor_scalar(ys[:, e, 512:1024], bank[5][:, :], gate_of(t, e), None, ALU.mult).then_inc(y_v, 1)

                def expert(t, e):
                    n = t * 2 + (E * L + e)
                    dve.wait_ge(sil_full, n + 1)
                    V_.tensor_tensor(act_sb[:, e, :], bank[e][:, DE:2 * DE], sil[:, e, :],
                                     ALU.mult).then_inc(act_full, 1)
                    if not is_first(t, e):
                        second_half(*before_one(t, e))
                    if not is_last(t, e):
                        turned_rows(n + 1, 1 - e)
                    if is_last(t, e):
                        second_half(t, e)

                turned_rows(E * L, 0)
                each_expert(dve, expert)
                if L < DEPTH - 1:
                    mod_columns(L + 1, 0)

                def step(n, q, e):
                    dve.wait_ge(ov_done, n + 1)
                    for b in range(NB):
                        V_.tensor_scalar(ov_member[:, b, :], iota[:, bass.ds(q * SLOTS + SLOTS, SLOTS)],
                                         slot_of[:, b, bass.ds(e, 1)], None, ALU.is_equal)
                    V_.tensor_copy(ov_vals[:, :, :], vals[:, :, bass.ds(e, 1), :].rearrange("p b e v -> p b (e v)"))\
                      .then_inc(ov_member_ready, 1)
                    dve.wait_ge(ov_idx_full, n + 1)
                    V_.tensor_copy(ov_slotted[:, :], bank[3][:, 0:4]).then_inc(ov_chain, 1)
                    dve.wait_ge(ov_chain, n * 4 + 1)
                    V_.tensor_scalar(idx_f[:, 1, 0:1], ov_slotted[:, 0:1], -BIG, BIG, ALU.mult,
                                     ALU.add).then_inc(ov_chain, 1)
                    dve.wait_ge(ov_chain, n * 4 + 2)
                    V_.tensor_tensor(idx_f[:, 0, 0:1], ov_slotted[:, 1:2], idx_f[:, 1, 0:1], ALU.add)\
                      .then_inc(ov_chain, 1)
                    dve.wait_ge(ov_chain, n * 4 + 3)
                    V_.scalar_tensor_tensor(out=idx_f[:, 1, 0:1], in0=ov_slotted[:, 2:3], scalar=float(NT),
                                            in1=idx_f[:, 0, 0:1], op0=ALU.mult, op1=ALU.add).then_inc(ov_chain, 1)
                    dve.wait_ge(ov_chain, n * 4 + 4)
                    V_.tensor_copy(ov_idx[:, :], idx_f[:, :, 0]).then_inc(ov_idx_ready, 1)
                    dve.wait_ge(ov_xT_full, n + 1)
                    for half in range(2):
                        last = V_.tensor_copy(xT[:, 0, 4 * half:4 * half + 4, :],
                                              bank[6 + half][:, :].rearrange("p (k n) -> p k n", k=4))
                    last.then_inc(ov_xT_ready, 1)
                    dve.wait_ge(ov_sil, n + 1)
                    V_.tensor_tensor(act_sb[:, 0, :], bank[0][:, DE:2 * DE], sil[:, 0, :], ALU.mult)\
                      .then_inc(ov_act, 1)
                    dve.wait_ge(ov_y_full, n + 2)
                    for half in range(2):
                        last = V_.tensor_scalar(ys[:, 0, half * 512:(half + 1) * 512], bank[4 + half][:, :],
                                                ov_slotted[:, 3:4], None, ALU.mult)
                    last.then_inc(ov_y, 1)

                further_passes(dve, L, step)
                for b in range(NB):
                    dve.wait_ge(y_in[b], 32 * (L + 1))
                    c = slice(0, VC)
                    link(V_.tensor_tensor(y_sum[:, b, c], y_sum[:, b, c], y_second[:, b, c], ALU.add))
                    link(V_.tensor_tensor(y_sum[:, b, c], y_sum[:, b, c], gbc[:, 1, COND[b], c], ALU.mult))
                    V_.tensor_tensor(x[:, b, c], x[:, b, c], y_sum[:, b, c], ALU.add).then_inc(x_moe_v, 1)
                if L < DEPTH - 1:
                    mod_columns(L + 1, 1)
                    spread_gates(L + 1, 0)
                    dve.wait_ge(x_moe, 3 * (L + 1))
                    spread_gates(L + 1, 1)
            norm_scale(2 * DEPTH)
            dve.wait_ge(x_in, 48)
            dve.wait_ge(xn_ready, 3 * (2 * DEPTH + 1))
            for b in range(NB):
                last = V_.tensor_tensor(xn[:, b, :], xn[:, b, :], gbc[:, 0, 0, :], ALU.mult)
            last.then_inc(xn_ready, 1)

        @block.tensor
        def _(pe):
            def done(ins):
                ins.then_inc(bank_full, 1)

            def wait_unit(key, i=None):
                slot, before = ring_place[key]
                pe.wait_ge(slot_full[slot], 16 * (before + 1) if i is None else i * 16 + 16 * (before + 1))

            def mm(out, lhsT, rhs, start, stop):
                return pe.matmul(out, lhsT, rhs, start=start, stop=stop)

            def mod_unit(key, base, m, bk, i=None):
                wait_unit(key, i)
                pe.wait_ge(rows_done, base + m + 1)
                w = unit(key).rearrange("p (k n) -> p k n", k=KC)
                for k in range(KC):
                    g = k % 4 * 32
                    ins = pe.matmul(bank[bk][g:g + 32, 0:UC], condT[:, k, :], w[:, k, :], start=k < 4, stop=k >= 4)
                ins.then_inc(mod_full, 1)

            def project(key, ukey, lhs, kcs, n):
                wait_bank_free(pe, key)
                w = unit(ukey)[:, 0:kcs * n].rearrange("p (k n) -> p k n", k=kcs)
                for k in range(kcs):
                    ins = mm(job_bank(key)[:, 0:n], lhs[:, k, key[3] * P:(key[3] + 1) * P], w[:, k, :],
                             k == 0, k == kcs - 1)
                done(ins)

            pe.wait_ge(cond_in, 16 * 8)
            pe.wait_ge(raw_silu, 1)
            done(pe.transpose(job_bank("cond")[:, 0:16], raw[0:16, 0:P], ident[0:16, 0:16]))
            done(pe.transpose(job_bank("gains")[:, 0:67], raw[0:67, P:2 * P], ident[0:67, 0:67]))
            for c in range(2):
                done(pe.transpose(job_bank(("bias", c))[:, 0:96], raw[0:96, (2 + c) * P:(3 + c) * P],
                                  ident[0:96, 0:96]))
            wait_evacuated(pe, "cond", "gains", ("bias", 1))
            for m in range(8):
                mod_unit(("mod0", m), 0, m, 7)
            pe.wait_ge(const_in, 16 * 15)

            def mod_columns(L, s):
                key = ("modc", L, s)
                wait_bank_free(pe, key)
                for v in range(2):
                    for k in range(KC):
                        c = (v * KC + k) * 2
                        at = (3 * s + v) * D + k * P
                        ins = mm(job_bank(key)[:, c:c + 2], rows[:, at:at + P], sel[:, 2 * P:2 * P + 2], True, True)
                done(ins)

            def spread_gates(L, g):
                for j in range(4 * g, 4 * g + 4):
                    key = ("gate", L, j)
                    wait_bank_free(pe, key)
                    c, c0 = j // 2 % 2, (2, 5)[g] * D + j % 2 * 512
                    done(mm(job_bank(key)[:, :], sel[:, c * P:(c + 1) * P], rows[:, c0:c0 + 512], True, True))

            def norm_turn(n):
                pe.wait_ge(xn_ready, 3 * n + 3)
                for k in range(KC):
                    key = ("norm", n, k)
                    wait_bank_free(pe, key)
                    for b in range(NB):
                        ins = pe.transpose(job_bank(key)[:, b * P:(b + 1) * P], xn[:, b, k * P:(k + 1) * P],
                                           ident[:, :])
                    done(ins)
                wait_evacuated(pe, *[("norm", n, k) for k in range(KC)])

            for L in range(DEPTH):
                kind = KINDS[L]
                if L == 0:
                    pe.wait_ge(rows_done, 9)
                    mod_columns(0, 0)
                norm_turn(2 * L)
                if kind < 2:
                    for u in range(6):
                        wait_unit(("qkv", L, u))
                        for b in range(NB):
                            project(("qkv", L, u, b), ("qkv", L, u), hT, KC, UC)
                else:
                    for u, (name, w, n) in enumerate(LAT):
                        wait_unit((name, L, w))
                        for b in range(NB):
                            project(("lat", L, u, b), (name, L, w), hT, KC, n)
                    pe.wait_ge(roped_v, 4)
                    pe.wait_ge(cache_in, 16 * 8)
                    for c in range(3):
                        key = ("qlT", L, c)
                        wait_bank_free(pe, key)
                        for b in range(NB):
                            ins = pe.transpose(job_bank(key)[:, b * P:(b + 1) * P], ql[:, b, c * P:(c + 1) * P],
                                               ident[:, :])
                        done(ins)
                    for c in range(2):
                        key = ("ckvT", L, c)
                        wait_bank_free(pe, key)
                        for b in range(4):
                            ins = pe.transpose(job_bank(key)[:, b * P:(b + 1) * P], ckv[:, b, c * P:(c + 1) * P],
                                               ident[:, :])
                        done(ins)
                    key = ("kpeT", L)
                    wait_bank_free(pe, key)
                    for b in range(4):
                        ins = pe.transpose(job_bank(key)[0:DQK, b * P:(b + 1) * P], kpe[:, b, :], ident[:, :])
                    done(ins)
                    wait_evacuated(pe, *[("qlT", L, c) for c in range(3)], *[("ckvT", L, c) for c in range(2)],
                                   ("kpeT", L))
                    for u in range(3):
                        wait_unit(("uq", L, u))
                        for b in range(NB):
                            project(("uq", L, u, b), ("uq", L, u), qlT, 3, 512)
                    for u in range(2):
                        wait_unit(("ukv", L, u))
                        w = unit(("ukv", L, u)).rearrange("p (c h n) -> p c h n", c=2, h=8)
                        for kb in range(4):
                            key = ("V", L, u, kb)
                            wait_bank_free(pe, key)
                            for c in range(2):
                                ins = mm(job_bank(key)[:, :].rearrange("p (h d) -> p h d", h=8),
                                         ckvT[:, c, kb * P:(kb + 1) * P], w[:, c, :, 64:128], c == 0, c == 1)
                            done(ins)

                def scores(h):
                    if kind < 2:
                        r0, r1, q, kk = (h % 2) * 64, (h % 2) * 64 + 64, h // 2, h // 4
                    else:
                        r0, r1, q, kk = 0, DQK, h % 8, h % 4
                    for i in range(2):
                        key = ("S", L, h, i)
                        wait_bank_free(pe, key)
                        b = 1 + i
                        ins = mm(job_bank(key)[:, 0:384], qT[r0:r1, q, b * P:(b + 1) * P], kT[r0:r1, kk, P:4 * P],
                                 True, kind != 0)
                        if kind == 0:
                            ins = mm(job_bank(key)[:, P * (1 - i):P * (2 - i)], ident[:, :], masks[:, i, :],
                                     False, True)
                        if i == 0:
                            ins = mm(job_bank(key)[:, 384:512], qT[r0:r1, q, 0:P], kT[r0:r1, kk, 0:P], True, True)
                        done(ins)

                def turn(h):
                    n = L * H + h
                    pe.wait_ge(probs, n + 1)
                    for i in range(2):
                        if n > 0:
                            pe.wait_ge((pt_a, pt_v)[i], n)
                        for t in range((4, 3)[i]):
                            ins = pe.transpose(bank[4 + i][:, t * P:(t + 1) * P],
                                               pp[:, 0, h % 2, 512 * i + t * P:512 * i + (t + 1) * P], ident[:, :])
                        ins.then_inc(pt_full, 1)

                def weigh(h):
                    n = L * H + h
                    j = L * 8 + h // 2
                    pe.wait_ge(pt_a, n + 1)
                    pe.wait_ge(pt_v, n + 1)
                    if h % 2 == 0 and j >= 2:
                        pe.wait_ge(o_ready, j - 1)
                    vc = (h // 4 if kind < 2 else h) * DH
                    for b, off, kbs in ((0, 384, (0,)), (1, 0, (1, 2, 3)), (2, 512, (1, 2, 3))):
                        out = bank[6 + h // 2 % 2][:, (2 * b + h % 2) * DH:(2 * b + h % 2 + 1) * DH]
                        for t, kb in enumerate(kbs):
                            ins = mm(out, pp[:, 1, h % 2, off + t * P:off + (t + 1) * P], V[:, kb, vc:vc + DH],
                                     t == 0, t == len(kbs) - 1)
                    if h % 2 == 1:
                        ins.then_inc(o_full, 1)

                if kind < 2:
                    if kind == 1:
                        pe.wait_ge(qk_ready, 5)
                    pe.wait_ge(roped_v, (1, 2, 0, 7)[L])
                    pe.wait_ge(roped_p, (1, 2, 0, 3)[L])
                    pe.wait_ge(cache_in, 16 * (3, 6, 0, 11)[L])
                    wait_evacuated(pe, *[("qkv", L, u, b) for u in range(6) for b in range(NB)])
                    for p in range(8):
                        key = ("qT", L, p)
                        wait_bank_free(pe, key)
                        for b in range(NB):
                            ins = pe.transpose(job_bank(key)[:, b * P:(b + 1) * P], qkv[:, b, p * P:(p + 1) * P],
                                               ident[:, :])
                        done(ins)
                    for g in range(G):
                        key = ("kT", L, g)
                        wait_bank_free(pe, key)
                        for b in range(4):
                            src = (qkv[:, b, 1024 + g * P:1024 + (g + 1) * P] if b < 3 else
                                   kc[:, g, :, :].rearrange("p t d -> p (t d)"))
                            ins = pe.transpose(job_bank(key)[:, b * P:(b + 1) * P], src, ident[:, :])
                        done(ins)
                for heads in CHUNKS[L]:
                    if kind == 2:
                        for h in heads:
                            key = ("kT", L, h)
                            wait_bank_free(pe, key)
                            w = unit(("ukv", L, h // 8)).rearrange("p (c h n) -> p c h n", c=2, h=8)
                            for c in range(2):
                                ins = mm(job_bank(key)[0:64, :], w[:, c, h % 8, 0:64], ckvT[:, c, :], c == 0, c == 1)
                            done(ins)
                        if heads[0] == 0:
                            pe.wait_ge(roped_v, 6)
                            wait_evacuated(pe, *[("uq", L, 2, b) for b in range(NB)],
                                           *[("V", L, 1, kb) for kb in range(4)])
                        for h in heads:
                            key = ("qT", L, h)
                            wait_bank_free(pe, key)
                            for b in range(NB):
                                ins = pe.transpose(job_bank(key)[0:DQK, b * P:(b + 1) * P],
                                                   qkv[:, b, h * DQK:(h + 1) * DQK], ident[:, :])
                            done(ins)
                        wait_evacuated(pe, *[(w, L, h) for h in heads for w in ("qT", "kT")])
                    else:
                        wait_evacuated(pe, *[("qT", L, p) for p in range(8)], *[("kT", L, g) for g in range(G)])
                    hs = list(heads)
                    for t in range(len(hs) + 2):
                        if t < len(hs):
                            scores(hs[t])
                        if 1 <= t <= len(hs):
                            turn(hs[t - 1])
                        if t >= 2:
                            weigh(hs[t - 2])
                pe.wait_ge(o_ready, 8 * (L + 1))
                for k in range(KC):
                    key = ("oT", L, k)
                    wait_bank_free(pe, key)
                    for b in range(NB):
                        ins = pe.transpose(job_bank(key)[:, b * P:(b + 1) * P], xn[:, b, k * P:(k + 1) * P],
                                           ident[:, :])
                    done(ins)
                if L == 0:
                    for m in range(8, 12):
                        mod_unit(("mod0", m), 0, m, 7)
                    pe.wait_ge(rows_done, 13)
                    spread_gates(0, 0)
                wait_evacuated(pe, *[("oT", L, k) for k in range(KC)])
                for u in range(4):
                    wait_unit(("wo", L, u))
                    for b in range(NB):
                        project(("wo", L, u, b), ("wo", L, u), hT, KC, UC)
                    for m in range(12 + 3 * u, 15 + 3 * u if L == 0 else 0):
                        mod_unit(("mod0", m), 0, m, 7)
                if L == 0:
                    pe.wait_ge(rows_done, 25)
                    mod_columns(0, 1)
                    spread_gates(0, 1)
                norm_turn(2 * L + 1)
                key = ("router", L)
                wait_bank_free(pe, key)
                for b in range(NB):
                    for k in range(KC):
                        ins = mm(job_bank(key)[:, b * E:(b + 1) * E], hT[:, k, b * P:(b + 1) * P], wr[:, k, :],
                                 k == 0, k == KC - 1)
                done(ins)
                for b in range(NB):
                    for half in range(2):
                        key = ("hrow", L, b, half)
                        wait_bank_free(pe, key)
                        for k in range(4):
                            ins = pe.transpose(job_bank(key)[:, k * P:(k + 1) * P],
                                               hT[:, 4 * half + k, b * P:(b + 1) * P], ident[:, :])
                        done(ins)
                mods = list(range(MODA if L < DEPTH - 1 else 0))

                def mod_a(count):
                    for m in mods[:count]:
                        mod_unit(("modA", L, m), 24 * (L + 1), m, 7)
                    del mods[:count]

                mod_a(2)
                pe.wait_ge(gates_ready, L + 1)
                key = ("rank", L)
                wait_bank_free(pe, key)
                for b in range(NB):
                    for c in range(b + 1):
                        mm(job_bank(key)[:, b * E:(b + 1) * E], before[:, :] if c == b else ones[:, :],
                           gates[:, c, :], c == 0, c == b)
                for c in range(NB):
                    ins = mm(job_bank(key)[:, 48:64], ones[:, :], gates[:, c, :], c == 0, c == NB - 1)
                done(ins)
                for g in range(4):
                    if g < 2:
                        mod_a(1)
                    key = ("idx", L, g)
                    wait_bank_free(pe, key)
                    pe.wait_ge(member_ready, 4 * L + g + 1)
                    for e in range(4):
                        for b in range(NB):
                            ins = mm(job_bank(key)[:, 4 * e:4 * e + 4], member[:, g % 2, b, e, :],
                                     vals[:, b, 4 * g + e, :], b == 0, b == NB - 1)
                    done(ins)
                pe.wait_ge(idx_ready, 4 * (L + 1))
                pe.wait_ge(rows_done, 24 * (L + 1) + MODA + 1 if L < DEPTH - 1 else 24 * DEPTH + 1)

                def turn_rows(n, slot, gathered):
                    pe.wait_ge(g_in[slot], gathered)
                    pe.wait_ge(xT_a, n + 1)
                    pe.wait_ge(xT_v, n + 1)
                    for k in range(KC):
                        ins = pe.transpose(bank[6 + k // 4][:, k % 4 * P:(k % 4 + 1) * P],
                                           xg[:, slot, k * P:(k + 1) * P], ident[:, :])
                    ins.then_inc(xT_full, 1)

                def gate_up(x_t, out, w):
                    for c in range(2):
                        for k in range(KC):
                            ins = mm(out[:, c * DE:(c + 1) * DE], x_t[:, k, :], w[c][:, k, :], k == 0, k == KC - 1)
                    return ins

                def turn_gated(src):
                    for c in range(2):
                        ins = pe.transpose(bank[2][:, c * P:(c + 1) * P], src[:, c * P:(c + 1) * P], ident[:, :])
                    return ins

                def down(a_t, w):
                    for half in range(2):
                        for c in range(2):
                            ins = mm(bank[4 + half][:, :], a_t[:, c, :], w[:, c, half * 512:(half + 1) * 512],
                                     c == 0, c == 1)
                    return ins

                def weights(w, e):
                    return unit(("exp", L, 4 * e + w)).rearrange("p (k n) -> p k n", k=(KC, KC, 2)[w])

                def finish(t, e):
                    n = t * 2 + (E * L + e)
                    wait_unit(("exp", L, 4 * e + 2), t)
                    pe.wait_ge(acT_ready, n + 2)
                    pe.wait_ge(y_a, n + 1)
                    pe.wait_ge(y_v, n + 1)
                    down(actT[:, e], weights(2, e)).then_inc(y_full, 1)

                def expert(t, e):
                    n = t * 2 + (E * L + e)
                    wait_unit(("exp", L, 4 * e), t)
                    wait_unit(("exp", L, 4 * e + 1), t)
                    pe.wait_ge(xT_a, n + 2)
                    pe.wait_ge(xT_v, n + 2)
                    pe.wait_ge(act_full, n + 1)
                    gate_up(xT[:, e], bank[e], [weights(0, e), weights(1, e)]).then_inc(au_full, 1)
                    if not is_first(t, e):
                        finish(*before_one(t, e))
                    if not is_last(t, e):
                        turn_rows(n + 1, 1 - e, (t + e) * 16 + 16 * (E // 2 * L + 1))
                    if L < DEPTH - 1:
                        mod_unit(("exp", L, 4 * e + 3), 24 * (L + 1), t * 2 + (MODA + e), 3, t)
                    pe.wait_ge(act_full, n + 3)
                    pe.wait_ge(acT_ready, n + 1)
                    turn_gated(act_sb[:, e, :]).then_inc(acT_full, 1)
                    if is_last(t, e):
                        finish(t, e)

                turn_rows(E * L, 0, 16 * (E // 2 * L + 1))
                each_expert(pe, expert)
                for m in range(MODB if L < DEPTH - 1 else 0):
                    mod_unit(("modB", L, m), 24 * (L + 1), MODA + E + m, 3)
                pe.wait_ge(y_a, E * (L + 1) + 1)
                pe.wait_ge(y_v, E * (L + 1) + 1)
                pe.wait_ge(rows_done, 24 * min(L + 2, DEPTH) + 1)
                if L < DEPTH - 1:
                    mod_columns(L + 1, 0)
                    wait_evacuated(pe, ("modc", L + 1, 0))

                def step(n, q, e):
                    pe.wait_ge(ov_member_ready, n + 1)
                    for b in range(NB):
                        ins = mm(bank[3][:, 0:4], ov_member[:, b, :], ov_vals[:, b, :], b == 0, b == NB - 1)
                    ins.then_inc(ov_idx_full, 1)
                    pe.wait_ge(ov_g_in, (n + 1) * 16)
                    for k in range(KC):
                        ins = pe.transpose(bank[6 + k // 4][:, k % 4 * P:(k % 4 + 1) * P],
                                           xg[:, 0, k * P:(k + 1) * P], ident[:, :])
                    ins.then_inc(ov_xT_full, 1)
                    pe.wait_ge(ov_xT_ready, n + 1)
                    pe.wait_ge(ov_w_in, (n + 1) * 48)
                    gate_up(xT[:, 0], bank[0], ov_w).then_inc(ov_au_full, 1)
                    pe.wait_ge(ov_act, n + 1)
                    turn_gated(act_sb[:, 0, :]).then_inc(ov_acT_full, 1)
                    pe.wait_ge(ov_acT_ready, n + 1)
                    down(actT[:, 0], ov_w[2]).then_inc(ov_y_full, 1)

                further_passes(pe, L, step)
                if L < DEPTH - 1:
                    mod_columns(L + 1, 1)
                    spread_gates(L + 1, 0)
                    spread_gates(L + 1, 1)


def launch_io():
    ins = ["x_prompt", "x_sample", "cache_swa_k", "cache_swa_v", "cache_qkn_k", "cache_qkn_v", "cache_mla_ckv",
           "cache_mla_kpe", "c", "c_ctx", "w_mod", "b_mod", "norm_mix", "norm_ffn", "swa_wqkv", "swa_wo", "swa_sink",
           "qkn_wqkv", "qkn_wo", "qkn_qnorm", "qkn_knorm", "mla_wdq", "mla_qnorm", "mla_wuq", "mla_wdkv",
           "mla_kvnorm", "mla_wukv", "mla_wo", "w_router", "router_bias", "moe_w_gate", "moe_w_up", "moe_w_down",
           "final_norm"]
    outs = {"y_prompt": (1, 128, 1024), "y_sample": (1, 256, 1024), "state_swa_k": (1, 2, 128, 4, 64),
            "state_swa_v": (1, 2, 128, 4, 64), "state_qkn_k": (1, 1, 128, 4, 64), "state_qkn_v": (1, 1, 128, 4, 64),
            "state_mla_ckv": (1, 1, 128, 256), "state_mla_kpe": (1, 1, 128, 32)}
    return ins, outs


def kernel(**inputs):
    import concourse.bacc as bacc
    from concourse.bass_utils import run_bass_kernel_spmd

    nc = bacc.Bacc("TRN2", target_bir_lowering=False, num_devices=1)
    names, outs = launch_io()
    arrays, A = {}, {}
    given = {n: np.ascontiguousarray(inputs[n]) for n in names}
    given.update(host_constants())
    for name, a in given.items():
        arrays[f"in_{name}"] = a
        A[name] = nc.dram_tensor(f"in_{name}", a.shape, mybir.dt.from_np(a.dtype), kind="ExternalInput").ap()
    for name, shape in outs.items():
        A[name] = nc.dram_tensor(f"out_{name}", shape, F32, kind="ExternalOutput").ap()
    build(nc, A)
    r = run_bass_kernel_spmd(nc, [arrays], core_ids=[0])
    return tuple(r.results[0][f"out_{name}"] for name in outs)
```
